# Optimizing a Trainium2 kernel written in Bass

```python
import math
import jax, jax.numpy as jnp
from jax import lax
import numpy as np

D_MODEL = 1024
BATCH = 1
SEQ = 256
DEPTH = 1

HEAD_DIM = 64
GDN_HEADS = 6
GDN_CONV = 4
GDN_CHUNK = 64
GDN_WIDTH = GDN_HEADS * HEAD_DIM
NSA_HEADS = 6
NSA_KV_HEADS = 2
NSA_GROUP = NSA_HEADS // NSA_KV_HEADS
NSA_WIDTH = NSA_HEADS * HEAD_DIM
NSA_KV_WIDTH = NSA_KV_HEADS * HEAD_DIM
CMP_LEN = 32
CMP_STRIDE = 16
CMP_HIDDEN = 256
SEL_BLOCK = 64
SEL_TOPK = 16
WINDOW = 512
Q_BLOCK = 128
FORCED_SCORE = 1e4
POOL_WINDOWS = (2, 4, 8, 16)
POOL_GROUP_DIM = 64
POOL_WIDTH = 4 * POOL_GROUP_DIM
D_MIX = GDN_WIDTH + NSA_WIDTH + POOL_WIDTH
IN_SPLITS = (3 * GDN_WIDTH, GDN_WIDTH, GDN_HEADS, GDN_HEADS, NSA_WIDTH, 6 * NSA_KV_WIDTH, 3 * NSA_HEADS, POOL_WIDTH)
D_IN = 3 * GDN_WIDTH + GDN_WIDTH + GDN_HEADS + GDN_HEADS + NSA_WIDTH + 6 * NSA_KV_WIDTH + 3 * NSA_HEADS + POOL_WIDTH
D_FF = 4 * D_MODEL
EPS = 1e-6


def rms_norm(x, g):
    xf = x.astype(jnp.float32)
    return (xf * lax.rsqrt(jnp.mean(xf * xf, axis=-1, keepdims=True) + EPS) * g).astype(x.dtype)

def l2norm(x):
    xf = x.astype(jnp.float32)
    return xf * lax.rsqrt(jnp.sum(xf * xf, axis=-1, keepdims=True) + EPS)

def masked_softmax(s, mask):
    s = jnp.where(mask, s.astype(jnp.float32), -1e30)
    return jax.nn.softmax(s, axis=-1) * mask

def split_columns(proj):
    offs = []
    acc = 0
    for s in IN_SPLITS[:-1]:
        acc += s
        offs.append(acc)
    return jnp.split(proj, offs, axis=-1)

def causal_conv(x, w):
    T = x.shape[1]
    K = w.shape[0]
    xp = jnp.pad(x, ((0, 0), (K - 1, 0), (0, 0)))
    return sum(xp[:, k:k + T] * w[k] for k in range(K))

def gated_delta_rule(q, k, v, beta, g):
    B, T, H, Dk = q.shape
    Dv = v.shape[-1]
    C = GDN_CHUNK
    N = T // C
    f32 = jnp.float32

    def chunks(a):
        a = a.astype(f32).reshape((B, N, C, H) + a.shape[3:])
        return jnp.moveaxis(a, 3, 1)

    q, k, v, beta, g = map(chunks, (q, k, v, beta, g))
    q = q * Dk ** -0.5
    gc = jnp.cumsum(g, axis=-1)
    causal = jnp.tril(jnp.ones((C, C), bool))
    strict = jnp.tril(jnp.ones((C, C), bool), -1)
    decay = jnp.exp(jnp.where(causal, gc[..., :, None] - gc[..., None, :], -jnp.inf))
    k_beta = k * beta[..., None]
    L = jnp.where(strict, jnp.einsum('bhncd,bhnsd->bhncs', k_beta, k) * decay, 0.0)
    A = jnp.eye(C, dtype=f32) + L
    u = lax.linalg.triangular_solve(A, v * beta[..., None], left_side=True, lower=True, unit_diagonal=True)
    w = lax.linalg.triangular_solve(A, k_beta * jnp.exp(gc)[..., None], left_side=True, lower=True, unit_diagonal=True)
    qk = jnp.einsum('bhncd,bhnsd->bhncs', q, k) * decay
    q_dec = q * jnp.exp(gc)[..., None]
    k_dec = k * jnp.exp(gc[..., -1:] - gc)[..., None]
    g_last = jnp.exp(gc[..., -1])

    def step(S, xs):
        u_i, w_i, qk_i, qd_i, kd_i, gl_i = xs
        v_new = u_i - jnp.einsum('bhcd,bhde->bhce', w_i, S)
        o = jnp.einsum('bhcd,bhde->bhce', qd_i, S) + jnp.einsum('bhcs,bhse->bhce', qk_i, v_new)
        S = S * gl_i[..., None, None] + jnp.einsum('bhcd,bhce->bhde', kd_i, v_new)
        return S, o

    xs = tuple(jnp.moveaxis(a, 2, 0) for a in (u, w, qk, q_dec, k_dec, g_last))
    S0 = jnp.zeros((B, H, Dk, Dv), f32)
    _, o = lax.scan(step, S0, xs)
    return jnp.transpose(o, (1, 0, 3, 2, 4)).reshape(B, T, H, Dv)

def gdn_mixer(qkv, z, b, a, conv_w, a_log, dt_bias, norm_g):
    B, T, _ = qkv.shape
    qkv = jax.nn.silu(causal_conv(qkv, conv_w))
    q, k, v = jnp.split(qkv, 3, axis=-1)
    heads = lambda t: t.reshape(B, T, GDN_HEADS, HEAD_DIM)
    q, k, v = l2norm(heads(q)), l2norm(heads(k)), heads(v)
    beta = jax.nn.sigmoid(b.astype(jnp.float32))
    g = -jnp.exp(a_log.astype(jnp.float32)) * jax.nn.softplus(a.astype(jnp.float32) + dt_bias)
    o = gated_delta_rule(q, k, v, beta, g)
    o = rms_norm(o, norm_g) * jax.nn.silu(heads(z).astype(jnp.float32))
    return o.reshape(B, T, GDN_WIDTH).astype(qkv.dtype)

def compress(x, pos, w1, w2):
    B, T, H, D = x.shape
    R = CMP_LEN // CMP_STRIDE
    Nr = T // CMP_STRIDE
    r = x.reshape(B, Nr, CMP_STRIDE, H, D)
    blocks = jnp.concatenate([r[:, i:Nr - R + 1 + i] for i in range(R)], axis=2)
    blocks = blocks + pos[None, None, :, None, :]
    Nc = blocks.shape[1]
    flat = blocks.transpose(0, 1, 3, 2, 4).reshape(B, Nc, H, CMP_LEN * D)
    out = jax.nn.silu(flat @ w1) @ w2
    return out.transpose(0, 2, 1, 3)

def cmp_to_sel(p):
    R = SEL_BLOCK // CMP_STRIDE
    P = CMP_LEN // CMP_STRIDE - 1
    Ns = (p.shape[-1] + P) // R
    pp = jnp.pad(p, [(0, 0)] * (p.ndim - 1) + [(P, P)])
    return sum(lax.slice_in_dim(pp, o, o + R * (Ns - 1) + 1, stride=R, axis=-1) for o in range(R + P))

def nsa_mixer(q, kv, gate_logits, q_norm, k_norm, cmp_pos, cmp_w1, cmp_w2):
    B, T, _ = q.shape
    Hkv, G, Dh = NSA_KV_HEADS, NSA_GROUP, HEAD_DIM
    out_dtype = q.dtype
    scale = Dh ** -0.5
    q = rms_norm(q.reshape(B, T, NSA_HEADS, Dh), q_norm)
    q = q.reshape(B, T, Hkv, G, Dh).transpose(0, 2, 3, 1, 4)
    kc, vc, ks, vs, kw, vw = [t.reshape(B, T, Hkv, Dh) for t in jnp.split(kv, 6, axis=-1)]
    kc = rms_norm(compress(kc, cmp_pos[0], cmp_w1[0], cmp_w2[0]), k_norm[0])
    vc = compress(vc, cmp_pos[1], cmp_w1[1], cmp_w2[1])
    Nc = kc.shape[2]
    Ns = T // SEL_BLOCK
    K_SEL = min(SEL_TOPK, Ns)
    ks = rms_norm(ks, k_norm[1]).transpose(0, 2, 1, 3).reshape(B, Hkv, Ns, SEL_BLOCK, Dh)
    vs = vs.transpose(0, 2, 1, 3).reshape(B, Hkv, Ns, SEL_BLOCK, Dh)
    pad = ((0, 0), (0, 0), (WINDOW, 0), (0, 0))
    kw = jnp.pad(rms_norm(kw, k_norm[2]).transpose(0, 2, 1, 3), pad)
    vw = jnp.pad(vw.transpose(0, 2, 1, 3), pad)
    gates = jax.nn.sigmoid(gate_logits.astype(jnp.float32)).reshape(B, T, Hkv, G, 3).transpose(0, 2, 3, 1, 4)
    cmp_end = jnp.arange(Nc) * CMP_STRIDE + CMP_LEN - 1
    blk = jnp.arange(Ns)
    bidx = jnp.arange(B)[:, None, None, None]
    hidx = jnp.arange(Hkv)[None, :, None, None]

    def block(i):
        t0 = i * Q_BLOCK
        pos = t0 + jnp.arange(Q_BLOCK)
        qb = lax.dynamic_slice_in_dim(q, t0, Q_BLOCK, axis=3) * scale
        gb = lax.dynamic_slice_in_dim(gates, t0, Q_BLOCK, axis=3)
        s = jnp.einsum('bhgqd,bhcd->bhgqc', qb, kc)
        p_c = masked_softmax(s, cmp_end[None, :] <= pos[:, None])
        o_c = jnp.einsum('bhgqc,bhcd->bhgqd', p_c, vc)
        imp = cmp_to_sel(p_c.sum(axis=2))
        cur = pos // SEL_BLOCK
        forced = (blk[None] == 0) | (blk[None] == cur[:, None]) | (blk[None] == cur[:, None] - 1)
        valid = blk[None] * SEL_BLOCK <= pos[:, None]
        imp = jnp.where(forced, FORCED_SCORE, jnp.where(valid, imp, -1.0))
        _, idx = lax.top_k(imp, K_SEL)
        ksel = ks[bidx, hidx, idx]
        vsel = vs[bidx, hidx, idx].reshape(B, Hkv, Q_BLOCK, K_SEL * SEL_BLOCK, Dh)
        s = jnp.einsum('bhgqd,bhqksd->bhgqks', qb, ksel).reshape(B, Hkv, G, Q_BLOCK, K_SEL * SEL_BLOCK)
        key_pos = idx[..., None] * SEL_BLOCK + jnp.arange(SEL_BLOCK)
        mask_s = (key_pos <= pos[:, None, None]).reshape(B, Hkv, 1, Q_BLOCK, K_SEL * SEL_BLOCK)
        o_s = jnp.einsum('bhgqn,bhqnd->bhgqd', masked_softmax(s, mask_s), vsel)
        kwb = lax.dynamic_slice_in_dim(kw, t0, Q_BLOCK + WINDOW, axis=2)
        vwb = lax.dynamic_slice_in_dim(vw, t0, Q_BLOCK + WINDOW, axis=2)
        kpos = t0 - WINDOW + jnp.arange(Q_BLOCK + WINDOW)
        mask_w = (kpos[None] <= pos[:, None]) & (kpos[None] > pos[:, None] - WINDOW) & (kpos[None] >= 0)
        s = jnp.einsum('bhgqd,bhkd->bhgqk', qb, kwb)
        o_w = jnp.einsum('bhgqk,bhkd->bhgqd', masked_softmax(s, mask_w), vwb)
        return gb[..., 0:1] * o_c + gb[..., 1:2] * o_s + gb[..., 2:3] * o_w

    out = lax.map(block, jnp.arange(T // Q_BLOCK))
    return out.transpose(1, 0, 4, 2, 3, 5).reshape(B, T, NSA_WIDTH).astype(out_dtype)

def pool_mixer(u, pool_w, pool_scale):
    B, T, _ = u.shape
    uf = u.astype(jnp.float32)
    c = jnp.pad(jnp.cumsum(uf, axis=1), ((0, 0), (1, 0), (0, 0)))
    t1 = jnp.arange(1, T + 1, dtype=jnp.float32)
    outs = []
    for gi, w in enumerate(POOL_WINDOWS):
        sl = slice(gi * POOL_GROUP_DIM, (gi + 1) * POOL_GROUP_DIM)
        cg = c[..., sl]
        cg_lag = jnp.pad(cg, ((0, 0), (w - 1, 0), (0, 0)))[:, :T]
        mean = (cg[:, 1:] - cg_lag) / jnp.minimum(t1, float(w))[None, :, None]
        outs.append(jnp.einsum('btc,cd->btd', mean - uf[..., sl], pool_w[gi]))
    return (jnp.concatenate(outs, axis=-1) * pool_scale).astype(u.dtype)

def first_inputs(seed: int = 0) -> dict:
    key = jax.random.key(seed)
    keys = jax.random.split(key, 20)
    nrm = lambda k, shape, s: jax.random.normal(k, shape, jnp.float32) * s
    L = DEPTH
    x = nrm(keys[0], (BATCH, SEQ, D_MODEL), 1.0)
    norm_mix = 1.0 + nrm(keys[1], (L, D_MODEL), 0.02)
    w_in = nrm(keys[2], (L, D_MODEL, D_IN), D_MODEL ** -0.5)
    conv_w = nrm(keys[3], (L, GDN_CONV, 3 * GDN_WIDTH), GDN_CONV ** -0.5)
    a_log = jnp.log(jax.random.uniform(keys[4], (L, GDN_HEADS), jnp.float32, 1.0, 16.0))
    dt = jnp.exp(jax.random.uniform(keys[5], (L, GDN_HEADS), jnp.float32, math.log(1e-3), math.log(1e-1)))
    dt_bias = dt + jnp.log(-jnp.expm1(-dt))
    gdn_norm = 1.0 + nrm(keys[6], (L, HEAD_DIM), 0.02)
    nsa_q_norm = 1.0 + nrm(keys[7], (L, HEAD_DIM), 0.02)
    nsa_k_norm = 1.0 + nrm(keys[8], (L, 3, HEAD_DIM), 0.02)
    cmp_pos = nrm(keys[9], (L, 2, CMP_LEN, HEAD_DIM), 0.1)
    cmp_w1 = nrm(keys[10], (L, 2, CMP_LEN * HEAD_DIM, CMP_HIDDEN), (CMP_LEN * HEAD_DIM) ** -0.5)
    cmp_w2 = nrm(keys[11], (L, 2, CMP_HIDDEN, HEAD_DIM), CMP_HIDDEN ** -0.5)
    pool_w = nrm(keys[12], (L, len(POOL_WINDOWS), POOL_GROUP_DIM, POOL_GROUP_DIM), POOL_GROUP_DIM ** -0.5)
    pool_scale = 1.0 + nrm(keys[13], (L, POOL_WIDTH), 0.1)
    w_out = nrm(keys[14], (L, D_MIX, D_MODEL), (2 * DEPTH * D_MIX) ** -0.5)
    norm_ffn = 1.0 + nrm(keys[15], (L, D_MODEL), 0.02)
    w_ffn1 = nrm(keys[16], (L, D_MODEL, D_FF), D_MODEL ** -0.5)
    w_ffn2 = nrm(keys[17], (L, D_FF, D_MODEL), (2 * DEPTH * D_FF) ** -0.5)
    return {"x": x, "norm_mix": norm_mix, "w_in": w_in, "conv_w": conv_w, "a_log": a_log, "dt_bias": dt_bias,
            "gdn_norm": gdn_norm, "nsa_q_norm": nsa_q_norm, "nsa_k_norm": nsa_k_norm, "cmp_pos": cmp_pos,
            "cmp_w1": cmp_w1, "cmp_w2": cmp_w2, "pool_w": pool_w, "pool_scale": pool_scale, "w_out": w_out,
            "norm_ffn": norm_ffn, "w_ffn1": w_ffn1, "w_ffn2": w_ffn2}

def first_block(x, norm_mix, w_in, conv_w, a_log, dt_bias, gdn_norm, nsa_q_norm, nsa_k_norm, cmp_pos,
              cmp_w1, cmp_w2, pool_w, pool_scale, w_out, norm_ffn, w_ffn1, w_ffn2):
    for l in range(DEPTH):
        h = rms_norm(x, norm_mix[l])
        proj = h @ w_in[l]
        qkv_a, z_a, b_a, a_a, q_b, kv_b, gate_b, u_c = split_columns(proj)
        y_a = gdn_mixer(qkv_a, z_a, b_a, a_a, conv_w[l], a_log[l], dt_bias[l], gdn_norm[l])
        y_b = nsa_mixer(q_b, kv_b, gate_b, nsa_q_norm[l], nsa_k_norm[l], cmp_pos[l], cmp_w1[l], cmp_w2[l])
        y_c = pool_mixer(u_c, pool_w[l], pool_scale[l])
        y = jnp.concatenate([y_a.astype(x.dtype), y_b.astype(x.dtype), y_c.astype(x.dtype)], axis=-1)
        x = x + y @ w_out[l]
        h = rms_norm(x, norm_ffn[l])
        x = x + jnp.square(jax.nn.relu(h @ w_ffn1[l])) @ w_ffn2[l]
    return x


CHUNK = 64
FOX_HEADS = 8
FOX_HEAD_DIM = 64
FOX_WIDTH = FOX_HEADS * FOX_HEAD_DIM
DIFF_HEADS = 4
DIFF_HEAD_DIM = 64
DIFF_V_DIM = 2 * DIFF_HEAD_DIM
DIFF_WIDTH = DIFF_HEADS * DIFF_V_DIM
N_BRANCH = 2
IN_COLS = 3 * FOX_WIDTH + FOX_HEADS + 3 * DIFF_WIDTH + N_BRANCH * D_MODEL
N_GROUPS = 4
EXPERTS_PER_GROUP = 8
N_EXPERTS = N_GROUPS * EXPERTS_PER_GROUP
TOP_K_EXPERT = 2
D_EXPERT = D_MODEL // 2
MOE_BLOCK = 128


def rms_norm_2(x, g):
    xf = x.astype(jnp.float32)
    y = xf * lax.rsqrt(jnp.mean(xf * xf, axis=-1, keepdims=True) + EPS)
    return (y * g.astype(jnp.float32)).astype(x.dtype)

def to_heads(t, n_heads):
    b, s, _ = t.shape
    return t.reshape(b, s, n_heads, -1).transpose(0, 2, 1, 3)

def from_heads(t):
    b, h, s, d = t.shape
    return t.transpose(0, 2, 1, 3).reshape(b, s, h * d)

def fox_attention(q, k, v, log_f):
    B, H, S, d = q.shape
    F = jnp.cumsum(log_f, axis=-1)
    pos = jnp.arange(S)
    scale = d ** -0.5

    def block(i):
        start = i * Q_BLOCK
        qb = lax.dynamic_slice_in_dim(q, start, Q_BLOCK, axis=2)
        Fq = lax.dynamic_slice_in_dim(F, start, Q_BLOCK, axis=2)
        tq = start + jnp.arange(Q_BLOCK)
        s = jnp.einsum('bhqd,bhkd->bhqk', qb, k, preferred_element_type=jnp.float32) * scale
        s = s + Fq[..., :, None] - F[..., None, :]
        mask = pos[None, :] <= tq[:, None]
        s = jnp.where(mask, s, -jnp.inf)
        p = jax.nn.softmax(s, axis=-1).astype(v.dtype)
        return jnp.einsum('bhqk,bhkd->bhqd', p, v)

    out = lax.map(block, jnp.arange(S // Q_BLOCK))
    return out.transpose(1, 2, 0, 3, 4).reshape(B, H, S, d)

def diff_attention(q1, q2, k1, k2, v, lam, slopes):
    B, H, S, d = q1.shape
    pos = jnp.arange(S)
    chunk_k = pos // CHUNK
    scale = d ** -0.5

    def block(i):
        start = i * Q_BLOCK
        q1b = lax.dynamic_slice_in_dim(q1, start, Q_BLOCK, axis=2)
        q2b = lax.dynamic_slice_in_dim(q2, start, Q_BLOCK, axis=2)
        tq = start + jnp.arange(Q_BLOCK)
        dist = jnp.abs(tq[:, None] - pos[None, :]).astype(jnp.float32)
        bias = -slopes[:, None, None] * dist
        mask = chunk_k[None, :] <= (tq // CHUNK)[:, None]
        s1 = jnp.einsum('bhqd,bhkd->bhqk', q1b, k1, preferred_element_type=jnp.float32) * scale + bias
        s2 = jnp.einsum('bhqd,bhkd->bhqk', q2b, k2, preferred_element_type=jnp.float32) * scale + bias
        p1 = jax.nn.softmax(jnp.where(mask, s1, -jnp.inf), axis=-1)
        p2 = jax.nn.softmax(jnp.where(mask, s2, -jnp.inf), axis=-1)
        a = (p1 - lam * p2).astype(v.dtype)
        return jnp.einsum('bhqk,bhkd->bhqd', a, v)

    out = lax.map(block, jnp.arange(S // Q_BLOCK))
    return out.transpose(1, 2, 0, 3, 4).reshape(B, H, S, v.shape[-1])

def hybrid_mixer(h, w_in, b_fgate, b_gate, lq1, lk1, lq2, lk2, g_subln, w_pa, w_pb, w_o, lam_init):
    z = h @ w_in
    widths = [FOX_WIDTH] * 3 + [FOX_HEADS] + [DIFF_WIDTH] * 3 + [D_MODEL] * N_BRANCH
    splits = [int(c) for c in np.cumsum(widths)[:-1]]
    fq, fk, fv, ff, dq, dk, dv, ga, gb = jnp.split(z, splits, axis=-1)

    log_f = jax.nn.log_sigmoid((ff + b_fgate).astype(jnp.float32)).transpose(0, 2, 1)
    o_a = from_heads(fox_attention(to_heads(fq, FOX_HEADS), to_heads(fk, FOX_HEADS),
                                   to_heads(fv, FOX_HEADS), log_f))

    qh = to_heads(dq, DIFF_HEADS)
    kh = to_heads(dk, DIFF_HEADS)
    vh = to_heads(dv, DIFF_HEADS)
    q1, q2 = qh[..., :DIFF_HEAD_DIM], qh[..., DIFF_HEAD_DIM:]
    k1, k2 = kh[..., :DIFF_HEAD_DIM], kh[..., DIFF_HEAD_DIM:]
    f32 = jnp.float32
    lam = (jnp.exp(jnp.sum(lq1.astype(f32) * lk1.astype(f32)))
           - jnp.exp(jnp.sum(lq2.astype(f32) * lk2.astype(f32))) + lam_init)
    slopes = jnp.exp2(-8.0 / DIFF_HEADS * jnp.arange(1, DIFF_HEADS + 1, dtype=f32))
    ob = diff_attention(q1, q2, k1, k2, vh, lam, slopes)
    ob = rms_norm_2(ob, g_subln) * (1.0 - lam_init)
    o_b = from_heads(ob)

    gate_a = jax.nn.sigmoid(ga + b_gate[:D_MODEL])
    gate_b = jax.nn.sigmoid(gb + b_gate[D_MODEL:])
    y = gate_a * (o_a @ w_pa) + gate_b * (o_b @ w_pb)
    return y @ w_o

def hier_moe(h, w_group, b_group, w_expert, b_expert, w1, w3, w2):
    B, S, D = h.shape
    N = B * S
    hf = h.reshape(N, D)
    f32 = jnp.float32
    gl = (hf @ w_group).astype(f32) + b_group.astype(f32)
    gp = jax.nn.softmax(gl, axis=-1)
    g_idx = jnp.argmax(gl, axis=-1)
    g_w = jnp.take_along_axis(gp, g_idx[:, None], axis=-1)[:, 0]
    el = (hf @ w_expert).astype(f32).reshape(N, N_GROUPS, EXPERTS_PER_GROUP)
    el = jnp.take_along_axis(el, g_idx[:, None, None], axis=1)[:, 0] + b_expert.astype(f32)[g_idx]
    ep = jax.nn.softmax(el, axis=-1)
    vals, idx = lax.top_k(ep, TOP_K_EXPERT)
    vals = vals / jnp.sum(vals, axis=-1, keepdims=True)
    weights = g_w[:, None] * vals
    expert_ids = (g_idx[:, None] * EXPERTS_PER_GROUP + idx).astype(jnp.int32)

    A = N * TOP_K_EXPERT
    e_flat = expert_ids.reshape(A)
    w_flat = weights.reshape(A)
    tok = jnp.repeat(jnp.arange(N, dtype=jnp.int32), TOP_K_EXPERT)
    order = jnp.argsort(e_flat)
    e_s, tok_s, w_s = e_flat[order], tok[order], w_flat[order]
    counts = jnp.bincount(e_flat, length=N_EXPERTS)
    padded = (counts + MOE_BLOCK - 1) // MOE_BLOCK * MOE_BLOCK
    start = jnp.cumsum(counts) - counts
    pstart = jnp.cumsum(padded) - padded
    dest = pstart[e_s] + jnp.arange(A) - start[e_s]
    P = A + N_EXPERTS * MOE_BLOCK
    n_blk = P // MOE_BLOCK
    row_tok = jnp.zeros((P,), jnp.int32).at[dest].set(tok_s)
    row_w = jnp.zeros((P,), f32).at[dest].set(w_s)
    blk_e = jnp.searchsorted(jnp.cumsum(padded), jnp.arange(n_blk) * MOE_BLOCK, side='right')
    blk_e = jnp.minimum(blk_e, N_EXPERTS - 1)
    xb = hf[row_tok].reshape(n_blk, MOE_BLOCK, D)

    def expert_block(args):
        xblk, e = args
        return (jax.nn.silu(xblk @ w1[e]) * (xblk @ w3[e])) @ w2[e]

    yb = lax.map(expert_block, (xb, blk_e)).reshape(P, D)
    out = jnp.zeros_like(hf).at[row_tok].add(yb * row_w[:, None].astype(yb.dtype))
    return out.reshape(B, S, D)

def second_inputs(seed: int = 0) -> dict:
    key = jax.random.key(seed)
    ks = jax.random.split(key, 24)
    n = jax.random.normal
    f = jnp.float32
    L = DEPTH
    return {
        "x": n(ks[0], (BATCH, SEQ, D_MODEL), f),
        "g_mix": 1.0 + 0.01 * n(ks[1], (L, D_MODEL), f),
        "w_in": n(ks[2], (L, D_MODEL, IN_COLS), f) * D_MODEL ** -0.5,
        "b_fgate": 1.0 + 0.5 * n(ks[3], (L, FOX_HEADS), f),
        "b_gate": 0.1 * n(ks[4], (L, N_BRANCH * D_MODEL), f),
        "lam_q1": 0.1 * n(ks[5], (L, DIFF_HEAD_DIM), f),
        "lam_k1": 0.1 * n(ks[6], (L, DIFF_HEAD_DIM), f),
        "lam_q2": 0.1 * n(ks[7], (L, DIFF_HEAD_DIM), f),
        "lam_k2": 0.1 * n(ks[8], (L, DIFF_HEAD_DIM), f),
        "g_subln": 1.0 + 0.01 * n(ks[9], (L, DIFF_V_DIM), f),
        "w_pa": n(ks[10], (L, FOX_WIDTH, D_MODEL), f) * FOX_WIDTH ** -0.5,
        "w_pb": n(ks[11], (L, DIFF_WIDTH, D_MODEL), f) * DIFF_WIDTH ** -0.5,
        "w_o": n(ks[12], (L, D_MODEL, D_MODEL), f) * D_MODEL ** -0.5,
        "g_moe": 1.0 + 0.01 * n(ks[13], (L, D_MODEL), f),
        "w_group": n(ks[14], (L, D_MODEL, N_GROUPS), f) * D_MODEL ** -0.5,
        "b_group": 0.01 * n(ks[15], (L, N_GROUPS), f),
        "w_expert": n(ks[16], (L, D_MODEL, N_EXPERTS), f) * D_MODEL ** -0.5,
        "b_expert": 0.01 * n(ks[17], (L, N_GROUPS, EXPERTS_PER_GROUP), f),
        "w1": n(ks[18], (L, N_EXPERTS, D_MODEL, D_EXPERT), f) * D_MODEL ** -0.5,
        "w3": n(ks[19], (L, N_EXPERTS, D_MODEL, D_EXPERT), f) * D_MODEL ** -0.5,
        "w2": n(ks[20], (L, N_EXPERTS, D_EXPERT, D_MODEL), f) * D_EXPERT ** -0.5,
        "g_final": 1.0 + 0.01 * n(ks[21], (D_MODEL,), f),
    }

def second_block(x, g_mix, w_in, b_fgate, b_gate, lam_q1, lam_k1, lam_q2, lam_k2, g_subln,
              w_pa, w_pb, w_o, g_moe, w_group, b_group, w_expert, b_expert, w1, w3, w2, g_final):
    for l in range(DEPTH):
        lam_init = 0.8 - 0.6 * math.exp(-0.3 * l)
        h = rms_norm_2(x, g_mix[l])
        x = x + hybrid_mixer(h, w_in[l], b_fgate[l], b_gate[l], lam_q1[l], lam_k1[l],
                             lam_q2[l], lam_k2[l], g_subln[l], w_pa[l], w_pb[l], w_o[l], lam_init)
        h = rms_norm_2(x, g_moe[l])
        x = x + hier_moe(h, w_group[l], b_group[l], w_expert[l], b_expert[l], w1[l], w3[l], w2[l])
    return rms_norm_2(x, g_final)


def setup_inputs(seed=0):
    out = dict(first_inputs(seed))
    for name, value in second_inputs(seed + 1).items():
        if name != "x":
            out[name + "_2"] = value
    return out


def reference(
    x, norm_mix, w_in, conv_w, a_log, dt_bias, gdn_norm, nsa_q_norm, nsa_k_norm, cmp_pos,
    cmp_w1, cmp_w2, pool_w, pool_scale, w_out, norm_ffn, w_ffn1, w_ffn2, g_mix_2, w_in_2,
    b_fgate_2, b_gate_2, lam_q1_2, lam_k1_2, lam_q2_2, lam_k2_2, g_subln_2, w_pa_2, w_pb_2,
    w_o_2, g_moe_2, w_group_2, b_group_2, w_expert_2, b_expert_2, w1_2, w3_2, w2_2, g_final_2,
):
    x = first_block(
        x, norm_mix, w_in, conv_w, a_log, dt_bias, gdn_norm, nsa_q_norm, nsa_k_norm, cmp_pos,
        cmp_w1, cmp_w2, pool_w, pool_scale, w_out, norm_ffn, w_ffn1, w_ffn2,
    )
    return second_block(
        x, g_mix_2, w_in_2, b_fgate_2, b_gate_2, lam_q1_2, lam_k1_2, lam_q2_2, lam_k2_2,
        g_subln_2, w_pa_2, w_pb_2, w_o_2, g_moe_2, w_group_2, b_group_2, w_expert_2, b_expert_2,
        w1_2, w3_2, w2_2, g_final_2,
    )


_drawn_inputs = setup_inputs


def setup_inputs(seed=0):
    import zlib

    import numpy as np

    out = dict(_drawn_inputs(seed))
    spreads = {}
    factors = {'norm_mix': 2.941,
     'gdn_norm': 5.953,
     'nsa_q_norm': 8.0,
     'nsa_k_norm': 8.0,
     'g_mix_2': 4.197,
     'lam_q1_2': 8.0,
     'lam_k1_2': 6.343,
     'lam_q2_2': 3.446,
     'lam_k2_2': 2.944,
     'g_subln_2': 4.478,
     'g_moe_2': 5.411,
     'b_group_2': 4.885,
     'b_expert_2': 6.787,
     'g_final_2': 5.639}
    for name, (base, spread) in spreads.items():
        noise = np.random.default_rng([zlib.crc32(name.encode()), seed]).standard_normal(out[name].shape)
        drawn = base * np.exp(spread * noise) if base else spread * noise
        out[name] = __import__('jax').numpy.asarray(drawn.astype(out[name].dtype))
    for name, factor in factors.items():
        out[name] = (out[name] * factor).astype(out[name].dtype)
    return out
```

```python
from contextlib import ExitStack

import numpy as np
import concourse.bass as bass
from concourse import mybir

F32 = mybir.dt.float32
I32 = mybir.dt.int32
ALU = mybir.AluOpType
ACT = mybir.ActivationFunctionType
AX = mybir.AxisListType.X

P = 128
T = 256
NT = T // P
D = 1024
KD = D // P
HD = 64
EPS = 1e-6
NEG = -1e30
GH = 6
CHUNK = 64
NCH = T // CHUNK
GW = GH * HD
CONV = 4
QF = 3 * GW // P
NH = 6
NKV = 2
NG = NH // NKV
CMP_LEN, CMP_STRIDE, CMP_HID = 32, 16, 256
NC = T // CMP_STRIDE - CMP_LEN // CMP_STRIDE + 1
CM = CMP_LEN * HD // P
POOLS = (2, 4, 8, 16)
FF = 4096
FT = FF // P
FOX = 8
DIF = 4
LAM0 = 0.8 - 0.6 * 1.0
EXPERTS = 32
NGRP = 4
DE = D // 2
CAP = 64
PAIRS = EXPERTS // 2
MAXPASS = T // CAP

CONSTS = {}
_at = 0
for _name, _w in (
    ("ident", P), ("le_chunk", P), ("gt_chunk", P), ("chunk0", P), ("chunk1", P), ("head_diag", P),
    ("invmask", 6 * P), ("le", P), ("gt", P), ("ones", P), ("lt", P), ("causal", 3 * P), ("slot", CAP),
    ("cmp_add", NT * NC), ("cmp_mul", NT * NC), ("rank32", EXPERTS), ("rank4", NGRP),
):
    CONSTS[_name] = (_at, _w)
    _at += _w
NCONST = _at
NBAND = 4 * 3 * P


def shape_constants():
    r = np.arange(P)
    row, col = r[:, None], r[None, :]
    same = (row // CHUNK) == (col // CHUNK)
    c = np.zeros((P, NCONST), np.float32)

    def put(name, a):
        at, w = CONSTS[name]
        c[:, at:at + w] = np.asarray(a, np.float32).reshape(P, w)

    put("ident", row == col)
    put("le_chunk", (row <= col) & same)
    put("gt_chunk", (row > col) & same)
    put("chunk0", np.broadcast_to(row < CHUNK, (P, P)))
    put("chunk1", np.broadcast_to(row >= CHUNK, (P, P)))
    put("head_diag", (row // HD) == (col // HD))
    put("invmask", np.stack([
        ((row // (2 * m)) == (col // (2 * m))) & ((row // m) % 2 == 1) & ((col // m) % 2 == 0)
        for m in (1, 2, 4, 8, 16, 32)], axis=1))
    put("le", row <= col)
    put("gt", row > col)
    put("ones", np.ones((P, P)))
    put("lt", row < col)
    put("causal", np.concatenate([
        np.where(col <= row, 0.0, NEG), np.zeros((P, P)), np.where(col <= row, 0.0, NEG)], axis=1))
    put("slot", np.broadcast_to(np.arange(CAP), (P, CAP)))
    end = np.arange(NC) * CMP_STRIDE + CMP_LEN - 1
    tok = np.arange(NT)[None, :, None] * P + r[:, None, None]
    valid = end[None, None, :] <= tok
    put("cmp_add", np.where(valid, 0.0, NEG))
    put("cmp_mul", valid)
    put("rank32", np.broadcast_to(np.arange(EXPERTS), (P, EXPERTS)))
    put("rank4", np.broadcast_to(np.arange(NGRP), (P, NGRP)))

    s, t = np.arange(T)[:, None], np.arange(T)[None, :]
    band = np.zeros((P, 4, 3 * P), np.float32)
    for g, w in enumerate(POOLS):
        m = np.where((s <= t) & (s > t - w), 1.0 / np.minimum(t + 1, w), 0.0) - (s == t)
        band[:, g, 0:T] = m[0:P]
        band[:, g, T:] = m[P:, P:]
    alibi = np.zeros((P, DIF, 3 * P), np.float32)
    for h in range(DIF):
        b = np.where((t // CHUNK) <= (s // CHUNK), -(2.0 ** (-8.0 / DIF * (h + 1))) * np.abs(s - t), NEG)
        alibi[:, h, 0:P] = b[0:P, 0:P]
        alibi[:, h, P:] = b[P:, :]
    return c, band.reshape(P, NBAND), alibi.reshape(P, NBAND)


VEC = {}
_at = 0
for _name, _w in (("norm_mix", 8), ("norm_ffn", 8), ("g_mix", 8), ("g_moe", 8), ("b_gate", 16),
                  ("conv_w", CONV * QF), ("pool_scale", 2), ("cmp_pos", 2 * CM)):
    VEC[_name] = (_at, _w)
    _at += _w
NVEC = _at

ROWS = {}
_at = 0
for _name, _w in (("a_log", GH), ("dt_bias", GH), ("gdn_norm", HD), ("q_norm", HD), ("k_norm", 3 * HD),
                  ("b_fgate", FOX), ("lam_q1", HD), ("lam_k1", HD), ("lam_q2", HD), ("lam_k2", HD),
                  ("g_subln", 2 * HD), ("b_group", NGRP), ("b_expert", EXPERTS)):
    ROWS[_name] = (_at, _w)
    _at += _w
NROWS = _at

GROUPS = []
for _kind, _n in (("nsa", 2 * NH), ("fox", FOX), ("dif", 2 * DIF)):
    GROUPS += [(_kind, 0, m, 4) for m in range(0, _n, 4)]
    GROUPS += [(_kind, 1, m, 2) for m in range(0, _n, 2)]
GFIRST = {k: min(i for i, g in enumerate(GROUPS) if g[0] == k) for k in ("nsa", "fox", "dif")}
GLAST = {k: max(i for i, g in enumerate(GROUPS) if g[0] == k) + 1 for k in ("nsa", "fox", "dif")}


def attention_tasks(kind):
    first, last = GFIRST[kind], GLAST[kind]
    out = []
    for g in range(first, last + 1):
        if g < last:
            out.append(("scores", g))
        if g > first:
            out.append(("probsT", g - 1))
    return out


TASKS = [("vec",)]
TASKS += [("hT", 0, i) for i in range(4)]
TASKS += [("qkv", i) for i in range((QF + 1) // 2)]
for _s in ("z", "baq", "kv4", "kvw", "gu"):
    TASKS += [(_s, t) for t in range(NT)]
TASKS += [("poolT", i) for i in range(2)] + [("poolY", i) for i in range(2)]
TASKS += [("win", k) for k in range(2)] + [("nq", t) for t in range(NT)] + [("nk",)]
TASKS += [("hid", k) for k in range(2)] + [("cmp",), ("kcT",)]
TASKS += [("cs", t) for t in range(NT)] + [("pcT", t) for t in range(NT)]
TASKS += attention_tasks("nsa")
TASKS += [("nsaY", i) for i in range(NH // 2)]
TASKS += [("gc",)] + [("dec", i) for i in range(3)]
TASKS += [("tok", s, t) for s in range(3) for t in range(NT)]
TASKS += [("gT", s, t) for s in ("k", "kb", "q", "qd") for t in range(NT)]
TASKS += [("kk", i) for i in range(GH)]
for _l in range(6):
    for _b in range(3):
        TASKS.append(("invP", _l, _b))
    for _b in range(3):
        TASKS += [("invQ", _l, _b)] if _l < 5 else []
        TASKS.append(("invR", _l, _b))
for _t in range(NT):
    TASKS += [("u", _t), ("wT", _t)]
for _n in range(NCH):
    TASKS += [("wS", _n), ("qS", _n)]
    if _n < NCH - 1:
        TASKS.append(("kV", _n))
    if _n % 2 == 1:
        TASKS.append(("o", _n // 2))
TASKS += [("gdnY", t) for t in range(NT)]
TASKS += [("mix", t, h) for t in range(NT) for h in range(2)]
TASKS += [("hT", 1, i) for i in range(4)]
TASKS += [("ff1", i) for i in range(FT // 2)]
TASKS += [("ff2", t, h) for t in range(NT) for h in range(2)]
TASKS += [("hT", 2, i) for i in range(4)]
TASKS += [("ff",)] + [("fq", i) for i in range(2)] + [("fk", i) for i in range(2)]
TASKS += [("fv", t) for t in range(NT)]
TASKS += [("dq", i) for i in range(2)] + [("dk", i) for i in range(2)]
TASKS += [("dv", t) for t in range(NT)]
TASKS += [("gate", i) for i in range(8)]
TASKS += attention_tasks("fox")
TASKS += [("foxY", i) for i in range(4)]
TASKS += attention_tasks("dif")
TASKS += [("difO", t) for t in range(NT)] + [("difT", t) for t in range(NT)]
TASKS += [("pa", i) for i in range(4)] + [("pb", i) for i in range(4)]
TASKS += [("wo", t, h) for t in range(NT) for h in range(2)]
TASKS += [("hT", 3, i) for i in range(4)]
TASKS += [("route",), ("rank",), ("count",)]
TASK = {name: i for i, name in enumerate(TASKS)}
BANKS = 8

WIN_COLS = [(0, 512), (512, 1024), (1024, 1536), (1536, 1932), (1932, 2444), (2444, 2700), (2700, 2974)]
WIN_LAST = [("qkv", 1), ("qkv", 3), ("z", 1), ("baq", 1), ("kv4", 1), ("kvw", 1), ("gu", 1)]
W2_COLS = [(0, 512, ("fq", 1)), (512, 1024, ("fk", 1)), (1024, 1536, ("fv", 1)),
           (1544, 2056, ("dq", 1)), (2056, 2568, ("dk", 1)), (2568, 3080, ("dv", 1)),
           (3080, 3592, ("gate", 1)), (3592, 4104, ("gate", 3)), (4104, 4616, ("gate", 5)), (4616, 5128, ("gate", 7))]
UNITS = [(("win", i), WIN_LAST[i]) for i in range(7)]
UNITS += [(("cmp1", k), ("hid", k)) for k in range(2)]
UNITS += [(("wout", h), ("mix", 1, h)) for h in range(2)]
UNITS += [(("w1", i), ("ff1", 2 * i + 1)) for i in range(8)]
UNITS += [(("w2", i), None if i < 7 else ("ff2", NT - 1, 1)) for i in range(8)]
UNITS += [(("win2", i), W2_COLS[i][2]) for i in range(10)]
UNITS += [(("pa",), ("pa", 3)), (("pb",), ("pb", 3))]
UNITS += [(("wo2", h), ("wo", 1, h)) for h in range(2)]
UNIT = {name: i for i, (name, _) in enumerate(UNITS)}
SLOTS = 6


def mixer_block_kernel(nc, a, consts, band_c, alibi_c, out):
    with ExitStack() as ctx:
        sems = {}

        def sb(name, shape, dt=F32):
            return ctx.enter_context(nc.sbuf_tensor(name, shape, dt))

        def sem(name):
            if name not in sems:
                sems[name] = ctx.enter_context(nc.semaphore(name))
            return sems[name]

        bank = [ctx.enter_context(nc.psum_tensor(f"bank{i}", [P, 512], F32)) for i in range(BANKS)]

        ring = sb("ring", [P, SLOTS, 4096])
        x_sb = sb("x_sb", [P, NT, D])
        yT = sb("yT", [P, KD, T])
        cst = sb("cst", [P, NCONST])
        bias_c = sb("bias_c", [P, NBAND])
        vrow = sb("vrow", [NVEC, P])
        vT = sb("vT", [P, NVEC])
        rows = sb("rows", [P, NROWS])
        small = sb("small", [P, 1280])
        cw2 = sb("cw2", [P, 2, 2, HD])
        poolw = sb("poolw", [P, 2, P])
        w_ff = sb("w_ff", [P, KD, FOX])
        w_route = sb("w_route", [P, KD, NGRP + EXPERTS])
        passes = sb("passes", [1, 1], I32)
        AR = 19968
        arena = sb("arena", [P, AR])

        def cut(at, *dims):
            n = int(np.prod(dims))
            assert at + n <= AR
            v = arena[:, at:at + n]
            if len(dims) == 2:
                v = v.rearrange("p (a b) -> p a b", b=dims[1])
            elif len(dims) == 3:
                v = v.rearrange("p (a b c) -> p a b c", b=dims[1], c=dims[2])
            elif len(dims) == 4:
                v = v.rearrange("p (a b c d) -> p a b c d", b=dims[1], c=dims[2], d=dims[3])
            return v

        used = [0]

        def tiny(*dims):
            n = int(np.prod(dims))
            at = used[0]
            used[0] += n
            assert used[0] <= 1280
            v = small[:, at:at + n]
            if len(dims) == 2:
                v = v.rearrange("p (a b) -> p a b", b=dims[1])
            elif len(dims) == 3:
                v = v.rearrange("p (a b c) -> p a b c", b=dims[1], c=dims[2])
            return v

        def const(name):
            at, w = CONSTS[name]
            return cst[:, at:at + w]

        def vec(name, i):
            return vT[:, VEC[name][0] + i:VEC[name][0] + i + 1]

        def row(name):
            at, w = ROWS[name]
            return rows[:, at:at + w]

        def wide(ap, n):
            return ap.unsqueeze(2).to_broadcast([ap.shape[0], ap.shape[1], n])

        def over(ap, n):
            return ap.unsqueeze(1).to_broadcast([ap.shape[0], n, ap.shape[1]])

        ident = const("ident")
        band = bias_c[:, :].rearrange("p (g n) -> p g n", g=4)
        alibi = bias_c[:, :].rearrange("p (h n) -> p h n", h=DIF)
        invmask = const("invmask").rearrange("p (l n) -> p l n", l=6)

        xn = cut(0, NT, D)
        hT = cut(2048, KD, T)
        conv = cut(4608, QF, T)
        z_silu = cut(19200, NT, GW)
        nsa_q = cut(6912, NT, NG * NKV, HD)
        nsa_qr = cut(6912, NT, NH * HD)
        nsa_kr = cut(8704, NT, 2, NKV * HD)
        cmp_in = cut(7680, NT, 4, P)
        nsa_k = cut(8704, NT, 2 * NKV, HD)
        nsa_v = cut(9216, NT, 2, NKV * HD)
        pool_in = cut(9728, NT, T)
        poolT = cut(10240, 2, T)
        sq1 = cut(10752, 1024)
        nsa_qT = cut(11776, NH, T)
        nsa_kT = cut(13312, 2, T)
        pc = cut(13824, NT, NG, P)
        pcT = cut(14592, NG, T)
        cmp_win = cut(15360, 4, T)
        cmp_x = cut(16384, 4, CM, NC)
        cmp_h = cut(17408, 2, 2, NKV * NC)
        cmp_vb = cut(17536, NKV, HD)
        cmp_kd = cut(17664, 2 * HD)
        cmp_kT = cut(17792, NKV * NC)
        scores1 = cut(15360, 2, 512)
        probs1 = cut(17920, 2, 512)
        nsa_pT = cut(0, 2 * NH, 3 * P)
        inv_d = cut(0, 12, P)
        inv_t = cut(1536, 12, P)
        inv_p = cut(3072, 12, P)
        g_cols = inv_p
        lT = cut(4608, 12, P)
        qkT = cut(6144, 12, P)
        g_q, g_k, g_v = (cut(7680 + 768 * i, 12, HD) for i in range(3))
        g_qk = cut(7680, 24, HD)
        g_qr, g_kr, g_kbr, g_qdr, g_kdr = (cut(at, NT, GW) for at in (7680, 8448, 9984, 11520, 12288))
        g_kb, g_kbe, g_qd, g_kd = (cut(9984 + 768 * i, 12, HD) for i in range(4))
        g_kT = cut(13056, 3, T)
        g_kbqT = cut(13824, GH, 2, T)
        g_qdT = cut(16896, 3, T)
        decay = cut(17664, 12, P)
        g_sq = cut(13824, 24, HD)
        g_wT = cut(7680, 3, T)
        g_vn = cut(8448, NT, GW)
        g_u = cut(9984, NT, GW)
        g_o = cut(13824, NT, GW)
        g_state = cut(14592, 3, P)
        g_upd = cut(14976, 3, P)
        g_osq = cut(15360, NT, GW)
        g_y = cut(16128, NT, GW)
        ff_hT = cut(4608, FT, T)
        ff_r = cut(12800, 2, 512)
        gates = cut(4608, 16, T)
        fqT = cut(8704, FOX, T)
        fkT = cut(10752, FOX // 2, T)
        dqT = cut(11776, 2 * DIF, T)
        dkT = cut(13824, DIF, T)
        fv = cut(14848, NT, FOX * HD)
        dv = cut(15872, NT, 2 * DIF * HD)
        f_cols = cut(16896, NT, FOX, P)
        scores2 = cut(18944, 2, 512)
        probs2 = cut(0, 2, 512)
        fox_pT = cut(1024, FOX, 3 * P)
        dif_pT = cut(1024, DIF, 3 * P)
        oaT = cut(10752, 4, T)
        obT = cut(13824, 4, T)
        dif_o = cut(16896, NT * DIF, 2 * HD)
        dif_sq = cut(17920, NT * DIF, 2 * HD)
        mix_b = cut(14848, 2, 512)
        xg = cut(4608, 2, KD, P)
        act1 = cut(6656, 512)
        act = cut(7168, 512)
        actT = cut(7680, 4, P)
        y_e = cut(8192, D)
        pick = cut(9216, 2, NT, P)
        give = cut(9728, 2, NT, P)
        giveT = cut(10240, NT, P)
        final_g = yT[:, 0:D // T, :].rearrange("p a b -> p (a b)")
        out_sb = cut(11520, NT, D)
        spos = cut(13568, NT, EXPERTS + 2)
        swgt = cut(13568 + 128, NT, EXPERTS + 2)
        r_a = cut(14080, NT, EXPERTS)
        r_b = cut(14080 + 64, NT, EXPERTS)
        r_c = cut(14080 + 128, NT, EXPERTS)
        r_l = cut(14080 + 192, NT, EXPERTS)
        r_hot1 = cut(14080 + 256, NT, EXPERTS)
        r_hot2 = cut(14080 + 320, NT, EXPERTS)
        r_hot = cut(14080 + 384, NT, EXPERTS)

        ssx, rsx = tiny(5, NT), tiny(5, NT)
        n_ss, n_rs = tiny(16 + 8), tiny(16 + 8)
        kc_ss, kc_rs, kc_raw, kc_sq = tiny(1), tiny(1), tiny(HD), tiny(HD)
        nsa_gate = tiny(NT, NH * 3)
        c_mx, c_sm, c_sc = tiny(NT, NH), tiny(NT, NH), tiny(NT, NH * NC)
        mx, nmx, esum, coef = tiny(2, 4), tiny(2, 4), tiny(2, 4), tiny(2, 4)
        ba, beta, g_log, g_t1, g_t2 = tiny(NT, 2 * GH), tiny(12), tiny(12), tiny(12), tiny(12)
        g_x = tiny(12)
        ealog = tiny(GH)
        e_gc, e_rest, e_last = tiny(12), tiny(12), tiny(NCH, 3)
        gq_ss, gq_rs = tiny(24), tiny(24)
        go_ss, go_rs = tiny(12), tiny(12)
        f_x, f_t, f_log = tiny(NT, FOX), tiny(NT, FOX), tiny(NT, FOX)
        lam_p, lam_s, lam = tiny(2, HD), tiny(2), tiny(1)
        d_ss, d_rs = tiny(NT * DIF), tiny(NT * DIF)
        logit = tiny(NT, NGRP + EXPERTS)
        gm, ghot, gtmp, gidx, gsum, gw = tiny(NT), tiny(NT, NGRP), tiny(NT, NGRP), tiny(NT), tiny(NT), tiny(NT)
        m1, m2, i1, i2, e21, den, w1s, w2s = (tiny(NT) for _ in range(8))
        cnt = tiny(EXPERTS)
        cmax = tiny(4)

        def filled(eng, *task):
            eng.wait_ge(sem("psum_full"), TASK[task] + 1)
            return bank[TASK[task] % BANKS]

        def emptied(*task):
            return sem(f"bank_free{TASK[task] % BANKS}")

        def taken(eng, *task):
            eng.wait_ge(emptied(*task), TASK[task] // BANKS + 1)

        class Chain:

            def __init__(self, eng, name):
                self.eng, self.sem, self.n = eng, sem(name), 0

            def __call__(self, ins):
                self.n += 1
                ins.then_inc(self.sem, 1)

            def own(self):
                if self.n:
                    self.eng.wait_ge(self.sem, self.n)

        def unit(name):
            return ring[:, UNIT[name] % SLOTS, :]

        def landed(eng, name):
            eng.wait_ge(sem(f"landed{UNIT[name] % SLOTS}"), 16 * (UNIT[name] // SLOTS + 1))

        NA = len(UNITS)
        eslot = [(NA + k) % SLOTS for k in range(6)]
        ebase = [len([u for u in range(NA) if u % SLOTS == s]) for s in eslot]

        def unit_source(name):
            kind = name[0]
            if kind == "win":
                lo, hi = WIN_COLS[name[1]]
                return a["w_in"][0][:, lo:hi].rearrange("(k p) n -> p k n", p=P)
            if kind == "cmp1":
                return a["cmp_w1"][0, name[1]].rearrange("(k p) n -> p k n", p=P)
            if kind == "wout":
                return a["w_out"][0][:, name[1] * 512:(name[1] + 1) * 512].rearrange("(k p) n -> p k n", p=P)
            if kind == "w1":
                return a["w_ffn1"][0][:, name[1] * 512:(name[1] + 1) * 512].rearrange("(k p) n -> p k n", p=P)
            if kind == "w2":
                return a["w_ffn2"][0][name[1] * 512:(name[1] + 1) * 512, :].rearrange("(k p) n -> p k n", p=P)
            if kind == "win2":
                lo, hi = W2_COLS[name[1]][:2]
                return a["w_in_2"][0][:, lo:hi].rearrange("(k p) n -> p k n", p=P)
            if kind == "pa":
                return a["w_pa_2"][0].rearrange("(k p) n -> p k n", p=P)
            if kind == "pb":
                return a["w_pb_2"][0].rearrange("(k p) n -> p k n", p=P)
            return a["w_o_2"][0][:, name[1] * 512:(name[1] + 1) * 512].rearrange("(k p) n -> p k n", p=P)

        def unit_view(name):
            src = unit_source(name)
            k, n = src.shape[1], src.shape[2]
            return unit(name)[:, 0:k * n].rearrange("p (k n) -> p k n", k=k)

        def expert_view(k):
            v = ring[:, eslot[k], :]
            return v.rearrange("p (k n) -> p k n", n=512 if k < 4 else D)

        block = ctx.enter_context(nc.Block())

        @block.sync
        def _(sp):
            sp.dma_start(x_sb[:, :, :], a["x"][0].rearrange("(t p) n -> p t n", p=P)).then_inc(sem("x_in"), 16)
            for u, (name, _) in enumerate(UNITS):
                if u >= SLOTS:
                    before, last = UNITS[u - SLOTS]
                    if last is None:
                        sp.wait_ge(sem("w2_used"), before[1] + 1)
                    else:
                        sp.wait_ge(sem("psum_full"), TASK[last] + 1)
                sp.dma_start(unit_view(name), unit_source(name)).then_inc(sem(f"landed{u % SLOTS}"), 16)

            def expert_unit(k, pair, shown=None):
                w = a[("w1_2", "w3_2", "w2_2")[k // 2]][0]
                src = w[pair * 2 + k % 2].rearrange("(k p) n -> p k n", p=P)
                sp.dma_start(expert_view(k), src).then_inc(sem(f"landed{eslot[k]}"), 16)

            def slot_free(k, it):
                sp.wait_ge(sem(("h1_full", "h3_full", "y_full")[k // 2]), it * (1 if k < 4 else 2))

            for k in range(6):
                before, last = UNITS[NA - SLOTS + k]
                sp.wait_ge(sem("psum_full"), TASK[last] + 1)
                expert_unit(k, 0)
            with sp.Fori(1, PAIRS) as it:
                for k in range(6):
                    slot_free(k, it)
                    expert_unit(k, it)
            sp.wait_ge(sem("passes_known"), 1)
            n = sp.value_load(passes[0:1, 0:1], min_val=1, max_val=MAXPASS)
            with sp.If(n > 1):
                with sp.Fori(1, n) as p:
                    with sp.Fori(0, PAIRS) as pair:
                        for k in range(6):
                            slot_free(k, p * PAIRS + pair)
                            expert_unit(k, pair)
            with sp.Else():
                sp.nop()
            for t in range(NT):
                sp.wait_ge(sem("out_ready"), t + 1)
                sp.dma_start(out[0, t * P:(t + 1) * P, :], out_sb[:, t, :]).then_inc(sem("out_done"), 16)
            sp.wait_ge(sem("out_done"), 16 * NT)

        @block.tensor
        def _(pe):
            nxt = [0]

            def empty(*task):
                i = TASK[task]
                assert i == nxt[0], (task, TASKS[nxt[0]])
                nxt[0] += 1
                if i >= BANKS:
                    pe.wait_ge(sem(f"bank_free{i % BANKS}"), i // BANKS)
                return bank[i % BANKS]

            def full(mm):
                mm.then_inc(sem("psum_full"), 1)

            def turn(out_ap, in_ap):
                k = in_ap.shape[0]
                return pe.transpose(out_ap, in_ap, ident[0:k, 0:k])

            def turn_rows(stage):
                for i in range(4):
                    b = empty("hT", stage, i)
                    if i == 0:
                        pe.wait_ge(sem("xn_ready"), NT * (stage + 1))
                    for kk in range(2):
                        for t in range(NT):
                            k = 2 * i + kk
                            mm = turn(b[:, kk * T + t * P:kk * T + (t + 1) * P], xn[:, t, k * P:(k + 1) * P])
                    full(mm)

            def hT_ready(stage):
                for i in range(4):
                    taken(pe, "hT", stage, i)

            def features(task, unit_name, cols, group, src=None, k_tiles=KD):
                b = empty(*task)
                landed(pe, unit_name)
                w = unit_view(unit_name)
                src = hT if src is None else src
                for j in range(group):
                    c = cols + j * P
                    for k in range(k_tiles):
                        mm = pe.matmul(b[:, j * T:(j + 1) * T], w[:, k, c:c + P], src[:, k, :],
                                       start=(k == 0), stop=(k == k_tiles - 1))
                full(mm)

            def tokens(task, unit_name, t, cols=0, width=None, src=None):
                b = empty(*task)
                landed(pe, unit_name)
                w = unit_view(unit_name)
                width = w.shape[2] - cols if width is None else width
                src = hT if src is None else src
                for k in range(KD):
                    mm = pe.matmul(b[:, 0:width], src[:, k, t * P:(t + 1) * P], w[:, k, cols:cols + width],
                                   start=(k == 0), stop=(k == KD - 1))
                full(mm)

            b = empty("vec")
            pe.wait_ge(sem("const_in"), 16)
            pe.wait_ge(sem("vrow_in"), 16 * len(VEC))
            full(turn(b[:, 0:NVEC], vrow[:, :]))

            turn_rows(0)
            hT_ready(0)
            for i in range(5):
                features(("qkv", i), ("win", i // 2), (i % 2) * 2 * P, 2 if i < 4 else 1)
            for t in range(NT):
                tokens(("z", t), ("win", 2), t, P, GW)
            for s, u in (("baq", 3), ("kv4", 4), ("kvw", 5), ("gu", 6)):
                for t in range(NT):
                    tokens((s, t), ("win", u), t)

            for t in range(NT):
                taken(pe, "gu", t)
            pe.wait_ge(sem("band_in"), 16)
            pe.wait_ge(sem("poolw_in"), 16 * 4)
            pe.wait_ge(sem("zero_start"), 1)
            for i in range(2):
                b = empty("poolT", i)
                for j in range(2):
                    g = 2 * i + j
                    o = b[j * HD:(j + 1) * HD, 0:T]
                    pe.matmul(o, pool_in[:, 0, g * HD:(g + 1) * HD], band[:, g, 0:T], start=True, stop=False)
                    mm = pe.matmul(o[:, P:T], pool_in[:, 1, g * HD:(g + 1) * HD], band[:, g, T:],
                                   start=False, stop=True)
                full(mm)
            for i in range(2):
                b = empty("poolY", i)
                taken(pe, "poolT", i)
                full(pe.matmul(b[:, 0:T], poolw[:, i, :], poolT[:, i, :], start=True, stop=True))

            for k in range(2):
                b = empty("win", k)
                for t in range(NT):
                    taken(pe, "kv4", t)
                for j in range(NKV):
                    for t in range(NT):
                        mm = turn(b[:, (j * NT + t) * P:(j * NT + t + 1) * P], cmp_in[:, t, 2 * k + j, :])
                full(mm)
            for t in range(NT):
                b = empty("nq", t)
                pe.wait_ge(sem("nsa_qk_ready"), 1)
                for g in range(NG):
                    mm = turn(b[:, g * P:(g + 1) * P], nsa_qr[:, t, g * P:(g + 1) * P])
                full(mm)
            b = empty("nk")
            for s in range(2):
                for t in range(NT):
                    mm = turn(b[:, (s * NT + t) * P:(s * NT + t + 1) * P], nsa_kr[:, t, s, :])
            full(mm)
            for k in range(2):
                b = empty("hid", k)
                landed(pe, ("cmp1", k))
                pe.wait_ge(sem("cmp_x_ready"), k + 1)
                w = unit_view(("cmp1", k))
                for i in range(2):
                    for m in range(CM):
                        mm = pe.matmul(b[:, i * NKV * NC:(i + 1) * NKV * NC].rearrange("p (a b) -> p a b", a=NKV),
                                       w[:, m, i * P:(i + 1) * P],
                                       cmp_x[:, 2 * k:2 * k + 2, m, :], start=(m == 0), stop=(m == CM - 1))
                full(mm)
            b = empty("cmp")
            for k in range(2):
                taken(pe, "hid", k)
            pe.wait_ge(sem("cw2_in"), 16)
            for i in range(2):
                pe.matmul(b[0:NKV * NC, 0:HD], cmp_h[:, 0, i, :], cw2[:, 0, i, :], start=(i == 0), stop=(i == 1))
            for j in range(NKV):
                for i in range(2):
                    mm = pe.matmul(b[j * HD:j * HD + NC, P:P + HD], cmp_h[:, 1, i, j * NC:(j + 1) * NC],
                                   cw2[:, 1, i, :], start=(i == 0), stop=(i == 1))
            full(mm)
            b = empty("kcT")
            pe.wait_ge(sem("kc_ready"), 1)
            full(turn(b[:, 0:NKV * NC], cmp_kd[0:NKV * NC, :]))
            for t in range(NT):
                b = empty("cs", t)
                taken(pe, "nq", t)
                taken(pe, "kcT")
                for h in range(NH):
                    j = h % 2
                    mm = pe.matmul(b[:, h * NC:(h + 1) * NC], nsa_qT[:, h, t * P:(t + 1) * P],
                                   cmp_kT[:, j * NC:(j + 1) * NC], start=True, stop=True)
                full(mm)
            for t in range(NT):
                b = empty("pcT", t)
                pe.wait_ge(sem("pc_ready"), t + 1)
                for g in range(NG):
                    mm = turn(b[:, g * P:(g + 1) * P], pc[:, t, g, :])
                full(mm)

            def scores(g):
                kind, t, m0, n = GROUPS[g]
                b = empty("scores", g)
                if kind == "nsa":
                    taken(pe, "nq", t)
                    taken(pe, "nk")
                W = P * (t + 1)
                q = slice(t * P, (t + 1) * P)
                if kind == "nsa":
                    for s in range(n // 2):
                        mm = pe.matmul(b[:, s * 2 * W:(s + 1) * 2 * W].rearrange("p (a b) -> p a b", a=2),
                                       nsa_qT[:, m0 // 2 + s, q], nsa_kT[:, :, 0:W], start=True, stop=True)
                for i in range(n if kind == "fox" else 0):
                    h = m0 + i
                    o = b[:, i * W:(i + 1) * W]
                    pe.matmul(o, fqT[:, h, q], fkT[:, h // 2, 0:W], start=True, stop=False)
                    if t == 0:
                        mm = pe.matmul(o, const("le"), f_cols[:, 0, h, :], start=False, stop=True)
                    else:
                        pe.matmul(o[:, 0:P], const("ones"), f_cols[:, 0, h, :], start=False, stop=False)
                        pe.matmul(o[:, 0:P], const("le"), f_log[:, 1, h:h + 1].to_broadcast([P, P]),
                                  start=False, stop=False)
                        mm = pe.matmul(o[:, P:2 * P], const("le"), f_cols[:, 1, h, :], start=False, stop=True)
                for i in range(n if kind == "dif" else 0):
                    m = m0 + i
                    mm = pe.matmul(b[:, i * W:(i + 1) * W], dqT[:, m, q], dkT[:, m // 2, 0:W], start=True, stop=True)
                full(mm)

            def probs_turned(g):
                kind, t, m0, n = GROUPS[g]
                b = empty("probsT", g)
                pe.wait_ge(sem("probs_ready"), g + 1)
                pr = (probs1 if kind == "nsa" else probs2)[:, g % 2, :]
                W = P * (t + 1)
                at = 0
                for i in range(0, n, 2 if kind == "dif" else 1):
                    for kt in range(t + 1):
                        mm = turn(b[:, at:at + P], pr[:, i * W + kt * P:i * W + (kt + 1) * P])
                        at += P
                full(mm)

            def attention(kind):
                for task in attention_tasks(kind):
                    (scores if task[0] == "scores" else probs_turned)(task[1])
                taken(pe, "probsT", GLAST[kind] - 1)

            attention("nsa")
            for t in range(NT):
                taken(pe, "pcT", t)
            for i in range(NH // 2):
                b = empty("nsaY", i)
                for step in range(5):
                    for hh in range(2):
                        h = 2 * i + hh
                        g, j = h % NG, h // NG
                        m = 2 * (2 * g + j)
                        o = b[hh * HD:(hh + 1) * HD, 0:T]
                        v = slice(j * HD, (j + 1) * HD)
                        if step == 0:
                            mm = pe.matmul(o, cmp_vb[:, j, :], pcT[:, g, :], start=True, stop=False)
                        elif step < 3:
                            s = step - 1
                            mm = pe.matmul(o, nsa_v[:, 0, s, v], nsa_pT[:, m + s, 0:T], start=False, stop=False)
                        else:
                            s = step - 3
                            mm = pe.matmul(o[:, P:T], nsa_v[:, 1, s, v], nsa_pT[:, m + s, T:3 * P],
                                           start=False, stop=(step == 4))
                full(mm)

            b = empty("gc")
            pe.wait_ge(sem("g_log_ready"), 1)
            for t in range(NT):
                pe.matmul(b[:, t * GH:(t + 1) * GH], const("le_chunk"), g_log[:, t * GH:(t + 1) * GH], start=True, stop=True)
                pe.matmul(b[:, 12 + t * GH:12 + (t + 1) * GH], const("gt_chunk"), g_log[:, t * GH:(t + 1) * GH],
                          start=True, stop=True)
            for n in range(NCH):
                mm = pe.matmul(b[:, 24 + n * GH:24 + (n + 1) * GH], const(f"chunk{n % 2}"),
                               g_log[:, (n // 2) * GH:(n // 2 + 1) * GH], start=True, stop=True)
            full(mm)
            for i in range(3):
                b = empty("dec", i)
                pe.wait_ge(sem("g_cols_ready"), 1)
                full(pe.matmul(b[:, :].rearrange("p (a b) -> p a b", b=P), const("gt_chunk"),
                               g_cols[:, 4 * i:4 * i + 4, :], start=True, stop=True))
            for s in range(3):
                for t in range(NT):
                    b = empty("tok", s, t)
                    pe.wait_ge(sem("conv_ready"), 1)
                    for j in range(3):
                        mm = turn(b[:, j * P:(j + 1) * P], conv[:, 3 * s + j, t * P:(t + 1) * P])
                    full(mm)
            for s, src in (("k", g_kr), ("kb", g_kbr), ("q", g_qr), ("qd", g_qdr)):
                for t in range(NT):
                    b = empty("gT", s, t)
                    pe.wait_ge(sem("g_tok_ready"), {"k": 1, "kb": 2, "q": 1, "qd": 2}[s])
                    if s == "qd":
                        pe.wait_ge(sem("g_pool_ready"), 1)
                    for j in range(3):
                        mm = turn(b[:, j * P:(j + 1) * P], src[:, t, j * P:(j + 1) * P])
                    full(mm)
            for i in range(GH):
                b = empty("kk", i)
                t, p = i // 3, i % 3
                for s in ("k", "kb", "q"):
                    taken(pe, "gT", s, t)
                for hh in range(2):
                    mm = pe.matmul(b[:, hh * 2 * P:(hh + 1) * 2 * P].rearrange("p (a b) -> p a b", a=2),
                                   g_kT[:, p, t * P:(t + 1) * P], g_kbqT[:, 2 * p + hh, :, t * P:(t + 1) * P],
                                   start=True, stop=True)
                full(mm)
            for lev in range(6):
                for bt in range(3):
                    b = empty("invP", lev, bt)
                    if lev == 0:
                        pe.wait_ge(sem("inv_start"), 2)
                        taken(pe, "kk", 2 * bt)
                        taken(pe, "kk", 2 * bt + 1)
                    else:
                        taken(pe, "invQ", lev - 1, bt)
                    for u in range(4):
                        mm = pe.matmul(b[:, u * P:(u + 1) * P], lT[:, 4 * bt + u, :], inv_d[:, 4 * bt + u, :],
                                       start=True, stop=True)
                    full(mm)
                for bt in range(3):
                    if lev < 5:
                        b = empty("invQ", lev, bt)
                        taken(pe, "invP", lev, bt)
                        if lev > 0:
                            taken(pe, "invR", lev - 1, bt)
                        for u in range(4):
                            mm = pe.matmul(b[:, u * P:(u + 1) * P], inv_t[:, 4 * bt + u, :], inv_p[:, 4 * bt + u, :],
                                           start=True, stop=True)
                        full(mm)
                    b = empty("invR", lev, bt)
                    taken(pe, "invP", lev, bt)
                    if lev > 0:
                        taken(pe, "invR", lev - 1, bt)
                    for u in range(4):
                        mm = pe.matmul(b[:, u * P:(u + 1) * P], inv_p[:, 4 * bt + u, :], inv_t[:, 4 * bt + u, :],
                                       start=True, stop=True)
                    full(mm)
            for t in range(NT):
                b = empty("u", t)
                for bt in range(3):
                    taken(pe, "invR", 5, bt)
                pe.wait_ge(sem("g_tok_ready"), 3)
                for h in range(GH):
                    mm = pe.matmul(b[:, h * HD:(h + 1) * HD], inv_t[:, t * GH + h, :], g_v[:, t * GH + h, :],
                                   start=True, stop=True)
                full(mm)
                b = empty("wT", t)
                for h in range(GH):
                    mm = pe.matmul(b[(h % 2) * HD:(h % 2 + 1) * HD, (h // 2) * P:(h // 2 + 1) * P],
                                   g_kbe[:, t * GH + h, :], inv_t[:, t * GH + h, :], start=True, stop=True)
                full(mm)
            for n in range(NCH):
                t, lo = n // 2, (n % 2) * CHUNK
                tok = slice(n * CHUNK, (n + 1) * CHUNK)
                b = empty("wS", n)
                taken(pe, "u", t)
                taken(pe, "wT", t)
                taken(pe, "gT", "qd", t)
                pe.wait_ge(sem("state_ready"), n + 1)
                for p in range(3):
                    mm = pe.matmul(b[lo:lo + CHUNK, p * P:(p + 1) * P], g_wT[:, p, tok], g_state[:, p, :],
                                   start=True, stop=True)
                full(mm)
                b = empty("qS", n)
                for p in range(3):
                    mm = pe.matmul(b[lo:lo + CHUNK, p * P:(p + 1) * P], g_qdT[:, p, tok], g_state[:, p, :],
                                   start=True, stop=True)
                full(mm)
                if n < NCH - 1:
                    b = empty("kV", n)
                    taken(pe, "wS", n)
                    for p in range(3):
                        mm = pe.matmul(b[:, p * P:(p + 1) * P], g_kdr[lo:lo + CHUNK, t, p * P:(p + 1) * P],
                                       g_vn[lo:lo + CHUNK, t, p * P:(p + 1) * P], start=True, stop=True)
                    full(mm)
                if n % 2 == 1:
                    b = empty("o", t)
                    taken(pe, "wS", n)
                    for h in range(GH):
                        mm = pe.matmul(b[:, h * HD:(h + 1) * HD], qkT[:, t * GH + h, :],
                                       g_vn[:, t, h * HD:(h + 1) * HD], start=True, stop=True)
                    full(mm)
            for t in range(NT):
                b = empty("gdnY", t)
                pe.wait_ge(sem("gdn_y_ready"), 1)
                for j in range(3):
                    mm = turn(b[:, j * P:(j + 1) * P], g_y[:, t, j * P:(j + 1) * P])
                full(mm)

            for task in (("poolY", 0), ("poolY", 1), ("nsaY", 2), ("gdnY", 0), ("gdnY", 1)):
                taken(pe, *task)
            for t in range(NT):
                for h in range(2):
                    tokens(("mix", t, h), ("wout", h), t, src=yT)
            turn_rows(1)
            hT_ready(1)
            for i in range(FT // 2):
                features(("ff1", i), ("w1", i // 2), (i % 2) * 2 * P, 2)
            acc = [empty("ff2", t, h) for t in range(NT) for h in range(2)]
            for i in range(8):
                landed(pe, ("w2", i))
                pe.wait_ge(sem("ff_h_ready"), 2 * i + 2)
                w = unit_view(("w2", i))
                for k in range(4):
                    for t in range(NT):
                        for h in range(2):
                            mm = pe.matmul(acc[2 * t + h][:, :], ff_hT[:, 4 * i + k, t * P:(t + 1) * P],
                                           w[:, k, h * 512:(h + 1) * 512],
                                           start=(i == 0 and k == 0), stop=(i == 7 and k == 3))
                            if i == 7 and k == 3:
                                full(mm)
                            elif k == 3 and t == 1 and h == 1:
                                mm.then_inc(sem("w2_used"), 1)

            turn_rows(2)
            hT_ready(2)
            b = empty("ff")
            pe.wait_ge(sem("w_ff_in"), 16)
            for t in range(NT):
                for k in range(KD):
                    mm = pe.matmul(b[:, t * FOX:(t + 1) * FOX], hT[:, k, t * P:(t + 1) * P], w_ff[:, k, :],
                                   start=(k == 0), stop=(k == KD - 1))
            full(mm)
            for s, u in (("fq", 0), ("fk", 1)):
                for i in range(2):
                    features((s, i), ("win2", u), i * 2 * P, 2)
            for t in range(NT):
                tokens(("fv", t), ("win2", 2), t)
            for s, u in (("dq", 3), ("dk", 4)):
                for i in range(2):
                    features((s, i), ("win2", u), i * 2 * P, 2)
            for t in range(NT):
                tokens(("dv", t), ("win2", 5), t)
            for i in range(8):
                features(("gate", i), ("win2", 6 + i // 2), (i % 2) * 2 * P, 2)

            for task in [(s, i) for s in ("fq", "fk", "fv", "dq", "dk", "dv") for i in range(2)]:
                taken(pe, *task)
            pe.wait_ge(sem("f_cols_ready"), NT)
            attention("fox")
            for i in range(4):
                b = empty("foxY", i)
                for kt in range(NT):
                    for hh in range(2):
                        h = 2 * i + hh
                        o = b[hh * HD:(hh + 1) * HD, kt * P:T]
                        mm = pe.matmul(o, fv[:, kt, h * HD:(h + 1) * HD], fox_pT[:, h, kt * T:kt * P + T],
                                       start=(kt == 0), stop=(kt == 1))
                full(mm)
            attention("dif")
            for t in range(NT):
                b = empty("difO", t)
                for h in range(DIF):
                    o = b[:, h * P:(h + 1) * P]
                    if t == 0:
                        mm = pe.matmul(o, dif_pT[:, h, 0:P], dv[:, 0, h * P:(h + 1) * P], start=True, stop=True)
                    else:
                        pe.matmul(o, dif_pT[:, h, P:2 * P], dv[:, 0, h * P:(h + 1) * P], start=True, stop=False)
                        mm = pe.matmul(o, dif_pT[:, h, 2 * P:3 * P], dv[:, 1, h * P:(h + 1) * P],
                                       start=False, stop=True)
                full(mm)
            for t in range(NT):
                b = empty("difT", t)
                pe.wait_ge(sem("dif_o_ready"), 1)
                for h in range(DIF):
                    mm = turn(b[:, h * P:(h + 1) * P], dif_o[:, t * DIF + h, :])
                full(mm)
            for i in range(4):
                taken(pe, "foxY", i)
            for i in range(4):
                features(("pa", i), ("pa",), i * 2 * P, 2, oaT, 4)
            for t in range(NT):
                taken(pe, "difT", t)
            for i in range(4):
                features(("pb", i), ("pb",), i * 2 * P, 2, obT, 4)
            pe.wait_ge(sem("yT2_ready"), 4)
            for t in range(NT):
                for h in range(2):
                    tokens(("wo", t, h), ("wo2", h), t, src=yT)

            turn_rows(3)
            hT_ready(3)
            b = empty("route")
            pe.wait_ge(sem("w_route_in"), 32)
            W = NGRP + EXPERTS
            for t in range(NT):
                for k in range(KD):
                    mm = pe.matmul(b[:, t * W:(t + 1) * W], hT[:, k, t * P:(t + 1) * P], w_route[:, k, :],
                                   start=(k == 0), stop=(k == KD - 1))
            full(mm)
            b = empty("rank")
            pe.wait_ge(sem("hot_ready"), 1)
            pe.matmul(b[:, 0:EXPERTS], const("lt"), r_hot[:, 0, :], start=True, stop=True)
            pe.matmul(b[:, EXPERTS:2 * EXPERTS], const("ones"), r_hot[:, 0, :], start=True, stop=False)
            full(pe.matmul(b[:, EXPERTS:2 * EXPERTS], const("lt"), r_hot[:, 1, :], start=False, stop=True))
            b = empty("count")
            pe.matmul(b[:, 0:EXPERTS], const("ones"), r_hot[:, 0, :], start=True, stop=False)
            full(pe.matmul(b[:, 0:EXPERTS], const("ones"), r_hot[:, 1, :], start=False, stop=True))

            for b in range(BANKS):
                pe.wait_ge(sem(f"bank_free{b}"), len([i for i in range(len(TASKS)) if i % BANKS == b]))
            pe.wait_ge(sem("passes_known"), 1)
            n = pe.value_load(passes[0:1, 0:1], min_val=1, max_val=MAXPASS)
            ps_h1, ps_h3, ps_x0, ps_x1, ps_t, ps_g, ps_y0, ps_y1 = bank
            with pe.Fori(0, n * PAIRS) as it:
                pe.wait_ge(sem("pick_ready"), it + 1)
                pe.wait_ge(sem("added"), it * 4 + 4)
                for half, b in enumerate((ps_x0, ps_x1)):
                    for kk in range(4):
                        k = 4 * half + kk
                        for t in range(NT):
                            mm = pe.matmul(b[:, kk * P:(kk + 1) * P], xn[:, t, k * P:(k + 1) * P],
                                           pick[:, 0, t, :], start=(t == 0), stop=(t == 1))
                    mm.then_inc(sem(f"x{half}_full"), 1)
                for t in range(NT):
                    mm = turn(ps_g[:, t * P:(t + 1) * P], give[:, 0, t, :])
                mm.then_inc(sem("giveT_full"), 1)
                pe.wait_ge(sem("xg0_ready"), it + 1)
                pe.wait_ge(sem("xg1_ready"), it + 1)
                for k, (b, done) in enumerate(((ps_h1, "h1_full"), (ps_h3, "h3_full"))):
                    for e in range(2):
                        pe.wait_ge(sem(f"landed{eslot[2 * k + e]}"), (it + ebase[2 * k + e] + 1) * 16)
                    for kk in range(KD):
                        for e in range(2):
                            mm = pe.matmul(b[e * CAP:(e + 1) * CAP, :], xg[:, 0, kk, e * CAP:(e + 1) * CAP],
                                           expert_view(2 * k + e)[:, kk, :], start=(kk == 0), stop=(kk == KD - 1))
                    mm.then_inc(sem(done), 1)
                pe.wait_ge(sem("act_ready"), it + 1)
                for f in range(4):
                    mm = turn(ps_t[:, f * P:(f + 1) * P], act[:, f * P:(f + 1) * P])
                mm.then_inc(sem("t_full"), 1)
                for e in range(2):
                    pe.wait_ge(sem(f"landed{eslot[4 + e]}"), (it + ebase[4 + e] + 1) * 16)
                pe.wait_ge(sem("actT_ready"), it + 1)
                for h, b in enumerate((ps_y0, ps_y1)):
                    for f in range(4):
                        for e in range(2):
                            mm = pe.matmul(b[e * CAP:(e + 1) * CAP, :], actT[:, f, e * CAP:(e + 1) * CAP],
                                           expert_view(4 + e)[:, f, h * 512:(h + 1) * 512],
                                           start=(f == 0), stop=(f == 3))
                    mm.then_inc(sem("y_full"), 1)
                pe.wait_ge(sem("giveT_ready"), it + 1)
                for h in range(2):
                    pe.wait_ge(sem(f"y{h}_ready"), it + 1)
                    for t in range(NT):
                        b = ((ps_x0, ps_x1), (ps_t, ps_g))[h][t]
                        pe.matmul(b[:, :], giveT[:, t, :], y_e[:, h * 512:(h + 1) * 512],
                                  start=True, stop=True).then_inc(sem("c_full"), 1)

        def rms_reciprocal(chain, ss, rs, n, done):
            chain(nc.scalar.activation(rs, ss, ACT.Ln, scale=1.0 / n, bias=EPS))
            chain.own()
            nc.scalar.activation(rs, rs, ACT.Exp, scale=-0.5).then_inc(sem(done), 1)

        @block.vector
        def _(dve):
            v = Chain(dve, "dve_own")
            TT, TS, STT, RED, CP = (nc.vector.tensor_tensor, nc.vector.tensor_scalar,
                                    nc.vector.scalar_tensor_tensor, nc.vector.tensor_reduce, nc.vector.tensor_copy)

            def normalize(stage):
                for t in range(NT):
                    dve.wait_ge(sem("rms_ready"), stage * NT + t + 1)
                    ins = TS(xn[:, t, :], x_sb[:, t, :], rsx[:, stage, t:t + 1], None, ALU.mult)
                    if stage < 3:
                        ins.then_inc(sem("xn_ready"), 1)
                    else:
                        v(ins)
                        v.own()
                        dve.wait_ge(sem("g_moe_in"), 16)
                        TT(xn[:, t, :], xn[:, t, :], bias_c[:, 0:D], ALU.mult).then_inc(sem("xn_ready"), 1)

            def take_hT(stage, name):
                for i in (0, 2):
                    b = filled(dve, "hT", stage, i)
                    if name is None:
                        CP(hT[:, 2 * i:2 * i + 2, :], b[:, :].rearrange("p (a b) -> p a b", b=T))\
                            .then_inc(emptied("hT", stage, i), 1)
                        continue
                    v(TS(hT[:, 2 * i, :], b[:, 0:T], vec(name, 2 * i), None, ALU.mult))
                    TS(hT[:, 2 * i + 1, :], b[:, T:2 * T], vec(name, 2 * i + 1), None, ALU.mult)\
                        .then_inc(emptied("hT", stage, i), 1)

            def sigmoid_end(ap, count):
                dve.wait_ge(sem("small_exp"), count)
                v(TS(ap, ap, 1.0, None, ALU.add))
                v.own()
                v(nc.vector.reciprocal(ap, ap))

            def add_to_x(*task):
                t, h = task[-2:]
                b = filled(dve, *task)
                o = x_sb[:, t, h * 512:(h + 1) * 512]
                TT(o, b[:, :], o, ALU.add).then_inc(emptied(*task), 1)

            CP(vT[:, :], filled(dve, "vec")[:, 0:NVEC]).then_inc(emptied("vec"), 1)
            taken(dve, "vec")
            normalize(0)
            take_hT(0, "norm_mix")

            for i in range(5):
                b = filled(dve, "qkv", i)
                dve.wait_ge(sem("tap_ready"), i + 1)
                n = 2 if i < 4 else 1
                for s in range(1, CONV):
                    for j in range(n):
                        f = 2 * i + j
                        ins = STT(conv[:, f, s:], b[:, j * T:(j + 1) * T - s], vec("conv_w", (CONV - 1 - s) * QF + f),
                                  conv[:, f, s:], ALU.mult, ALU.add)
                        if s == CONV - 1 and j == n - 1:
                            ins.then_inc(emptied("qkv", i), 1)
                        else:
                            v(ins)
                    v.own()

            taken(dve, "baq", 1)
            dve.wait_ge(sem("rows_in"), 16 * len(ROWS))
            v(TT(g_x.rearrange("p (t h) -> p t h", t=NT), ba[:, :, GH:], over(row("dt_bias"), NT), ALU.add))
            v.own()
            STT(g_t1, g_x, -1.0, g_x, ALU.mult, ALU.max).then_inc(sem("softplus_in"), 1)
            sigmoid_end(beta, 1)
            taken(dve, "gu", 1)
            sigmoid_end(nsa_gate.rearrange("p a b -> p (a b)"), 2)
            dve.wait_ge(sem("softplus_ln"), 1)
            v(STT(g_t2, g_x, 0.0, g_t2, ALU.max, ALU.add))
            v.own()
            v(TS(g_t2, g_t2, -1.0, None, ALU.mult))
            v.own()
            TT(g_log.rearrange("p (t h) -> p t h", t=NT), g_t2.rearrange("p (t h) -> p t h", t=NT),
               over(ealog, NT), ALU.mult).then_inc(sem("g_log_ready"), 1)

            nq = cut(6912, NT * NH, HD)
            nk = cut(8704, NT * 4, HD)
            sq_q, sq_k = cut(0, NT * NH, HD), cut(768, NT * 4, HD)
            taken(dve, "kvw", 1)
            for i in range(4):
                taken(dve, "hT", 0, i)
            v(TT(sq_q, nq, nq, ALU.mult))
            v(TT(sq_k, nk, nk, ALU.mult))
            v.own()
            v(RED(n_ss[:, 0:12], sq_q, AX, ALU.add))
            RED(n_ss[:, 12:20], sq_k, AX, ALU.add).then_inc(sem("n_ss_ready"), 1)
            qn8 = kc_sq
            v(TS(qn8, row("q_norm"), HD ** -0.5, None, ALU.mult))
            dve.wait_ge(sem("n_rs_ready"), 1)
            v(TT(nq, nq, wide(n_rs[:, 0:12], HD), ALU.mult))
            v(TT(nk, nk, wide(n_rs[:, 12:20], HD), ALU.mult))
            v.own()
            v(TT(nq, nq, over(qn8, 12), ALU.mult))
            kn = row("k_norm")
            for t in range(NT):
                for s in range(2):
                    o = cut(8704 + (t * 2 + s) * NKV * HD, NKV, HD)
                    ins = TT(o, o, over(kn[:, (s + 1) * HD:(s + 2) * HD], NKV), ALU.mult)
                    v(ins) if (t, s) != (1, 1) else ins.then_inc(sem("nsa_qk_ready"), 1)

            for i in range(2):
                CP(poolT[:, i, :], filled(dve, "poolT", i)[:, 0:T]).then_inc(emptied("poolT", i), 1)
            for i in range(2):
                TS(yT[:, 6 + i, :], filled(dve, "poolY", i)[:, 0:T], vec("pool_scale", i), None, ALU.mult)\
                    .then_inc(emptied("poolY", i), 1)

            for k in range(2):
                b = filled(dve, "win", k)[:, :].rearrange("p (j t) -> p j t", j=NKV)
                v(CP(cmp_win[0:HD, 2 * k:2 * k + 2, :], b[0:HD, :, :]))
                CP(cmp_win[HD:P, 2 * k:2 * k + 2, 0:T - 1], b[HD:P, :, 1:T]).then_inc(emptied("win", k), 1)
                taken(dve, "win", k)
                for j in range(NKV):
                    w = cmp_win[:, 2 * k + j, :].rearrange("p (b m two) -> p m b two", m=8, two=2)
                    for half in range(2):
                        at = VEC["cmp_pos"][0] + k * CM + half * 8
                        ins = TT(cmp_x[:, 2 * k + j, 8 * half:8 * half + 8, :], w[:, :, half:half + NC, 0],
                                 wide(vT[:, at:at + 8], NC), ALU.add)
                        v(ins) if (j, half) != (1, 1) else ins.then_inc(sem("cmp_x_ready"), 1)
            for k in range(2):
                n = 2 * NKV * NC
                b = filled(dve, "hid", k)
                h = cmp_h[:, k, :, :].rearrange("p a b -> p (a b)")
                sigmoid_end(h, 3 + k)
                v.own()
                TT(h, b[:, 0:n], h, ALU.mult).then_inc(emptied("hid", k), 1)
            b = filled(dve, "cmp")
            r = NKV * NC
            dve.wait_ge(sem("zero_nsa"), 1)
            v(CP(kc_raw[0:r, :], b[0:r, 0:HD]))
            for j in range(NKV):
                ins = CP(cmp_vb[j * HD:j * HD + NC, j, :], b[j * HD:j * HD + NC, P:P + HD])
                v(ins) if j == 0 else ins.then_inc(emptied("cmp"), 1)
            v.own()
            v(TT(kc_sq[0:r, :], kc_raw[0:r, :], kc_raw[0:r, :], ALU.mult))
            v.own()
            RED(kc_ss[0:r, :], kc_sq[0:r, :], AX, ALU.add).then_inc(sem("kc_ss_ready"), 1)
            dve.wait_ge(sem("kc_rs_ready"), 1)
            for i in range(2):
                ins = STT(cmp_kd[0:r, i * HD:(i + 1) * HD], kc_raw[0:r, :], kc_rs[0:r, :], kn[0:r, 0:HD],
                          ALU.mult, ALU.mult)
                v(ins) if i == 0 else ins.then_inc(sem("kc_ready"), 1)
            add, mul = const("cmp_add"), const("cmp_mul")
            for t in range(NT):
                b = filled(dve, "cs", t)
                s = c_sc[:, t, :].rearrange("p (h n) -> p h n", n=NC)
                TT(s, b[:, 0:NH * NC].rearrange("p (h n) -> p h n", n=NC), over(add[:, t * NC:(t + 1) * NC], NH),
                   ALU.add).then_inc(emptied("cs", t), 1)
                taken(dve, "cs", t)
                v(RED(c_mx[:, t, :], s, AX, ALU.max))
                v.own()
                TT(s, s, wide(c_mx[:, t, :], NC), ALU.subtract).then_inc(sem("c_sc_ready"), 1)
            for t in range(NT):
                s = c_sc[:, t, :].rearrange("p (h n) -> p h n", n=NC)
                dve.wait_ge(sem("c_exp_ready"), t + 1)
                v(RED(c_sm[:, t, :], s, AX, ALU.add))
                v.own()
                v(nc.vector.reciprocal(c_sm[:, t, :], c_sm[:, t, :]))
                v(TT(s, s, over(mul[:, t * NC:(t + 1) * NC], NH), ALU.mult))
                v.own()
                gate = nsa_gate[:, t, :].rearrange("p (j g c) -> p g j c", j=NKV, c=3)[:, :, :, 0]
                cs = c_sm[:, t, :].rearrange("p (g j) -> p g j", j=NKV)
                v(TT(cs, cs, gate, ALU.mult))
                v.own()
                o = pc[:, t, :, :].rearrange("p g (j n) -> p (g j) n", j=NKV)[:, :, 0:NC]
                TT(o, s, wide(c_sm[:, t, :], NC), ALU.mult).then_inc(sem("pc_ready"), 1)

            def maxima(g):
                kind, t, m0, n = GROUPS[g]
                b = filled(dve, "scores", g)
                sc = (scores1 if kind == "nsa" else scores2)[:, g % 2, :]
                W = P * (t + 1)
                for i in range(n):
                    if kind == "dif":
                        bias = alibi[:, (m0 + i) // 2, 0:P] if t == 0 else alibi[:, (m0 + i) // 2, P:3 * P]
                    else:
                        bias = const("causal")[:, 0:P] if t == 0 else const("causal")[:, P:3 * P]
                    ins = nc.vector.tensor_tensor_reduce(
                        sc[:, i * W:(i + 1) * W], b[:, i * W:(i + 1) * W], bias, 1.0, -3e38,
                        ALU.add, ALU.max, mx[:, g % 2, i:i + 1])
                    v(ins) if i < n - 1 else ins.then_inc(emptied("scores", g), 1)
                taken(dve, "scores", g)
                TS(nmx[:, g % 2, 0:n], mx[:, g % 2, 0:n], -1.0, None, ALU.mult).then_inc(sem("max_ready"), 1)

            def weights(g):
                kind, t, m0, n = GROUPS[g]
                pr = (probs1 if kind == "nsa" else probs2)[:, g % 2, :]
                W = P * (t + 1)
                c = coef[:, g % 2, 0:n]
                dve.wait_ge(sem("exp_ready"), g + 1)
                v(nc.vector.reciprocal(c, esum[:, g % 2, 0:n]))
                v.own()
                if kind == "nsa":
                    for i in range(n // 2):
                        slot = m0 // 2 + i
                        h = (slot % 2) * NG + slot // 2
                        v(TT(c[:, 2 * i:2 * i + 2], c[:, 2 * i:2 * i + 2], nsa_gate[:, t, 3 * h + 1:3 * h + 3], ALU.mult))
                    v.own()
                if kind == "dif":
                    c2 = c.rearrange("p (a b) -> p a b", b=2)[:, :, 1]
                    v(TS(c2, c2, lam[:, 0:1], None, ALU.mult))
                    v.own()
                    for i in range(0, n, 2):
                        v(TS(pr[:, i * W:(i + 1) * W], pr[:, i * W:(i + 1) * W], c[:, i:i + 1], None, ALU.mult))
                    v.own()
                    for i in range(0, n, 2):
                        ins = STT(pr[:, i * W:(i + 1) * W], pr[:, (i + 1) * W:(i + 2) * W], c[:, i + 1:i + 2],
                                  pr[:, i * W:(i + 1) * W], ALU.mult, ALU.add)
                        v(ins) if i < n - 2 else ins.then_inc(sem("probs_ready"), 1)
                    return
                for i in range(n):
                    ins = TS(pr[:, i * W:(i + 1) * W], pr[:, i * W:(i + 1) * W], c[:, i:i + 1], None, ALU.mult)
                    v(ins) if i < n - 1 else ins.then_inc(sem("probs_ready"), 1)

            def attention(kind):
                for g in range(GFIRST[kind], GLAST[kind] + 1):
                    if g < GLAST[kind]:
                        maxima(g)
                    if g > GFIRST[kind]:
                        weights(g - 1)

            attention("nsa")

            for s in range(3):
                taken(dve, "tok", s, 1)
            v(TT(g_sq, g_qk, g_qk, ALU.mult))
            v.own()
            RED(gq_ss, g_sq, AX, ALU.add).then_inc(sem("gq_ss_ready"), 1)
            dve.wait_ge(sem("gq_rs_ready"), 1)
            v(TS(gq_rs[:, 0:12], gq_rs[:, 0:12], HD ** -0.5, None, ALU.mult))
            v.own()
            TT(g_qk, g_qk, wide(gq_rs, HD), ALU.mult).then_inc(sem("g_tok_ready"), 1)
            dve.wait_ge(sem("g_tok_ready"), 1)
            TT(g_kb, g_k, wide(beta, HD), ALU.mult).then_inc(sem("g_tok_ready"), 1)
            taken(dve, "gc")
            dve.wait_ge(sem("g_tok_ready"), 2)
            v(TT(g_kbe, g_kb, wide(e_gc, HD), ALU.mult))
            TT(g_v, g_v, wide(beta, HD), ALU.mult).then_inc(sem("g_tok_ready"), 1)
            dve.wait_ge(sem("zero_kbq"), 1)
            for t in range(NT):
                b = filled(dve, "gT", "kb", t)[:, 0:GW].rearrange("p (j n) -> p j n", n=P)
                for hh in range(2):
                    r = slice(hh * HD, (hh + 1) * HD)
                    ins = CP(g_kbqT[r, hh::2, 0, t * P:(t + 1) * P], b[r, :, :])
                    v(ins) if hh == 0 else ins.then_inc(emptied("gT", "kb", t), 1)
            dve.wait_ge(sem("decay_ready"), 1)
            for i in range(GH):
                b = filled(dve, "kk", i)[:, :].rearrange("p (u w n) -> p u w n", w=2, n=P)
                d = decay[:, 2 * i:2 * i + 2, :]
                v(TT(lT[:, 2 * i:2 * i + 2, :], b[:, :, 0, :], d, ALU.mult))
                TT(qkT[:, 2 * i:2 * i + 2, :], b[:, :, 1, :], d, ALU.mult).then_inc(emptied("kk", i), 1)
            for lev in range(6):
                for bt in range(3):
                    u = slice(4 * bt, 4 * bt + 4)
                    b = filled(dve, "invP", lev, bt)[:, :].rearrange("p (u n) -> p u n", n=P)
                    TT(inv_p[:, u, :], b, over(invmask[:, lev, :], 4), ALU.mult).then_inc(emptied("invP", lev, bt), 1)
                for bt in range(3):
                    u = slice(4 * bt, 4 * bt + 4)
                    for name, m in ((("invQ", inv_d),) if lev < 5 else ()) + (("invR", inv_t),):
                        b = filled(dve, name, lev, bt)[:, :].rearrange("p (u n) -> p u n", n=P)
                        if lev == 0:
                            dve.wait_ge(sem("inv_start"), 2)
                        TT(m[:, u, :], m[:, u, :], b, ALU.subtract).then_inc(emptied(name, lev, bt), 1)
            for n in range(NCH):
                t, r = n // 2, slice((n % 2) * CHUNK, (n % 2 + 1) * CHUNK)
                b = filled(dve, "wS", n)
                taken(dve, "u", t)
                TT(g_vn[r, t, :], g_u[r, t, :], b[r, 0:GW], ALU.subtract).then_inc(emptied("wS", n), 1)
                if n < NCH - 1:
                    b = filled(dve, "kV", n)[:, 0:GW].rearrange("p (j n) -> p j n", n=P)
                    TT(g_upd, b, over(const("head_diag"), 3), ALU.mult).then_inc(emptied("kV", n), 1)
                    taken(dve, "kV", n)
                    dve.wait_ge(sem("state_ready"), n + 1)
                    taken(dve, "gc")
                    for p in range(3):
                        ins = STT(g_state[:, p, :], g_state[:, p, :], e_last[:, n, p:p + 1], g_upd[:, p, :],
                                  ALU.mult, ALU.add)
                        v(ins) if p < 2 else ins.then_inc(sem("state_ready"), 1)
                if n % 2 == 1:
                    b = filled(dve, "o", t)
                    taken(dve, "qS", n - 1)
                    taken(dve, "qS", n)
                    TT(g_o[:, t, :], g_o[:, t, :], b[:, 0:GW], ALU.add).then_inc(emptied("o", t), 1)
            taken(dve, "o", 1)
            o12 = cut(13824, 12, HD)
            q12 = cut(15360, 12, HD)
            y12 = cut(16128, 12, HD)
            v(TT(q12, o12, o12, ALU.mult))
            v.own()
            RED(go_ss, q12, AX, ALU.add).then_inc(sem("go_ss_ready"), 1)
            v(TT(y12, cut(19200, 12, HD), over(row("gdn_norm"), 12), ALU.mult))
            dve.wait_ge(sem("go_rs_ready"), 1)
            v(TT(o12, o12, wide(go_rs, HD), ALU.mult))
            v.own()
            TT(y12, y12, o12, ALU.mult).then_inc(sem("gdn_y_ready"), 1)

            for t in range(NT):
                for h in range(2):
                    add_to_x("mix", t, h)
            normalize(1)
            take_hT(1, "norm_ffn")
            for i in range(FT // 2):
                taken(dve, "ff1", i)
                r = ff_r[:, i % 2, :].rearrange("p (a b) -> p a b", b=T)
                TT(ff_hT[:, 2 * i:2 * i + 2, :], r, r, ALU.mult).then_inc(sem("ff_h_ready"), 1)
            for t in range(NT):
                for h in range(2):
                    add_to_x("ff2", t, h)

            for i in range(2):
                ins = nc.vector.tensor_tensor_reduce(lam_p[:, i, :], row(f"lam_q{i + 1}"), row(f"lam_k{i + 1}"),
                                                     1.0, 0.0, ALU.mult, ALU.add, lam_s[:, i:i + 1])
            ins.then_inc(sem("lam_in"), 1)
            dve.wait_ge(sem("lam_exp"), 1)
            v(STT(lam, lam_s[:, 1:2], -LAM0, lam_s[:, 0:1], ALU.add, ALU.subtract))
            v(TS(row("g_subln"), row("g_subln"), 1.0 - LAM0, None, ALU.mult))
            normalize(2)
            take_hT(2, "g_mix")
            b = filled(dve, "ff")
            TT(f_x, b[:, 0:NT * FOX].rearrange("p (t h) -> p t h", t=NT), over(row("b_fgate"), NT), ALU.add)\
                .then_inc(emptied("ff"), 1)
            taken(dve, "ff")
            STT(f_t, f_x, -1.0, f_x, ALU.mult, ALU.max).then_inc(sem("softplus_in"), 1)
            dve.wait_ge(sem("softplus_ln"), 2)
            STT(f_log, f_x, 0.0, f_t, ALU.min, ALU.subtract).then_inc(sem("f_log_ready"), 1)

            def take_heads(name, dst, scale):
                dve.wait_ge(sem("zero_q"), 1)
                for i in range(2):
                    b = filled(dve, name, i)[:, :].rearrange("p (a b) -> p a b", b=T)
                    for hh in range(2):
                        r = slice(hh * HD, (hh + 1) * HD)
                        ins = TS(dst[r, 4 * i + hh:4 * i + hh + 3:2, :], b[r, :, :], scale, None, ALU.mult)
                        v(ins) if hh == 0 else ins.then_inc(emptied(name, i), 1)

            take_heads("fq", fqT, HD ** -0.5)
            for t in range(NT):
                CP(fv[:, t, :], filled(dve, "fv", t)[:, :]).then_inc(emptied("fv", t), 1)
            take_heads("dq", dqT, HD ** -0.5)
            for t in range(NT):
                CP(dv[:, t, :], filled(dve, "dv", t)[:, :]).then_inc(emptied("dv", t), 1)
            attention("fox")
            dve.wait_ge(sem("alibi_in"), 16)
            attention("dif")
            for t in range(NT):
                CP(dif_o[:, 4 * t:4 * t + 4, :].rearrange("p a b -> p (a b)"), filled(dve, "difO", t)[:, :])\
                    .then_inc(emptied("difO", t), 1)
            taken(dve, "difO", 0)
            taken(dve, "difO", 1)
            v(TT(dif_sq, dif_o, dif_o, ALU.mult))
            v.own()
            RED(d_ss, dif_sq, AX, ALU.add).then_inc(sem("d_ss_ready"), 1)
            dve.wait_ge(sem("d_rs_ready"), 1)
            v(TT(dif_o, dif_o, wide(d_rs, 2 * HD), ALU.mult))
            v.own()
            TT(dif_o, dif_o, over(row("g_subln"), NT * DIF), ALU.mult).then_inc(sem("dif_o_ready"), 1)
            for i in range(8):
                taken(dve, "gate", i)
            for i in range(4):
                b = filled(dve, "pa", i)[:, :].rearrange("p (a b) -> p a b", b=T)
                TT(yT[:, 2 * i:2 * i + 2, :], gates[:, 2 * i:2 * i + 2, :], b, ALU.mult).then_inc(emptied("pa", i), 1)
            for i in range(4):
                b = filled(dve, "pb", i)[:, :].rearrange("p (a b) -> p a b", b=T)
                m = mix_b[:, i % 2, :].rearrange("p (a b) -> p a b", b=T)
                TT(m, gates[:, 8 + 2 * i:10 + 2 * i, :], b, ALU.mult).then_inc(emptied("pb", i), 1)
                taken(dve, "pb", i)
                y = yT[:, 2 * i:2 * i + 2, :]
                TT(y, y, m, ALU.add).then_inc(sem("yT2_ready"), 1)
                dve.wait_ge(sem("yT2_ready"), i + 1)
            for t in range(NT):
                for h in range(2):
                    add_to_x("wo", t, h)
            normalize(3)
            take_hT(3, None)

            b = filled(dve, "route")
            W = NGRP + EXPERTS
            at = ROWS["b_group"][0]
            TT(logit, b[:, 0:NT * W].rearrange("p (t n) -> p t n", t=NT), over(rows[:, at:at + W], NT), ALU.add)\
                .then_inc(emptied("route"), 1)
            taken(dve, "route")

            def step(ins):
                v(ins)
                v.own()

            def first_largest(src, ranks, top, idx, hot, tmp, n):
                step(RED(top, src, AX, ALU.max))
                step(TT(tmp, src, wide(top, n), ALU.is_equal))
                step(STT(tmp, tmp, -1000.0, over(ranks, NT), ALU.mult, ALU.add))
                step(RED(idx, tmp, AX, ALU.min))
                step(TT(hot, tmp, wide(idx, n), ALU.is_equal))

            gl = logit[:, :, 0:NGRP]
            first_largest(gl, const("rank4"), gm, gidx, ghot, gtmp, NGRP)
            TT(gtmp, gl, wide(gm, NGRP), ALU.subtract).then_inc(sem("group_in"), 1)
            step(TS(ghot, ghot, -NEG, NEG, ALU.mult, ALU.add))
            for t in range(NT):
                o = cut(14080 + 192 + t * EXPERTS, NGRP, EXPERTS // NGRP)
                step(TT(o, logit[:, t, NGRP:].rearrange("p (g e) -> p g e", g=NGRP),
                        wide(ghot[:, t, :], EXPERTS // NGRP), ALU.add))
            first_largest(r_l, const("rank32"), m1, i1, r_hot1, r_a, EXPERTS)
            step(STT(r_b, r_hot1, 3 * NEG, r_l, ALU.mult, ALU.add))
            first_largest(r_b, const("rank32"), m2, i2, r_hot2, r_a, EXPERTS)
            TT(e21, m2, m1, ALU.subtract).then_inc(sem("second_in"), 1)
            TT(r_hot, r_hot1, r_hot2, ALU.add).then_inc(sem("hot_ready"), 1)
            dve.wait_ge(sem("route_exp"), 2)
            step(RED(gsum, gtmp, AX, ALU.add))
            step(TS(den, e21, 1.0, None, ALU.add))
            step(TT(den, den, gsum, ALU.mult))
            step(nc.vector.reciprocal(w1s, den))
            step(TT(w2s, w1s, e21, ALU.mult))
            step(TT(r_a, r_hot1, wide(w1s, EXPERTS), ALU.mult))
            step(TT(r_b, r_hot2, wide(w2s, EXPERTS), ALU.mult))
            step(TT(swgt[:, :, 0:EXPERTS], r_a, r_b, ALU.add))
            step(CP(swgt[:, :, EXPERTS:], swgt[:, :, 0:2]))
            b = filled(dve, "rank")
            s = spos[:, :, 0:EXPERTS]
            dve.wait_ge(sem("hot_ready"), 1)
            STT(s, b[:, 0:NT * EXPERTS].rearrange("p (t e) -> p t e", t=NT), 1.0, r_hot, ALU.add, ALU.mult)\
                .then_inc(emptied("rank"), 1)
            taken(dve, "rank")
            step(TS(s, s, -1.0, None, ALU.add))
            step(TS(spos[:, :, EXPERTS:], spos[:, :, 0:2], -float(CAP), None, ALU.add))
            b = filled(dve, "count")
            RED(cmax[:, 0:1], b[:, 0:EXPERTS], AX, ALU.max).then_inc(emptied("count"), 1)
            taken(dve, "count")
            step(TS(cmax[:, 1:2], cmax[:, 0:1], float(CAP), 1.0, ALU.is_gt, ALU.add))
            for i in range(2, MAXPASS):
                step(STT(cmax[:, i:i + 1], cmax[:, 0:1], float(i * CAP), cmax[:, i - 1:i], ALU.is_gt, ALU.add))
            CP(passes[0:1, 0:1], cmax[0:1, 3:4]).then_inc(sem("passes_known"), 1)

            dve.wait_ge(sem("passes_known"), 1)
            n = dve.value_load(passes[0:1, 0:1], min_val=1, max_val=MAXPASS)
            ps_h3, ps_x0, ps_x1, ps_t, ps_g, ps_y0 = bank[1], bank[2], bank[3], bank[4], bank[5], bank[6]

            def choose(first):
                for t in range(NT):
                    for e in range(2):
                        o = slice(e * CAP, (e + 1) * CAP)
                        pos = spos[:, t, bass.ds(first + e, 1)]
                        v_in = const("slot")
                        TS(pick[:, 0, t, o], v_in, pos, None, ALU.is_equal)
                        ins = TS(give[:, 0, t, o], v_in, pos, swgt[:, t, bass.ds(first + e, 1)],
                                 ALU.is_equal, ALU.mult)
                ins.then_inc(sem("pick_ready"), 1)

            choose(0)
            nc.vector.memset(g_t1[:, 0:1], 0.0).then_inc(sem("added"), 4)
            with dve.Fori(0, n) as p:
                with dve.Fori(0, PAIRS) as pair:
                    it = p * PAIRS + pair
                    dve.wait_ge(sem("x0_full"), it + 1)
                    CP(xg[:, 0, 0:4, :].rearrange("p a b -> p (a b)"), ps_x0[:, :]).then_inc(sem("xg0_ready"), 1)
                    dve.wait_ge(sem("giveT_full"), it + 1)
                    choose(pair * 2 + 2)
                    dve.wait_ge(sem("h3_full"), it + 1)
                    dve.wait_ge(sem("h1_read"), it + 1)
                    TT(act, act1, ps_h3[:, :], ALU.mult).then_inc(sem("act_ready"), 1)
                    dve.wait_ge(sem("y_full"), it * 2 + 1)
                    CP(y_e[:, 0:512], ps_y0[:, :]).then_inc(sem("y0_ready"), 1)
                    for h in range(2):
                        for t in range(NT):
                            dve.wait_ge(sem("c_full"), it * 4 + 2 * h + t + 1)
                            o = x_sb[:, t, h * 512:(h + 1) * 512]
                            b = ((ps_x0, ps_x1), (ps_t, ps_g))[h][t]
                            TT(o, b[:, :], o, ALU.add).then_inc(sem("added"), 1)
                dve.wait_ge(sem("pick_ready"), p * PAIRS + PAIRS + 1)
                TS(spos[:, :, :], spos[:, :, :], -float(CAP), None, ALU.add).then_inc(sem("next_slots"), 1)
                dve.wait_ge(sem("next_slots"), p + 1)

            dve.wait_ge(sem("final_g_in"), 16)
            for t in range(NT):
                dve.wait_ge(sem("rms_ready"), 4 * NT + t + 1)
                STT(out_sb[:, t, :], x_sb[:, t, :], rsx[:, 4, t:t + 1], final_g, ALU.mult, ALU.mult)\
                    .then_inc(sem("out_ready"), 1)

        @block.scalar
        def _(act):
            c = Chain(act, "act_own")
            ACTV, CPY = nc.scalar.activation, ACT.Copy

            act.dma_start(cst[:, :], consts).then_inc(sem("const_in"), 16)
            for name, (at, w) in VEC.items():
                src = {"norm_mix": a["norm_mix"][0].rearrange("(k p) -> k p", p=P),
                       "norm_ffn": a["norm_ffn"][0].rearrange("(k p) -> k p", p=P),
                       "g_mix": a["g_mix_2"][0].rearrange("(k p) -> k p", p=P),
                       "g_moe": a["g_moe_2"][0].rearrange("(k p) -> k p", p=P),
                       "b_gate": a["b_gate_2"][0].rearrange("(k p) -> k p", p=P),
                       "conv_w": a["conv_w"][0].rearrange("w (k p) -> (w k) p", p=P),
                       "pool_scale": a["pool_scale"][0].rearrange("(k p) -> k p", p=P),
                       "cmp_pos": a["cmp_pos"][0].rearrange("k (m two) d -> (k m) (two d)", two=2)}[name]
                act.dma_start(vrow[at:at + w, :], src).then_inc(sem("vrow_in"), 16)
            for name, (at, w) in ROWS.items():
                src = {"a_log": a["a_log"][0], "dt_bias": a["dt_bias"][0], "gdn_norm": a["gdn_norm"][0],
                       "q_norm": a["nsa_q_norm"][0], "k_norm": a["nsa_k_norm"][0].rearrange("a b -> (a b)"),
                       "b_fgate": a["b_fgate_2"][0], "lam_q1": a["lam_q1_2"][0], "lam_k1": a["lam_k1_2"][0],
                       "lam_q2": a["lam_q2_2"][0], "lam_k2": a["lam_k2_2"][0], "g_subln": a["g_subln_2"][0],
                       "b_group": a["b_group_2"][0], "b_expert": a["b_expert_2"][0].rearrange("a b -> (a b)")}[name]
                act.dma_start(rows[:, at:at + w], src.partition_broadcast(P)).then_inc(sem("rows_in"), 16)
            act.dma_start(bias_c[:, :], band_c).then_inc(sem("band_in"), 16)
            act.dma_start(cw2[:, :, :, :].rearrange("p k i d -> p (k i) d"),
                          a["cmp_w2"][0].rearrange("k (i p) d -> p (k i) d", p=P)).then_inc(sem("cw2_in"), 16)
            act.wait_ge(sem("zero_start"), 1)
            for g in range(4):
                r = slice((g % 2) * HD, (g % 2 + 1) * HD)
                act.dma_start(poolw[r, g // 2, r], a["pool_w"][0, g]).then_inc(sem("poolw_in"), 16)
            at = 1536
            act.dma_start(w_ff[:, :, :], a["w_in_2"][0][:, at:at + FOX].rearrange("(k p) n -> p k n", p=P))\
                .then_inc(sem("w_ff_in"), 16)
            act.dma_start(w_route[:, :, 0:NGRP], a["w_group_2"][0].rearrange("(k p) n -> p k n", p=P))\
                .then_inc(sem("w_route_in"), 16)
            act.dma_start(w_route[:, :, NGRP:], a["w_expert_2"][0].rearrange("(k p) n -> p k n", p=P))\
                .then_inc(sem("w_route_in"), 16)

            def rms(stage, junk):
                for t in range(NT):
                    if 1 <= stage <= 3:
                        taken(act, ("mix", "ff2", "wo")[stage - 1], t, 1)
                    c(ACTV(junk[:, t, :], x_sb[:, t, :], ACT.Square, accum_out=ssx[:, stage, t:t + 1]))
                    c.own()
                    rms_reciprocal(c, ssx[:, stage, t:t + 1], rsx[:, stage, t:t + 1], D, "rms_ready")

            def take_hT(stage, name):
                for i in (1, 3):
                    b = filled(act, "hT", stage, i)
                    if name is None:
                        ACTV(hT[:, 2 * i:2 * i + 2, :], b[:, :].rearrange("p (a b) -> p a b", b=T), CPY)\
                            .then_inc(emptied("hT", stage, i), 1)
                        continue
                    c(ACTV(hT[:, 2 * i, :], b[:, 0:T], CPY, scale=vec(name, 2 * i)))
                    ACTV(hT[:, 2 * i + 1, :], b[:, T:2 * T], CPY, scale=vec(name, 2 * i + 1))\
                        .then_inc(emptied("hT", stage, i), 1)

            def copy_out(dst, src, *task):
                ACTV(dst, src, CPY).then_inc(emptied(*task), 1)

            act.preload_act_table_set("natural_log_exp_and_others")
            act.wait_ge(sem("x_in"), 16)
            rms(0, xn)
            taken(act, "vec")
            take_hT(0, "norm_mix")
            for i in range(5):
                b = filled(act, "qkv", i)
                for j in range(2 if i < 4 else 1):
                    f = 2 * i + j
                    ins = ACTV(conv[:, f, :], b[:, j * T:(j + 1) * T], CPY, scale=vec("conv_w", (CONV - 1) * QF + f))
                    if j == 0 and i < 4:
                        c(ins)
                    else:
                        ins.then_inc(sem("tap_ready"), 1)
            act.preload_act_table(ACT.Silu)
            for t in range(NT):
                ACTV(z_silu[:, t, :], filled(act, "z", t)[:, 0:GW], ACT.Silu).then_inc(emptied("z", t), 1)
            for i in range(5):
                taken(act, "qkv", i)
                s = conv[:, 2 * i:2 * i + (2 if i < 4 else 1), :]
                ins = ACTV(s, s, ACT.Silu)
                c(ins) if i < 4 else ins.then_inc(sem("conv_ready"), 1)
            act.preload_act_table_set("natural_log_exp_and_others")
            for t in range(NT):
                b = filled(act, "baq", t)
                c(ACTV(ba[:, t, :], b[:, 0:2 * GH], CPY))
                c(ACTV(beta[:, t * GH:(t + 1) * GH], b[:, 0:GH], ACT.Exp, scale=-1.0))
                if t == 1:
                    act.wait_ge(sem("rows_in"), 16 * len(ROWS))
                    ACTV(ealog, row("a_log"), ACT.Exp).then_inc(sem("small_exp"), 1)
                for j in range(NKV):
                    q = b[:, 2 * GH + j * NG * HD:2 * GH + (j + 1) * NG * HD].rearrange("p (g d) -> p g d", d=HD)
                    o = nsa_qr[:, t, :].rearrange("p (g j d) -> p j g d", j=NKV, d=HD)[:, j, :, :]
                    ins = ACTV(o, q, CPY)
                    c(ins) if j == 0 else ins.then_inc(emptied("baq", t), 1)
            act.wait_ge(sem("softplus_in"), 1)
            c(ACTV(g_t1, g_t1, ACT.Exp, scale=-1.0))
            c.own()
            ACTV(g_t2, g_t1, ACT.Ln, bias=1.0).then_inc(sem("softplus_ln"), 1)
            for t in range(NT):
                b = filled(act, "kv4", t)
                for i in range(2):
                    c(ACTV(cmp_in[:, t, :, i * HD:(i + 1) * HD], b[:, 0:4 * HD].rearrange("p (a d) -> p a d", d=HD), CPY))
                c(ACTV(nsa_kr[:, t, 0, :], b[:, 4 * HD:6 * HD], CPY))
                copy_out(nsa_v[:, t, 0, :], b[:, 6 * HD:8 * HD], "kv4", t)
            for t in range(NT):
                b = filled(act, "kvw", t)
                c(ACTV(nsa_kr[:, t, 1, :], b[:, 0:2 * HD], CPY))
                copy_out(nsa_v[:, t, 1, :], b[:, 2 * HD:4 * HD], "kvw", t)
            for t in range(NT):
                b = filled(act, "gu", t)
                ins = ACTV(nsa_gate[:, t, :], b[:, 0:3 * NH], ACT.Exp, scale=-1.0)
                c(ins) if t == 0 else ins.then_inc(sem("small_exp"), 1)
                copy_out(pool_in[:, t, :], b[:, 3 * NH:3 * NH + T], "gu", t)
            act.wait_ge(sem("n_ss_ready"), 1)
            rms_reciprocal(c, n_ss[:, 0:20], n_rs[:, 0:20], HD, "n_rs_ready")
            act.wait_ge(sem("zero_nsa"), 1)
            for t in range(NT):
                b = filled(act, "nq", t)[:, 0:NG * P].rearrange("p (g n) -> p g n", n=P)
                for j in range(NKV):
                    r = slice(j * HD, (j + 1) * HD)
                    ins = ACTV(nsa_qT[r, j::2, t * P:(t + 1) * P], b[r, :, :], CPY)
                    c(ins) if j == 0 else ins.then_inc(emptied("nq", t), 1)
            copy_out(nsa_kT.rearrange("p a b -> p (a b)"), filled(act, "nk")[:, :], "nk")
            for k in range(2):
                b = filled(act, "hid", k)
                n = 2 * NKV * NC
                ACTV(cmp_h[:, k, :, :].rearrange("p a b -> p (a b)"), b[:, 0:n], ACT.Exp, scale=-1.0)\
                    .then_inc(sem("small_exp"), 1)
            act.wait_ge(sem("kc_ss_ready"), 1)
            r = NKV * NC
            rms_reciprocal(c, kc_ss[0:r, :], kc_rs[0:r, :], HD, "kc_rs_ready")
            copy_out(cmp_kT, filled(act, "kcT")[:, 0:r], "kcT")
            for t in range(NT):
                act.wait_ge(sem("c_sc_ready"), t + 1)
                ACTV(c_sc[:, t, :], c_sc[:, t, :], ACT.Exp).then_inc(sem("c_exp_ready"), 1)
            for t in range(NT):
                copy_out(pcT[:, :, t * P:(t + 1) * P], filled(act, "pcT", t)[:, 0:NG * P].rearrange("p (g n) -> p g n", n=P),
                         "pcT", t)

            def exps(g):
                kind, t, m0, n = GROUPS[g]
                first = kind == "nsa"
                sc, pr = (scores1 if first else scores2)[:, g % 2, :], (probs1 if first else probs2)[:, g % 2, :]
                W = P * (t + 1)
                act.wait_ge(sem("max_ready"), g + 1)
                if g >= 2:
                    filled(act, "probsT", g - 2)
                for i in range(n):
                    ins = ACTV(pr[:, i * W:(i + 1) * W], sc[:, i * W:(i + 1) * W], ACT.Exp,
                               bias=nmx[:, g % 2, i:i + 1], accum_out=esum[:, g % 2, i:i + 1])
                    c(ins) if i < n - 1 else ins.then_inc(sem("exp_ready"), 1)

            def take_probs(g):
                kind, t, m0, n = GROUPS[g]
                b = filled(act, "probsT", g)
                pT = {"nsa": nsa_pT, "fox": fox_pT, "dif": dif_pT}[kind]
                if kind == "dif":
                    m0, n = m0 // 2, n // 2
                W = P * (t + 1)
                o = pT[:, m0:m0 + n, 0:P] if t == 0 else pT[:, m0:m0 + n, P:3 * P]
                copy_out(o, b[:, 0:n * W].rearrange("p (m n) -> p m n", n=W), "probsT", g)

            def attention(kind):
                for g in range(GFIRST[kind], GLAST[kind] + 1):
                    if g < GLAST[kind]:
                        exps(g)
                    if g > GFIRST[kind]:
                        take_probs(g - 1)

            attention("nsa")
            for i in range(3):
                copy_out(yT[:, 3 + i, :], filled(act, "nsaY", i)[:, 0:T], "nsaY", i)

            b = filled(act, "gc")
            c(ACTV(e_gc, b[:, 0:12], ACT.Exp))
            c(ACTV(e_rest, b[:, 12:24], ACT.Exp))
            last = b[:, 24:24 + NCH * GH].rearrange("p (n q two) -> p n q two", q=3, two=2)
            c(ACTV(e_last[0:HD, :, :], last[0:HD, :, :, 0], ACT.Exp))
            ACTV(e_last[HD:P, :, :], last[HD:P, :, :, 1], ACT.Exp).then_inc(emptied("gc"), 1)
            for i in range(3):
                b = filled(act, "dec", i)
                ACTV(decay[:, 4 * i:4 * i + 4, :].rearrange("p a b -> p (a b)"), b[:, :], ACT.Exp)\
                    .then_inc(emptied("dec", i), 1)
            for s in range(3):
                for t in range(NT):
                    copy_out(cut(7680 + s * 768 + t * GW, GW), filled(act, "tok", s, t)[:, 0:GW], "tok", s, t)
            act.wait_ge(sem("gq_ss_ready"), 1)
            rms_reciprocal(c, gq_ss, gq_rs, 1, "gq_rs_ready")

            def tile3(*task):
                return filled(act, *task)[:, 0:GW].rearrange("p (j n) -> p j n", n=P)

            for t in range(NT):
                copy_out(g_kT[:, :, t * P:(t + 1) * P], tile3("gT", "k", t), "gT", "k", t)
            act.wait_ge(sem("zero_kbq"), 1)
            for t in range(NT):
                b = tile3("gT", "q", t)
                for hh in range(2):
                    r = slice(hh * HD, (hh + 1) * HD)
                    ins = ACTV(g_kbqT[r, hh::2, 1, t * P:(t + 1) * P], b[r, :, :], CPY)
                    c(ins) if hh == 0 else ins.then_inc(emptied("gT", "q", t), 1)
            for t in range(NT):
                copy_out(g_qdT[:, :, t * P:(t + 1) * P], tile3("gT", "qd", t), "gT", "qd", t)
            for t in range(NT):
                copy_out(g_u[:, t, :], filled(act, "u", t)[:, 0:GW], "u", t)
                copy_out(g_wT[:, :, t * P:(t + 1) * P], tile3("wT", t), "wT", t)
            for n in range(NCH):
                r = slice((n % 2) * CHUNK, (n % 2 + 1) * CHUNK)
                copy_out(g_o[r, n // 2, :], filled(act, "qS", n)[r, 0:GW], "qS", n)
            act.wait_ge(sem("go_ss_ready"), 1)
            rms_reciprocal(c, go_ss, go_rs, HD, "go_rs_ready")
            for t in range(NT):
                copy_out(yT[:, 0:3, t * P:(t + 1) * P], tile3("gdnY", t), "gdnY", t)

            rms(1, xn)
            take_hT(1, "norm_ffn")
            for i in range(FT // 2):
                b = filled(act, "ff1", i)
                if i >= 2:
                    act.wait_ge(sem("ff_h_ready"), i - 1)
                ACTV(ff_r[:, i % 2, :], b[:, :], ACT.Relu).then_inc(emptied("ff1", i), 1)

            filled(act, "poolT", 1)
            act.dma_start(bias_c[:, :], alibi_c).then_inc(sem("alibi_in"), 16)
            act.wait_ge(sem("lam_in"), 1)
            ACTV(lam_s, lam_s, ACT.Exp).then_inc(sem("lam_exp"), 1)
            rms(2, xn)
            take_hT(2, "g_mix")
            act.wait_ge(sem("softplus_in"), 2)
            c(ACTV(f_t, f_t, ACT.Exp, scale=-1.0))
            c.own()
            ACTV(f_t, f_t, ACT.Ln, bias=1.0).then_inc(sem("softplus_ln"), 1)
            for s, dst in (("fk", fkT), ("dk", dkT)):
                for i in range(2):
                    copy_out(dst[:, 2 * i:2 * i + 2, :], filled(act, s, i)[:, :].rearrange("p (a b) -> p a b", b=T), s, i)
            act.preload_act_table(ACT.Sigmoid)
            for i in range(8):
                b = filled(act, "gate", i)
                c(ACTV(gates[:, 2 * i, :], b[:, 0:T], ACT.Sigmoid, bias=vec("b_gate", 2 * i)))
                ACTV(gates[:, 2 * i + 1, :], b[:, T:2 * T], ACT.Sigmoid, bias=vec("b_gate", 2 * i + 1))\
                    .then_inc(emptied("gate", i), 1)
            act.preload_act_table_set("natural_log_exp_and_others")
            attention("fox")
            for i in range(4):
                copy_out(oaT[:, i, :], filled(act, "foxY", i)[:, 0:T], "foxY", i)
            attention("dif")
            taken(act, "scores", len(GROUPS) - 1)
            act.dma_start(bias_c[:, 0:D], a["g_moe_2"][0].partition_broadcast(P)).then_inc(sem("g_moe_in"), 16)
            act.wait_ge(sem("d_ss_ready"), 1)
            rms_reciprocal(c, d_ss, d_rs, 2 * HD, "d_rs_ready")
            for t in range(NT):
                copy_out(obT[:, :, t * P:(t + 1) * P], filled(act, "difT", t)[:, :].rearrange("p (j n) -> p j n", n=P),
                         "difT", t)
            rms(3, xn)
            filled(act, "wo", 1, 1)
            fg = yT[:, 0:D // T, :].rearrange("p a b -> p (a b)")
            act.dma_start(fg, a["g_final_2"].partition_broadcast(P)).then_inc(sem("final_g_in"), 16)
            take_hT(3, None)
            act.wait_ge(sem("group_in"), 1)
            ACTV(gtmp, gtmp, ACT.Exp).then_inc(sem("route_exp"), 1)
            act.wait_ge(sem("second_in"), 1)
            ACTV(e21, e21, ACT.Exp).then_inc(sem("route_exp"), 1)

            act.preload_act_table(ACT.Silu)
            act.wait_ge(sem("passes_known"), 1)
            n = act.value_load(passes[0:1, 0:1], min_val=1, max_val=MAXPASS)
            ps_h1, ps_x1, ps_t, ps_g, ps_y1 = bank[0], bank[3], bank[4], bank[5], bank[7]
            with act.Fori(0, n * PAIRS) as it:
                act.wait_ge(sem("x1_full"), it + 1)
                ACTV(xg[:, 0, 4:8, :].rearrange("p a b -> p (a b)"), ps_x1[:, :], CPY).then_inc(sem("xg1_ready"), 1)
                act.wait_ge(sem("giveT_full"), it + 1)
                ACTV(giveT.rearrange("p a b -> p (a b)"), ps_g[:, 0:T], CPY).then_inc(sem("giveT_ready"), 1)
                act.wait_ge(sem("h1_full"), it + 1)
                ACTV(act1, ps_h1[:, :], ACT.Silu).then_inc(sem("h1_read"), 1)
                act.wait_ge(sem("t_full"), it + 1)
                ACTV(actT.rearrange("p a b -> p (a b)"), ps_t[:, :], CPY).then_inc(sem("actT_ready"), 1)
                act.wait_ge(sem("y_full"), it * 2 + 2)
                ACTV(y_e[:, 512:1024], ps_y1[:, :], CPY).then_inc(sem("y1_ready"), 1)
            act.preload_act_table_set("natural_log_exp_and_others")
            act.wait_ge(sem("added"), n * (4 * PAIRS) + 4)
            rms(4, out_sb)

        @block.gpsimd
        def _(pool):
            GT = nc.gpsimd.tensor_tensor
            nc.gpsimd.memset(poolw[:, :, :], 0.0).then_inc(sem("zero_start"), 1)
            nc.gpsimd.memset(nsa_qT, 0.0)
            nc.gpsimd.memset(pc, 0.0)
            nc.gpsimd.memset(cmp_vb, 0.0).then_inc(sem("zero_nsa"), 1)
            pool.wait_ge(sem("g_log_ready"), 1)
            filled(pool, "nsaY", 2)
            pool.wait_ge(sem("const_in"), 16)
            GT(g_cols, over(const("le_chunk"), 12), wide(g_log, P), ALU.mult).then_inc(sem("g_cols_ready"), 1)
            for m in (inv_d, inv_t):
                nc.gpsimd.tensor_copy(m, over(ident, 12)).then_inc(sem("inv_start"), 1)
            for i in range(3):
                taken(pool, "dec", i)
            GT(decay, decay, over(const("le_chunk"), 12), ALU.mult).then_inc(sem("decay_ready"), 1)
            pool.wait_ge(sem("gq_ss_ready"), 1)
            nc.gpsimd.memset(g_kbqT, 0.0).then_inc(sem("zero_kbq"), 1)
            pool.wait_ge(sem("g_tok_ready"), 1)
            taken(pool, "gc")
            GT(g_qd, g_q, wide(e_gc, HD), ALU.mult)
            GT(g_kd, g_k, wide(e_rest, HD), ALU.mult).then_inc(sem("g_pool_ready"), 1)
            filled(pool, "kk", GH - 1)
            nc.gpsimd.memset(g_state, 0.0).then_inc(sem("state_ready"), 1)
            filled(pool, "ff2", 1, 1)
            nc.gpsimd.memset(fqT, 0.0)
            nc.gpsimd.memset(dqT, 0.0).then_inc(sem("zero_q"), 1)
            pool.wait_ge(sem("f_log_ready"), 1)
            for t in range(NT):
                GT(f_cols[:, t, :, :], over(const("gt"), FOX), wide(f_log[:, t, :], P), ALU.mult)\
                    .then_inc(sem("f_cols_ready"), 1)


_INS = ['x', 'norm_mix', 'w_in', 'conv_w', 'a_log', 'dt_bias', 'gdn_norm', 'nsa_q_norm', 'nsa_k_norm', 'cmp_pos',
        'cmp_w1', 'cmp_w2', 'pool_w', 'pool_scale', 'w_out', 'norm_ffn', 'w_ffn1', 'w_ffn2', 'g_mix_2', 'w_in_2',
        'b_fgate_2', 'b_gate_2', 'lam_q1_2', 'lam_k1_2', 'lam_q2_2', 'lam_k2_2', 'g_subln_2', 'w_pa_2', 'w_pb_2',
        'w_o_2', 'g_moe_2', 'w_group_2', 'b_group_2', 'w_expert_2', 'b_expert_2', 'w1_2', 'w3_2', 'w2_2', 'g_final_2']
_OUT = (1, T, D)


def kernel(**inputs):
    import numpy as _np
    import concourse.bacc as _bacc
    from concourse import mybir as _mybir
    from concourse.bass_utils import run_bass_kernel_spmd as _run

    nc = _bacc.Bacc("TRN2", target_bir_lowering=False, num_devices=1, dynamic_dma_scratch_size=1024)
    arrays, args = {}, {}
    for name in _INS:
        arr = _np.ascontiguousarray(inputs[name])
        arrays[f"in_{name}_dram"] = arr
        args[name] = nc.dram_tensor(f"in_{name}_dram", arr.shape, _mybir.dt.from_np(arr.dtype),
                                    kind="ExternalInput").ap()
    extra = []
    for name, arr in zip(("consts", "band", "alibi"), shape_constants()):
        arrays[f"in_{name}_dram"] = arr
        extra.append(nc.dram_tensor(f"in_{name}_dram", arr.shape, _mybir.dt.from_np(arr.dtype),
                                    kind="ExternalInput").ap())
    out = nc.dram_tensor("out_0_dram", _OUT, _mybir.dt.float32, kind="ExternalOutput").ap()
    mixer_block_kernel(nc, args, *extra, out)
    r = _run(nc, [arrays], core_ids=[0])
    return r.results[0]["out_0_dram"]
```

```python
from contextlib import ExitStack

import numpy as np
import concourse.bass as bass
from concourse import mybir

F32 = mybir.dt.float32
F32R = mybir.dt.float32r
I32 = mybir.dt.int32
ALU = mybir.AluOpType
ACT = mybir.ActivationFunctionType
AX = mybir.AxisListType.X

P = 128
T = 256
NT = T // P
D = 1024
KD = D // P
HD = 64
EPS = 1e-6
NEG = -1e30
GH = 6
CHUNK = 64
NCH = T // CHUNK
GW = GH * HD
CONV = 4
QF = 3 * GW // P
NH = 6
NKV = 2
NG = NH // NKV
CMP_LEN, CMP_STRIDE, CMP_HID = 32, 16, 256
NC = T // CMP_STRIDE - CMP_LEN // CMP_STRIDE + 1
CM = CMP_LEN * HD // P
POOLS = (2, 4, 8, 16)
FF = 4096
FT = FF // P
FOX = 8
DIF = 4
LAM0 = 0.8 - 0.6 * 1.0
EXPERTS = 32
NGRP = 4
DE = D // 2
CAP = 64
PAIRS = EXPERTS // 2
MAXPASS = T // CAP

CONSTS = {}
_at = 0
for _name, _w in (
    ("ident", P), ("le_chunk", P), ("gt_chunk", P), ("chunk0", P), ("chunk1", P), ("head_diag", P),
    ("invmask", 6 * P), ("le", P), ("gt", P), ("ones", P), ("lt", P), ("causal", 3 * P), ("slot", CAP),
    ("cmp_add", NT * NC), ("cmp_mul", NT * NC), ("rank32", EXPERTS), ("rank4", NGRP),
):
    CONSTS[_name] = (_at, _w)
    _at += _w
NCONST = _at
NBAND = 4 * 3 * P


def shape_constants():
    r = np.arange(P)
    row, col = r[:, None], r[None, :]
    same = (row // CHUNK) == (col // CHUNK)
    c = np.zeros((P, NCONST), np.float32)

    def put(name, a):
        at, w = CONSTS[name]
        c[:, at:at + w] = np.asarray(a, np.float32).reshape(P, w)

    put("ident", row == col)
    put("le_chunk", (row <= col) & same)
    put("gt_chunk", (row > col) & same)
    put("chunk0", np.broadcast_to(row < CHUNK, (P, P)))
    put("chunk1", np.broadcast_to(row >= CHUNK, (P, P)))
    put("head_diag", (row // HD) == (col // HD))
    put("invmask", np.stack([
        ((row // (2 * m)) == (col // (2 * m))) & ((row // m) % 2 == 1) & ((col // m) % 2 == 0)
        for m in (1, 2, 4, 8, 16, 32)], axis=1))
    put("le", row <= col)
    put("gt", row > col)
    put("ones", np.ones((P, P)))
    put("lt", row < col)
    put("causal", np.concatenate([
        np.where(col <= row, 0.0, NEG), np.zeros((P, P)), np.where(col <= row, 0.0, NEG)], axis=1))
    put("slot", np.broadcast_to(np.arange(CAP), (P, CAP)))
    end = np.arange(NC) * CMP_STRIDE + CMP_LEN - 1
    tok = np.arange(NT)[None, :, None] * P + r[:, None, None]
    valid = end[None, None, :] <= tok
    put("cmp_add", np.where(valid, 0.0, NEG))
    put("cmp_mul", valid)
    put("rank32", np.broadcast_to(np.arange(EXPERTS), (P, EXPERTS)))
    put("rank4", np.broadcast_to(np.arange(NGRP), (P, NGRP)))

    s, t = np.arange(T)[:, None], np.arange(T)[None, :]
    band = np.zeros((P, 4, 3 * P), np.float32)
    for g, w in enumerate(POOLS):
        m = np.where((s <= t) & (s > t - w), 1.0 / np.minimum(t + 1, w), 0.0) - (s == t)
        band[:, g, 0:T] = m[0:P]
        band[:, g, T:] = m[P:, P:]
    alibi = np.zeros((P, DIF, 3 * P), np.float32)
    for h in range(DIF):
        b = np.where((t // CHUNK) <= (s // CHUNK), -(2.0 ** (-8.0 / DIF * (h + 1))) * np.abs(s - t), NEG)
        alibi[:, h, 0:P] = b[0:P, 0:P]
        alibi[:, h, P:] = b[P:, :]
    return c, band.reshape(P, NBAND), alibi.reshape(P, NBAND)


VEC = {}
_at = 0
for _name, _w in (("norm_mix", 8), ("norm_ffn", 8), ("g_mix", 8), ("g_moe", 8), ("b_gate", 16),
                  ("conv_w", CONV * QF), ("pool_scale", 2), ("cmp_pos", 2 * CM)):
    VEC[_name] = (_at, _w)
    _at += _w
NVEC = _at

ROWS = {}
_at = 0
for _name, _w in (("a_log", GH), ("dt_bias", GH), ("gdn_norm", HD), ("q_norm", HD), ("k_norm", 3 * HD),
                  ("b_fgate", FOX), ("lam_q1", HD), ("lam_k1", HD), ("lam_q2", HD), ("lam_k2", HD),
                  ("g_subln", 2 * HD), ("b_group", NGRP), ("b_expert", EXPERTS)):
    ROWS[_name] = (_at, _w)
    _at += _w
NROWS = _at

GROUPS = []
for _kind, _n in (("nsa", 2 * NH), ("fox", FOX), ("dif", 2 * DIF)):
    GROUPS += [(_kind, 0, m, 4) for m in range(0, _n, 4)]
    GROUPS += [(_kind, 1, m, 2) for m in range(0, _n, 2)]
GFIRST = {k: min(i for i, g in enumerate(GROUPS) if g[0] == k) for k in ("nsa", "fox", "dif")}
GLAST = {k: max(i for i, g in enumerate(GROUPS) if g[0] == k) + 1 for k in ("nsa", "fox", "dif")}


def attention_tasks(kind):
    first, last = GFIRST[kind], GLAST[kind]
    out = []
    for g in range(first, last + 2):
        if g < last:
            out.append(("scores", g))
        if g > first + 1:
            out.append(("probsT", g - 2))
    return out


PA_AFTER = (3, 6, 9)

TASKS = [("vec",)]
TASKS += [("hT", 0, i) for i in range(4)]
for _s in ("kvw", "baq", "kv4", "gu"):
    TASKS += [(_s, t) for t in range(NT)]
TASKS += [("poolT", i) for i in range(2)] + [("win", k) for k in range(2)]
TASKS += [("qkv", i) for i in range(2)] + [("poolY", i) for i in range(2)] + [("hid", k) for k in range(2)]
TASKS += [("nq", t) for t in range(NT)] + [("nk",)] + [("qkv", 2), ("cmp",), ("qkv", 3), ("kcT",), ("qkv", 4)]
TASKS += [("cs", t) for t in range(NT)] + [("z", t) for t in range(NT)] + [("pcT", t) for t in range(NT)]
TASKS += attention_tasks("nsa")
TASKS += [("nsaY", i) for i in range(NH // 2)]
TASKS += [("gc",)] + [("dec", i) for i in range(3)]
TASKS += [("tok", s, t) for s in range(3) for t in range(NT)]
TASKS += [("gT", s, t) for s in ("k", "kb", "q", "qd") for t in range(NT)]
TASKS += [("kk", i) for i in range(GH)]
for _l in range(6):
    for _b in range(3):
        TASKS.append(("invP", _l, _b))
    for _b in range(3):
        TASKS += [("invQ", _l, _b)] if 0 < _l < 5 else []
        TASKS.append(("invR", _l, _b))
for _t in range(NT):
    TASKS += [("u", _t), ("wT", _t)]
for _n in range(NCH):
    TASKS += [("wS", _n), ("qS", _n)]
    if _n < NCH - 1:
        TASKS.append(("kV", _n))
    if _n % 2 == 1:
        TASKS.append(("o", _n // 2))
TASKS += [("gdnY", t) for t in range(NT)]
TASKS += [("mix", t, h) for h in range(2) for t in range(NT)]
TASKS += [("hT", 1, i) for i in range(4)]
TASKS += [("ff1", i) for i in range(FT // 2)]
TASKS += [("ff2", t, h) for t in range(NT) for h in range(2)]
TASKS += [("hT", 2, i) for i in range(4)]
TASKS += [("ff",)] + [("fq", i) for i in range(2)] + [("ffT",)] + [("fk", i) for i in range(2)]
TASKS += [("fv", t) for t in range(NT)]
TASKS += [("dq", i) for i in range(2)] + [("dk", i) for i in range(2)]
TASKS += [("dv", t) for t in range(NT)]
TASKS += [("gate", i) for i in range(8)]
TASKS += attention_tasks("fox")
TASKS += [("foxY", i) for i in range(4)]
for _i, _task in enumerate(attention_tasks("dif")):
    TASKS += [_task] + ([("pa", PA_AFTER.index(_i))] if _i in PA_AFTER else [])
TASKS += [("difO", t) for t in range(NT)] + [("pa", 3)] + [("difT", t) for t in range(NT)]
TASKS += [("pb", i) for i in range(4)]
TASKS += [("wo", t, h) for h in range(2) for t in range(NT)]
TASKS += [("hT", 3, i) for i in range(4)]
TASKS += [("route",), ("rank",), ("count",)]
TASK = {name: i for i, name in enumerate(TASKS)}
BANKS = 8
MIX_BANK = {("mix", t, h): 4 + 2 * h + t for h in range(2) for t in range(NT)}
_state = range(TASK[("u", 0)], TASK[("gdnY", NT - 1)] + 1)
BANK, USES, _use, _at = {}, {}, [0] * BANKS, 0
for _i, _task in enumerate(TASKS):
    if _task in MIX_BANK:
        _b = MIX_BANK[_task]
    elif _i in _state:
        _b = (_i - _state[0]) % 4
    else:
        _b, _at = _at % BANKS, _at + 1
    BANK[_task], USES[_task] = _b, _use[_b]
    _use[_b] += 1
BANK_USES = list(_use)

WIN_COLS = [(0, 512), (512, 1024), (1024, 1536), (1536, 1932), (1932, 2444), (2444, 2700), (2700, 2974)]
WIN_LAST = [("qkv", 1), ("qkv", 3), ("z", 1), ("baq", 1), ("kv4", 1), ("kvw", 1), ("gu", 1)]
W2_COLS = [(0, 512, ("fq", 1)), (512, 1024, ("fk", 1)), (1024, 1536, ("fv", 1)),
           (1544, 2056, ("dq", 1)), (2056, 2568, ("dk", 1)), (2568, 3080, ("dv", 1)),
           (3080, 3592, ("gate", 1)), (3592, 4104, ("gate", 3)), (4104, 4616, ("gate", 5)), (4616, 5128, ("gate", 7))]
UNITS = [(("win", i), WIN_LAST[i]) for i in (5, 3, 4, 6, 0, 1)]
UNITS += [(("cmp1", k), ("hid", k)) for k in range(2)] + [(("win", 2), WIN_LAST[2])]
UNITS += [(("wout", h), ("mix", 1, h)) for h in range(2)]
UNITS += [(("w1", i), ("ff1", 2 * i + 1)) for i in range(8)]
UNITS += [(("w2", i), None if i < 7 else ("ff2", NT - 1, 1)) for i in range(8)]
UNITS += [(("win2", i), W2_COLS[i][2]) for i in range(10)]
UNITS += [(("pa",), ("pa", 3)), (("pb",), ("pb", 3))]
UNITS += [(("wo2", h), ("wo", 1, h)) for h in range(2)]
UNIT = {name: i for i, (name, _) in enumerate(UNITS)}
SPLITS = [name for name, _ in UNITS if name[0] != "cmp1"]
SPLIT = {name: i for i, name in enumerate(SPLITS)}
PARTS = 4
RAW = 2
SLOTS = 6


def mixer_block_kernel(nc, a, consts, band_c, alibi_c, out):
    with ExitStack() as ctx:
        sems = {}

        def sb(name, shape, dt=F32):
            return ctx.enter_context(nc.sbuf_tensor(name, shape, dt))

        def sem(name):
            if name not in sems:
                sems[name] = ctx.enter_context(nc.semaphore(name))
            return sems[name]

        bank = [ctx.enter_context(nc.psum_tensor(f"bank{i}", [P, 512], F32)) for i in range(BANKS)]

        twins = {}

        def two_types(name, shape):
            with nc.sbuf_tensor(name + "_r", shape, F32R) as twin:
                twins[name] = twin
            return sb(name, shape)

        def rounded(ap):
            return bass.AP(tensor=twins[ap.tensor.name], offset=ap.offset, ap=ap.ap)

        def reread(ap):
            return rounded(ap).bitcast(F32)

        ring = two_types("ring", [P, SLOTS, 4096])
        x_sb = sb("x_sb", [P, NT, D])
        yT = two_types("yT", [P, KD, T])
        cst = sb("cst", [P, NCONST])
        bias_c = sb("bias_c", [P, NBAND])
        vrow = sb("vrow", [NVEC, P])
        vT = sb("vT", [P, NVEC])
        rows = sb("rows", [P, NROWS])
        small = sb("small", [P, 1280])
        cw2 = sb("cw2", [P, 2, 2, HD])
        poolw = sb("poolw", [P, 2, P])
        w_ff = sb("w_ff", [P, KD, FOX])
        w_route = sb("w_route", [P, KD, NGRP + EXPERTS])
        passes = sb("passes", [1, 1], I32)
        AR = 19968
        arena = two_types("arena", [P, AR])

        def cut(at, *dims):
            n = int(np.prod(dims))
            assert at + n <= AR
            v = arena[:, at:at + n]
            if len(dims) == 2:
                v = v.rearrange("p (a b) -> p a b", b=dims[1])
            elif len(dims) == 3:
                v = v.rearrange("p (a b c) -> p a b c", b=dims[1], c=dims[2])
            elif len(dims) == 4:
                v = v.rearrange("p (a b c d) -> p a b c d", b=dims[1], c=dims[2], d=dims[3])
            return v

        used = [0]

        def tiny(*dims):
            n = int(np.prod(dims))
            at = used[0]
            used[0] += n
            assert used[0] <= 1280
            v = small[:, at:at + n]
            if len(dims) == 2:
                v = v.rearrange("p (a b) -> p a b", b=dims[1])
            elif len(dims) == 3:
                v = v.rearrange("p (a b c) -> p a b c", b=dims[1], c=dims[2])
            return v

        def const(name):
            at, w = CONSTS[name]
            return cst[:, at:at + w]

        def vec(name, i):
            return vT[:, VEC[name][0] + i:VEC[name][0] + i + 1]

        def row(name):
            at, w = ROWS[name]
            return rows[:, at:at + w]

        def wide(ap, n):
            return ap.unsqueeze(2).to_broadcast([ap.shape[0], ap.shape[1], n])

        def over(ap, n):
            return ap.unsqueeze(1).to_broadcast([ap.shape[0], n, ap.shape[1]])

        ident = const("ident")
        band = bias_c[:, :].rearrange("p (g n) -> p g n", g=4)
        alibi = bias_c[:, :].rearrange("p (h n) -> p h n", h=DIF)
        invmask = const("invmask").rearrange("p (l n) -> p l n", l=6)

        xn = cut(0, NT, D)
        hT = cut(2048, KD, T)
        hT_lo = [[yT[:, k, :] for k in range(6)] + [cut(10752 + k * T, T) for k in range(2)]]
        hT_lo += [[yT[:, k, :] for k in range(KD)]] * 2
        y_lo = cut(16896, KD, T)
        conv = cut(4608, QF, T)
        z_silu = cut(19200, NT, GW)
        nsa_qr = cut(6912, NT, NH * HD)
        nsa_kr = cut(8704, NT, 2, NKV * HD)
        cmp_in = cut(7680, NT, 4, P)
        nsa_v = cut(9216, NT, 2, NKV * HD)
        pool_in = cut(9728, NT, T)
        poolT = cut(10240, 2, T)
        nsa_qT = cut(11776, NH, T)
        nsa_kT = cut(13312, 2, T)
        pc = cut(13824, NT, NG, P)
        pcT = cut(14592, NG, T)
        cmp_win = cut(15360, 4, T)
        cmp_x = cut(16384, 4, CM, NC)
        cmp_h = cut(17408, 2, 2, NKV * NC)
        cmp_vb = cut(17536, NKV, HD)
        cmp_kd = cut(17664, 2 * HD)
        cmp_kT = cut(17792, NKV * NC)
        scores1 = cut(15360, 2, 512)
        probs1 = cut(17920, 2, 512)
        nsa_pT = cut(0, 2 * NH, 3 * P)
        inv_d = cut(0, 12, P)
        inv_t = cut(1536, 12, P)
        inv_p = cut(3072, 12, P)
        g_cols = inv_p
        lT = cut(4608, 12, P)
        qkT = cut(6144, 12, P)
        g_q, g_k, g_v = (cut(7680 + 768 * i, 12, HD) for i in range(3))
        g_qk = cut(7680, 24, HD)
        g_qr, g_kr, g_kbr, g_qdr, g_kdr = (cut(at, NT, GW) for at in (7680, 8448, 9984, 11520, 12288))
        g_kb, g_kbe, g_qd, g_kd = (cut(9984 + 768 * i, 12, HD) for i in range(4))
        g_kT = cut(13056, 3, T)
        g_kbqT = cut(13824, GH, 2, T)
        g_qdT = cut(16896, 3, T)
        decay = cut(17664, 12, P)
        g_sq = cut(13824, 24, HD)
        g_wT = cut(7680, 3, T)
        g_vn = cut(8448, NT, GW)
        g_u = cut(9984, NT, GW)
        g_o = cut(13824, NT, GW)
        g_state = cut(14592, 3, P)
        g_upd = cut(14976, 3, P)
        g_y = cut(16128, NT, GW)
        ff_r = cut(0, 2, 512)
        ff_main, ff_rest = cut(4096, FT - 2, T), cut(1024, 2, T)
        ff_lo = cut(11776, FT, T)

        def ff_hi(k, n=1):
            return ff_main[:, k:k + n, :] if k < FT - 2 else ff_rest[:, k - FT + 2:k - FT + 2 + n, :]

        gates = cut(4608, 16, T)
        fqT = cut(8704, FOX, T)
        fkT = cut(10752, FOX // 2, T)
        dqT = cut(11776, 2 * DIF, T)
        dkT = cut(13824, DIF, T)
        fv = cut(14848, NT, FOX * HD)
        dv = cut(15872, NT, 2 * DIF * HD)
        f_cols = cut(16896, NT, FOX, P)
        scores2 = cut(18944, 2, 512)
        f_raw = cut(18944, T)
        probs2 = cut(0, 2, 512)
        fox_pT = cut(1024, FOX, 3 * P)
        dif_pT = cut(1024, DIF, 3 * P)
        oaT = cut(10752, 4, T)
        obT = cut(13824, 4, T)
        dif_o = cut(16896, NT * DIF, 2 * HD)
        dif_sq = cut(17920, NT * DIF, 2 * HD)
        oaT_lo, obT_lo = cut(8704, 4, T), cut(17920, 4, T)
        y2_hi, y2_lo = cut(8704, KD, T), cut(11776, KD, T)
        mix_b = cut(14848, 2, 512)
        xg = cut(4608, 2, KD, P)
        act1 = cut(6656, 512)
        act = cut(7168, 512)
        actT = cut(7680, 4, P)
        y_e = cut(8192, D)
        pick = cut(9216, NT, P)
        give = cut(9728, 2, NT, P)
        giveT = cut(10240, NT, P)
        final_g = yT[:, 0:D // T, :].rearrange("p a b -> p (a b)")
        out_sb = cut(11520, NT, D)
        spos = cut(13568, NT, EXPERTS + 2)
        swgt = cut(13568 + 128, NT, EXPERTS + 2)
        r_a = cut(14080, NT, EXPERTS)
        r_b = cut(14080 + 64, NT, EXPERTS)
        r_l = cut(14080 + 192, NT, EXPERTS)
        r_hot1 = cut(14080 + 256, NT, EXPERTS)
        r_hot2 = cut(14080 + 320, NT, EXPERTS)
        r_hot = cut(14080 + 384, NT, EXPERTS)

        ssx, rsx = tiny(5, NT), tiny(5, NT)
        n_ss, n_rs = tiny(16 + 8), tiny(16 + 8)
        kc_ss, kc_rs, kc_raw, kc_sq = tiny(1), tiny(1), tiny(HD), tiny(HD)
        nsa_gate = tiny(NT, NH * 3)
        c_mx, c_sm, c_sc = tiny(NT, NH), tiny(NT, NH), tiny(NT, NH * NC)
        mx, nmx, esum, coef = tiny(2, 4), tiny(2, 4), tiny(2, 4), tiny(2, 4)
        ba, beta, g_log, g_t1, g_t2 = tiny(NT, 2 * GH), tiny(12), tiny(12), tiny(12), tiny(12)
        g_x = tiny(12)
        ealog = tiny(GH)
        e_gc, e_rest, e_last = tiny(12), tiny(12), tiny(NCH, 3)
        gq_ss, gq_rs = tiny(24), tiny(24)
        go_ss, go_rs = tiny(12), tiny(12)
        f_x, f_t, f_log = tiny(NT, FOX), tiny(NT, FOX), tiny(NT, FOX)
        lam_p, lam_s, lam = tiny(2, HD), tiny(2), tiny(1)
        d_ss, d_rs = tiny(NT * DIF), tiny(NT * DIF)
        logit = tiny(NT, NGRP + EXPERTS)
        gm, ghot, gtmp, gidx, gsum, gw = tiny(NT), tiny(NT, NGRP), tiny(NT, NGRP), tiny(NT), tiny(NT), tiny(NT)
        m1, m2, i1, i2, e21, den, w1s, w2s = (tiny(NT) for _ in range(8))
        cmax = tiny(4)

        def tiles(m):
            return m if isinstance(m, list) else [m[:, k, :] for k in range(m.shape[1])]

        def filled(eng, *task):
            eng.wait_ge(sem("psum_full"), TASK[task] + 1)
            return bank[BANK[task]]

        def emptied(*task):
            return sem(f"bank_free{BANK[task]}")

        def taken(eng, *task):
            eng.wait_ge(emptied(*task), USES[task] + 1)

        class Chain:

            def __init__(self, eng, name):
                self.eng, self.sem, self.n = eng, sem(name), 0

            def __call__(self, ins):
                self.n += 1
                ins.then_inc(self.sem, 1)

            def own(self):
                if self.n:
                    self.eng.wait_ge(self.sem, self.n)

        def landed(eng, name):
            eng.wait_ge(sem(f"landed{UNIT[name] % RAW}"), 16 * (UNIT[name] // RAW + 1))

        NA = len(UNITS)
        eslot = list(range(SLOTS))
        ebase = [len([u for u in range(NA) if u % RAW == s]) if s < RAW else 0 for s in eslot]

        def unit_source(name):
            kind = name[0]
            if kind == "win":
                lo, hi = WIN_COLS[name[1]]
                return a["w_in"][0][:, lo:hi].rearrange("(k p) n -> p k n", p=P)
            if kind == "cmp1":
                return a["cmp_w1"][0, name[1]].rearrange("(k p) n -> p k n", p=P)
            if kind == "wout":
                return a["w_out"][0][:, name[1] * 512:(name[1] + 1) * 512].rearrange("(k p) n -> p k n", p=P)
            if kind == "w1":
                return a["w_ffn1"][0][:, name[1] * 512:(name[1] + 1) * 512].rearrange("(k p) n -> p k n", p=P)
            if kind == "w2":
                return a["w_ffn2"][0][name[1] * 512:(name[1] + 1) * 512, :].rearrange("(k p) n -> p k n", p=P)
            if kind == "win2":
                lo, hi = W2_COLS[name[1]][:2]
                return a["w_in_2"][0][:, lo:hi].rearrange("(k p) n -> p k n", p=P)
            if kind == "pa":
                return a["w_pa_2"][0].rearrange("(k p) n -> p k n", p=P)
            if kind == "pb":
                return a["w_pb_2"][0].rearrange("(k p) n -> p k n", p=P)
            return a["w_o_2"][0][:, name[1] * 512:(name[1] + 1) * 512].rearrange("(k p) n -> p k n", p=P)

        def unit_view(name):
            src = unit_source(name)
            k, n = src.shape[1], src.shape[2]
            return ring[:, UNIT[name] % RAW, 0:k * n].rearrange("p (k n) -> p k n", k=k)

        def high_low(name):
            src = unit_source(name)
            k, n = src.shape[1], src.shape[2]
            at = RAW + 2 * (SPLIT[name] % 2)
            return [rounded(ring[:, at + i, 0:k * n].rearrange("p (k n) -> p k n", k=k)) for i in range(2)]

        def split_step(name, q):
            src = unit_source(name)
            n = src.shape[1] * src.shape[2] // PARTS
            at = RAW + 2 * (SPLIT[name] % 2)
            cols = slice(q * n, (q + 1) * n)
            return ring[:, UNIT[name] % RAW, cols], ring[:, at, cols], ring[:, at + 1, cols]

        def split_free(eng, name):
            s = SPLIT[name]
            if s >= 2:
                before, last = UNITS[UNIT[SPLITS[s - 2]]]
                if last is None:
                    eng.wait_ge(sem("w2_used"), before[1] + 1)
                else:
                    eng.wait_ge(sem("psum_full"), TASK[last] + 1)

        def split_ready(eng, name):
            eng.wait_ge(sem("lo_ready"), PARTS * (SPLIT[name] + 1))

        w1_odd = cut(15872, 4096)

        def expert_landed(k, odd):
            return sem("landed_w1_odd" if k == 0 and odd else f"landed{eslot[k]}")

        def expert_view(k, odd):
            v = w1_odd if k == 0 and odd else ring[:, eslot[k], :]
            return v.rearrange("p (k n) -> p k n", n=512 if k < 4 else D)

        block = ctx.enter_context(nc.Block())

        @block.sync
        def _(sp):
            def later_inputs():
                for name, (at, w) in ROWS.items():
                    src = {"a_log": a["a_log"][0], "dt_bias": a["dt_bias"][0], "gdn_norm": a["gdn_norm"][0],
                           "q_norm": a["nsa_q_norm"][0], "k_norm": a["nsa_k_norm"][0].rearrange("a b -> (a b)"),
                           "b_fgate": a["b_fgate_2"][0], "lam_q1": a["lam_q1_2"][0], "lam_k1": a["lam_k1_2"][0],
                           "lam_q2": a["lam_q2_2"][0], "lam_k2": a["lam_k2_2"][0], "g_subln": a["g_subln_2"][0],
                           "b_group": a["b_group_2"][0], "b_expert": a["b_expert_2"][0].rearrange("a b -> (a b)")}[name]
                    sp.dma_start(rows[:, at:at + w], src.partition_broadcast(P)).then_inc(sem("rows_in"), 16)
                sp.dma_start(bias_c[:, :], band_c).then_inc(sem("band_in"), 16)
                sp.dma_start(cw2[:, :, :, :].rearrange("p k i d -> p (k i) d"),
                             a["cmp_w2"][0].rearrange("k (i p) d -> p (k i) d", p=P)).then_inc(sem("cw2_in"), 16)
                sp.wait_ge(sem("zero_start"), 1)
                for g in range(4):
                    r = slice((g % 2) * HD, (g % 2 + 1) * HD)
                    sp.dma_start(poolw[r, g // 2, r], a["pool_w"][0, g]).then_inc(sem("poolw_in"), 16)
                at = 1536
                sp.dma_start(w_ff[:, :, :], a["w_in_2"][0][:, at:at + FOX].rearrange("(k p) n -> p k n", p=P))\
                    .then_inc(sem("w_ff_in"), 16)
                sp.dma_start(w_route[:, :, 0:NGRP], a["w_group_2"][0].rearrange("(k p) n -> p k n", p=P))\
                    .then_inc(sem("w_route_in"), 16)
                sp.dma_start(w_route[:, :, NGRP:], a["w_expert_2"][0].rearrange("(k p) n -> p k n", p=P))\
                    .then_inc(sem("w_route_in"), 16)

            sp.dma_start(x_sb[:, :, :], a["x"][0].rearrange("(t p) n -> p t n", p=P)).then_inc(sem("x_in"), 16)
            for u, (name, _) in enumerate(UNITS):
                if u == 0:
                    sp.wait_ge(sem("const_in"), 16)
                    sp.wait_ge(sem("vrow_in"), 16 * len(VEC))
                if u == RAW:
                    later_inputs()
                if u >= RAW:
                    before, last = UNITS[u - RAW]
                    if before in SPLIT:
                        split_ready(sp, before)
                    else:
                        sp.wait_ge(sem("psum_full"), TASK[last] + 1)
                sp.dma_start(unit_view(name), unit_source(name)).then_inc(sem(f"landed{u % RAW}"), 16)

            def expert_unit(k, pair, odd):
                w = a[("w1_2", "w3_2", "w2_2")[k // 2]][0]
                src = w[pair * 2 + k % 2].rearrange("(k p) n -> p k n", p=P)
                sp.dma_start(expert_view(k, odd), src).then_inc(expert_landed(k, odd), 16)

            def slot_free(k, it):
                sp.wait_ge(sem(("h1_full", "h3_full", "y_full")[k // 2]), it * (1 if k < 4 else 2))

            def pair_loads(base, pair, odd, ahead=True):
                for k in range(1, 6):
                    slot_free(k, base + pair)
                    expert_unit(k, pair, odd)
                    if k == 1 and ahead:
                        expert_unit(0, pair + 1, 1 - odd)

            def other_pairs(base):
                with sp.Fori(0, PAIRS // 2 - 1) as i:
                    pair_loads(base, i * 2 + 1, 1)
                    pair_loads(base, i * 2 + 2, 0)
                pair_loads(base, PAIRS - 1, 1, ahead=False)

            for k in range(6):
                if k < RAW:
                    split_ready(sp, [name for name, _ in UNITS[-RAW:] if UNIT[name] % RAW == k][0])
                else:
                    last = [name for name in SPLITS[-2:] if SPLIT[name] % 2 == (k - RAW) // 2][0]
                    sp.wait_ge(sem("psum_full"), TASK[UNITS[UNIT[last]][1]] + 1)
                expert_unit(k, 0, 0)
                if k == 1:
                    sp.wait_ge(sem("psum_full"), TASK["pb", 3] + 1)
                    expert_unit(0, 1, 1)
            other_pairs(0)
            sp.wait_ge(sem("passes_known"), 1)
            n = sp.value_load(passes[0:1, 0:1], min_val=1, max_val=MAXPASS)
            with sp.If(n > 1):
                with sp.Fori(1, n) as p:
                    for k in range(6):
                        slot_free(k, p * PAIRS)
                        expert_unit(k, 0, 0)
                        if k == 1:
                            expert_unit(0, 1, 1)
                    other_pairs(p * PAIRS)
            with sp.Else():
                sp.nop()
            for t in range(NT):
                sp.wait_ge(sem("out_ready"), t + 1)
                sp.dma_start(out[0, t * P:(t + 1) * P, :], out_sb[:, t, :]).then_inc(sem("out_done"), 16)
            sp.wait_ge(sem("out_done"), 16 * NT)

        @block.tensor
        def _(pe):
            nxt = [0]

            def empty(*task):
                i = TASK[task]
                assert i == nxt[0], (task, TASKS[nxt[0]])
                nxt[0] += 1
                return bank_of(*task)

            def bank_of(*task):
                if USES[task]:
                    pe.wait_ge(emptied(*task), USES[task])
                return bank[BANK[task]]

            def full(mm):
                mm.then_inc(sem("psum_full"), 1)

            def turn(out_ap, in_ap):
                k = in_ap.shape[0]
                return pe.transpose(out_ap, in_ap, ident[0:k, 0:k])

            def turn_rows(stage):
                for i in range(4):
                    b = empty("hT", stage, i)
                    if i == 0:
                        pe.wait_ge(sem("xn_ready"), NT * (stage + 1))
                    for kk in range(2):
                        for t in range(NT):
                            k = 2 * i + kk
                            mm = turn(b[:, kk * T + t * P:kk * T + (t + 1) * P], xn[:, t, k * P:(k + 1) * P])
                    full(mm)

            def hT_ready(stage):
                for i in range(4):
                    taken(pe, "hT", stage, i)

            def features(task, unit_name, cols, group, src, k_tiles=KD):
                b = empty(*task)
                split_ready(pe, unit_name)
                wh, wl = high_low(unit_name)
                xh, xl = ([rounded(x) for x in tiles(s)] for s in src)
                for j in range(group):
                    c = slice(cols + j * P, cols + (j + 1) * P)
                    for k in range(k_tiles):
                        for i, (w, x) in enumerate(((wl, xh), (wh, xh), (wh, xl))):
                            mm = pe.matmul(b[:, j * T:(j + 1) * T], w[:, k, c], x[k],
                                           start=(k == 0 and i == 0), stop=(k == k_tiles - 1 and i == 2))
                full(mm)

            def tokens(task, unit_name, t, src, cols=0, width=None):
                b = empty(*task)
                split_ready(pe, unit_name)
                wh, wl = high_low(unit_name)
                width = wh.shape[2] - cols if width is None else width
                xh, xl = ([rounded(x) for x in tiles(s)] for s in src)
                for k in range(KD):
                    for i, (w, x) in enumerate(((wh, xl), (wh, xh), (wl, xh))):
                        mm = pe.matmul(b[:, 0:width], x[k][:, t * P:(t + 1) * P], w[:, k, cols:cols + width],
                                       start=(k == 0 and i == 0), stop=(k == KD - 1 and i == 2))
                full(mm)

            b = empty("vec")
            pe.wait_ge(sem("const_in"), 16)
            pe.wait_ge(sem("vrow_in"), 16 * len(VEC))
            full(turn(b[:, 0:NVEC], vrow[:, :]))

            turn_rows(0)
            hT_ready(0)
            h0 = (hT, hT_lo[0])
            for s, u in (("kvw", 5), ("baq", 3), ("kv4", 4), ("gu", 6)):
                for t in range(NT):
                    tokens((s, t), ("win", u), t, h0)

            def qkv(i):
                features(("qkv", i), ("win", i // 2), (i % 2) * 2 * P, 2 if i < 4 else 1, h0)

            for t in range(NT):
                taken(pe, "gu", t)
            pe.wait_ge(sem("band_in"), 16)
            pe.wait_ge(sem("poolw_in"), 16 * 4)
            pe.wait_ge(sem("zero_start"), 1)
            for i in range(2):
                b = empty("poolT", i)
                for j in range(2):
                    g = 2 * i + j
                    o = b[j * HD:(j + 1) * HD, 0:T]
                    pe.matmul(o, pool_in[:, 0, g * HD:(g + 1) * HD], band[:, g, 0:T], start=True, stop=False)
                    mm = pe.matmul(o[:, P:T], pool_in[:, 1, g * HD:(g + 1) * HD], band[:, g, T:],
                                   start=False, stop=True)
                full(mm)
            for k in range(2):
                b = empty("win", k)
                for t in range(NT):
                    taken(pe, "kv4", t)
                for j in range(NKV):
                    for t in range(NT):
                        mm = turn(b[:, (j * NT + t) * P:(j * NT + t + 1) * P], cmp_in[:, t, 2 * k + j, :])
                full(mm)
            qkv(0)
            qkv(1)
            for i in range(2):
                b = empty("poolY", i)
                taken(pe, "poolT", i)
                full(pe.matmul(b[:, 0:T], poolw[:, i, :], poolT[:, i, :], start=True, stop=True))
            for k in range(2):
                b = empty("hid", k)
                landed(pe, ("cmp1", k))
                pe.wait_ge(sem("cmp_x_ready"), k + 1)
                w = unit_view(("cmp1", k))
                for i in range(2):
                    for m in range(CM):
                        mm = pe.matmul(b[:, i * NKV * NC:(i + 1) * NKV * NC].rearrange("p (a b) -> p a b", a=NKV),
                                       w[:, m, i * P:(i + 1) * P],
                                       cmp_x[:, 2 * k:2 * k + 2, m, :], start=(m == 0), stop=(m == CM - 1))
                full(mm)
            for t in range(NT):
                b = empty("nq", t)
                pe.wait_ge(sem("nsa_qk_ready"), 1)
                for g in range(NG):
                    mm = turn(b[:, g * P:(g + 1) * P], nsa_qr[:, t, g * P:(g + 1) * P])
                full(mm)
            b = empty("nk")
            for s in range(2):
                for t in range(NT):
                    mm = turn(b[:, (s * NT + t) * P:(s * NT + t + 1) * P], nsa_kr[:, t, s, :])
            full(mm)
            qkv(2)
            b = empty("cmp")
            for k in range(2):
                taken(pe, "hid", k)
            pe.wait_ge(sem("cw2_in"), 16)
            for i in range(2):
                pe.matmul(b[0:NKV * NC, 0:HD], cmp_h[:, 0, i, :], cw2[:, 0, i, :], start=(i == 0), stop=(i == 1))
            for j in range(NKV):
                for i in range(2):
                    mm = pe.matmul(b[j * HD:j * HD + NC, P:P + HD], cmp_h[:, 1, i, j * NC:(j + 1) * NC],
                                   cw2[:, 1, i, :], start=(i == 0), stop=(i == 1))
            full(mm)
            qkv(3)
            b = empty("kcT")
            pe.wait_ge(sem("kc_ready"), 1)
            full(turn(b[:, 0:NKV * NC], cmp_kd[0:NKV * NC, :]))
            qkv(4)
            for t in range(NT):
                b = empty("cs", t)
                taken(pe, "nq", t)
                taken(pe, "kcT")
                for h in range(NH):
                    j = h % 2
                    mm = pe.matmul(b[:, h * NC:(h + 1) * NC], nsa_qT[:, h, t * P:(t + 1) * P],
                                   cmp_kT[:, j * NC:(j + 1) * NC], start=True, stop=True)
                full(mm)
            for t in range(NT):
                tokens(("z", t), ("win", 2), t, h0, P, GW)
            for t in range(NT):
                b = empty("pcT", t)
                pe.wait_ge(sem("pc_ready"), t + 1)
                for g in range(NG):
                    mm = turn(b[:, g * P:(g + 1) * P], pc[:, t, g, :])
                full(mm)

            def scores(g):
                kind, t, m0, n = GROUPS[g]
                b = empty("scores", g)
                if kind == "nsa":
                    taken(pe, "nq", t)
                    taken(pe, "nk")
                W = P * (t + 1)
                q = slice(t * P, (t + 1) * P)
                if kind == "nsa":
                    for s in range(n // 2):
                        mm = pe.matmul(b[:, s * 2 * W:(s + 1) * 2 * W].rearrange("p (a b) -> p a b", a=2),
                                       nsa_qT[:, m0 // 2 + s, q], nsa_kT[:, :, 0:W], start=True, stop=True)
                for i in range(n if kind == "fox" else 0):
                    h = m0 + i
                    o = b[:, i * W:(i + 1) * W]
                    pe.matmul(o, fqT[:, h, q], fkT[:, h // 2, 0:W], start=True, stop=False)
                    if t == 0:
                        mm = pe.matmul(o, const("le"), f_cols[:, 0, h, :], start=False, stop=True)
                    else:
                        pe.matmul(o[:, 0:P], const("ones"), f_cols[:, 0, h, :], start=False, stop=False)
                        pe.matmul(o[:, 0:P], const("le"), f_log[:, 1, h:h + 1].to_broadcast([P, P]),
                                  start=False, stop=False)
                        mm = pe.matmul(o[:, P:2 * P], const("le"), f_cols[:, 1, h, :], start=False, stop=True)
                for i in range(n if kind == "dif" else 0):
                    m = m0 + i
                    mm = pe.matmul(b[:, i * W:(i + 1) * W], dqT[:, m, q], dkT[:, m // 2, 0:W], start=True, stop=True)
                full(mm)

            def probs_turned(g):
                kind, t, m0, n = GROUPS[g]
                b = empty("probsT", g)
                pe.wait_ge(sem("probs_ready"), g + 1)
                pr = (probs1 if kind == "nsa" else probs2)[:, g % 2, :]
                W = P * (t + 1)
                at = 0
                for i in range(0, n, 2 if kind == "dif" else 1):
                    for kt in range(t + 1):
                        mm = turn(b[:, at:at + P], pr[:, i * W + kt * P:i * W + (kt + 1) * P])
                        at += P
                full(mm)

            def attention(kind):
                for i, task in enumerate(attention_tasks(kind)):
                    (scores if task[0] == "scores" else probs_turned)(task[1])
                    if kind == "dif" and i in PA_AFTER:
                        branch_a(PA_AFTER.index(i))
                taken(pe, "probsT", GLAST[kind] - 1)

            def branch_a(i):
                for j in range(4):
                    taken(pe, "foxY", j)
                features(("pa", i), ("pa",), i * 2 * P, 2, (oaT, oaT_lo), 4)

            attention("nsa")
            for t in range(NT):
                taken(pe, "pcT", t)
            for i in range(NH // 2):
                b = empty("nsaY", i)
                for step in range(5):
                    for hh in range(2):
                        h = 2 * i + hh
                        g, j = h % NG, h // NG
                        m = 2 * (2 * g + j)
                        o = b[hh * HD:(hh + 1) * HD, 0:T]
                        v = slice(j * HD, (j + 1) * HD)
                        if step == 0:
                            mm = pe.matmul(o, cmp_vb[:, j, :], pcT[:, g, :], start=True, stop=False)
                        elif step < 3:
                            s = step - 1
                            mm = pe.matmul(o, nsa_v[:, 0, s, v], nsa_pT[:, m + s, 0:T], start=False, stop=False)
                        else:
                            s = step - 3
                            mm = pe.matmul(o[:, P:T], nsa_v[:, 1, s, v], nsa_pT[:, m + s, T:3 * P],
                                           start=False, stop=(step == 4))
                full(mm)

            b = empty("gc")
            pe.wait_ge(sem("g_log_ready"), 1)
            for t in range(NT):
                pe.matmul(b[:, t * GH:(t + 1) * GH], const("le_chunk"), g_log[:, t * GH:(t + 1) * GH], start=True, stop=True)
                pe.matmul(b[:, 12 + t * GH:12 + (t + 1) * GH], const("gt_chunk"), g_log[:, t * GH:(t + 1) * GH],
                          start=True, stop=True)
            for n in range(NCH):
                mm = pe.matmul(b[:, 24 + n * GH:24 + (n + 1) * GH], const(f"chunk{n % 2}"),
                               g_log[:, (n // 2) * GH:(n // 2 + 1) * GH], start=True, stop=True)
            full(mm)
            for i in range(3):
                b = empty("dec", i)
                pe.wait_ge(sem("g_cols_ready"), 1)
                full(pe.matmul(b[:, :].rearrange("p (a b) -> p a b", b=P), const("gt_chunk"),
                               g_cols[:, 4 * i:4 * i + 4, :], start=True, stop=True))
            for s in range(3):
                for t in range(NT):
                    b = empty("tok", s, t)
                    pe.wait_ge(sem("conv_ready"), 1)
                    for j in range(3):
                        mm = turn(b[:, j * P:(j + 1) * P], conv[:, 3 * s + j, t * P:(t + 1) * P])
                    full(mm)
            for s, src in (("k", g_kr), ("kb", g_kbr), ("q", g_qr), ("qd", g_qdr)):
                for t in range(NT):
                    b = empty("gT", s, t)
                    pe.wait_ge(sem("g_tok_ready"), {"k": 1, "kb": 2, "q": 1, "qd": 2}[s])
                    if s == "qd":
                        pe.wait_ge(sem("g_pool_ready"), 1)
                    for j in range(3):
                        mm = turn(b[:, j * P:(j + 1) * P], src[:, t, j * P:(j + 1) * P])
                    full(mm)
            for i in range(GH):
                b = empty("kk", i)
                t, p = i // 3, i % 3
                for s in ("k", "kb", "q"):
                    taken(pe, "gT", s, t)
                for hh in range(2):
                    mm = pe.matmul(b[:, hh * 2 * P:(hh + 1) * 2 * P].rearrange("p (a b) -> p a b", a=2),
                                   g_kT[:, p, t * P:(t + 1) * P], g_kbqT[:, 2 * p + hh, :, t * P:(t + 1) * P],
                                   start=True, stop=True)
                full(mm)
            for lev in range(6):
                for bt in range(3):
                    b = empty("invP", lev, bt)
                    if lev == 0:
                        pe.wait_ge(sem("inv_start"), 2)
                        taken(pe, "kk", 2 * bt)
                        taken(pe, "kk", 2 * bt + 1)
                    elif lev == 1:
                        pe.wait_ge(sem("inv_first"), bt + 1)
                    else:
                        taken(pe, "invQ", lev - 1, bt)
                    for u in range(4):
                        mm = pe.matmul(b[:, u * P:(u + 1) * P], lT[:, 4 * bt + u, :], inv_d[:, 4 * bt + u, :],
                                       start=True, stop=True)
                    full(mm)
                for bt in range(3):
                    if 0 < lev < 5:
                        b = empty("invQ", lev, bt)
                        taken(pe, "invP", lev, bt)
                        if lev > 0:
                            taken(pe, "invR", lev - 1, bt)
                        for u in range(4):
                            mm = pe.matmul(b[:, u * P:(u + 1) * P], inv_t[:, 4 * bt + u, :], inv_p[:, 4 * bt + u, :],
                                           start=True, stop=True)
                        full(mm)
                    b = empty("invR", lev, bt)
                    taken(pe, "invP", lev, bt)
                    if lev > 0:
                        taken(pe, "invR", lev - 1, bt)
                    for u in range(4):
                        mm = pe.matmul(b[:, u * P:(u + 1) * P], inv_p[:, 4 * bt + u, :], inv_t[:, 4 * bt + u, :],
                                       start=True, stop=True)
                    full(mm)
            def mix_step(t, h, k):
                wh, wl = high_low(("wout", h))
                xh, xl = rounded(yT[:, k, t * P:(t + 1) * P]), rounded(y_lo[:, k, t * P:(t + 1) * P])
                for i, (w, x) in enumerate(((wh, xl), (wh, xh), (wl, xh))):
                    mm = pe.matmul(bank[MIX_BANK["mix", t, h]][:, :], x, w[:, k, :],
                                   start=(k == 3 and i == 0), stop=(k == 2 and i == 2))
                return mm

            ahead = [(t, h, k) for h in range(2) for t in range(NT) for k in range(3, KD)]

            def mix_ahead(n):
                if len(ahead) == 4 * (KD - 3):
                    pe.wait_ge(sem("y_split"), 2)
                    split_ready(pe, ("wout", 1))
                    for task in MIX_BANK:
                        bank_of(*task)
                for _ in range(min(n, len(ahead))):
                    mix_step(*ahead.pop(0))

            for t in range(NT):
                b = empty("u", t)
                for bt in range(3):
                    taken(pe, "invR", 5, bt)
                pe.wait_ge(sem("g_tok_ready"), 3)
                for h in range(GH):
                    mm = pe.matmul(b[:, h * HD:(h + 1) * HD], inv_t[:, t * GH + h, :], g_v[:, t * GH + h, :],
                                   start=True, stop=True)
                full(mm)
                b = empty("wT", t)
                for h in range(GH):
                    mm = pe.matmul(b[(h % 2) * HD:(h % 2 + 1) * HD, (h // 2) * P:(h // 2 + 1) * P],
                                   g_kbe[:, t * GH + h, :], inv_t[:, t * GH + h, :], start=True, stop=True)
                full(mm)
            for n in range(NCH):
                t, lo = n // 2, (n % 2) * CHUNK
                tok = slice(n * CHUNK, (n + 1) * CHUNK)
                b = empty("wS", n)
                taken(pe, "u", t)
                taken(pe, "wT", t)
                taken(pe, "gT", "qd", t)
                pe.wait_ge(sem("state_ready"), n + 1)
                for p in range(3):
                    mm = pe.matmul(b[lo:lo + CHUNK, p * P:(p + 1) * P], g_wT[:, p, tok], g_state[:, p, :],
                                   start=True, stop=True)
                full(mm)
                b = empty("qS", n)
                for p in range(3):
                    mm = pe.matmul(b[lo:lo + CHUNK, p * P:(p + 1) * P], g_qdT[:, p, tok], g_state[:, p, :],
                                   start=True, stop=True)
                full(mm)
                mix_ahead(1)
                if n < NCH - 1:
                    b = empty("kV", n)
                    taken(pe, "wS", n)
                    for p in range(3):
                        mm = pe.matmul(b[:, p * P:(p + 1) * P], g_kdr[lo:lo + CHUNK, t, p * P:(p + 1) * P],
                                       g_vn[lo:lo + CHUNK, t, p * P:(p + 1) * P], start=True, stop=True)
                    full(mm)
                    mix_ahead(2)
                if n % 2 == 1:
                    b = empty("o", t)
                    taken(pe, "wS", n)
                    for h in range(GH):
                        mm = pe.matmul(b[:, h * HD:(h + 1) * HD], qkT[:, t * GH + h, :],
                                       g_vn[:, t, h * HD:(h + 1) * HD], start=True, stop=True)
                    full(mm)
            mix_ahead(len(ahead))
            for t in range(NT):
                b = empty("gdnY", t)
                pe.wait_ge(sem("gdn_y_ready"), 1)
                for j in range(3):
                    mm = turn(b[:, j * P:(j + 1) * P], g_y[:, t, j * P:(j + 1) * P])
                full(mm)

            for t in range(NT):
                taken(pe, "gdnY", t)
            for h in range(2):
                for t in range(NT):
                    empty("mix", t, h)
                    for k in range(3):
                        mm = mix_step(t, h, k)
                    full(mm)
            turn_rows(1)
            hT_ready(1)
            for i in range(FT // 2):
                features(("ff1", i), ("w1", i // 2), (i % 2) * 2 * P, 2, (hT, hT_lo[1]))
            acc = [empty("ff2", t, h) for t in range(NT) for h in range(2)]
            for i in range(8):
                split_ready(pe, ("w2", i))
                pe.wait_ge(sem("ff_h_ready"), 2 * i + 2)
                wh, wl = high_low(("w2", i))
                for k in range(4):
                    xh, xl = rounded(ff_hi(4 * i + k)[:, 0, :]), rounded(ff_lo[:, 4 * i + k, :])
                    for t in range(NT):
                        for h in range(2):
                            for j, (w, x) in enumerate(((wh, xl), (wh, xh), (wl, xh))):
                                mm = pe.matmul(acc[2 * t + h][:, :], x[:, t * P:(t + 1) * P],
                                               w[:, k, h * 512:(h + 1) * 512],
                                               start=(i == 0 and k == 0 and j == 0), stop=(i == 7 and k == 3 and j == 2))
                            if i == 7 and k == 3:
                                full(mm)
                            elif k == 3 and t == 1 and h == 1:
                                mm.then_inc(sem("w2_used"), 1)

            turn_rows(2)
            hT_ready(2)
            b = empty("ff")
            pe.wait_ge(sem("w_ff_in"), 16)
            h2 = (hT, hT_lo[2])
            for k in range(KD):
                for i, x in enumerate(h2):
                    mm = pe.matmul(b[0:FOX, 0:T], w_ff[:, k, :], reread(tiles(x)[k]),
                                   start=(k == 0 and i == 0), stop=(k == KD - 1 and i == 1))
            full(mm)
            for i in range(2):
                features(("fq", i), ("win2", 0), i * 2 * P, 2, h2)
            b = empty("ffT")
            taken(pe, "ff")
            for t in range(NT):
                mm = turn(b[:, t * FOX:(t + 1) * FOX], f_raw[0:FOX, t * P:(t + 1) * P])
            full(mm)
            for i in range(2):
                features(("fk", i), ("win2", 1), i * 2 * P, 2, h2)
            for t in range(NT):
                tokens(("fv", t), ("win2", 2), t, h2)
            for s, u in (("dq", 3), ("dk", 4)):
                for i in range(2):
                    features((s, i), ("win2", u), i * 2 * P, 2, h2)
            for t in range(NT):
                tokens(("dv", t), ("win2", 5), t, h2)
            for i in range(8):
                features(("gate", i), ("win2", 6 + i // 2), (i % 2) * 2 * P, 2, h2)

            for task in [(s, i) for s in ("fq", "fk", "fv", "dq", "dk", "dv") for i in range(2)]:
                taken(pe, *task)
            pe.wait_ge(sem("f_cols_ready"), NT)
            attention("fox")
            for i in range(4):
                b = empty("foxY", i)
                for kt in range(NT):
                    for hh in range(2):
                        h = 2 * i + hh
                        o = b[hh * HD:(hh + 1) * HD, kt * P:T]
                        mm = pe.matmul(o, fv[:, kt, h * HD:(h + 1) * HD], fox_pT[:, h, kt * T:kt * P + T],
                                       start=(kt == 0), stop=(kt == 1))
                full(mm)
            attention("dif")
            for t in range(NT):
                b = empty("difO", t)
                for h in range(DIF):
                    o = b[:, h * P:(h + 1) * P]
                    if t == 0:
                        mm = pe.matmul(o, dif_pT[:, h, 0:P], dv[:, 0, h * P:(h + 1) * P], start=True, stop=True)
                    else:
                        pe.matmul(o, dif_pT[:, h, P:2 * P], dv[:, 0, h * P:(h + 1) * P], start=True, stop=False)
                        mm = pe.matmul(o, dif_pT[:, h, 2 * P:3 * P], dv[:, 1, h * P:(h + 1) * P],
                                       start=False, stop=True)
                full(mm)
            branch_a(3)
            for t in range(NT):
                b = empty("difT", t)
                pe.wait_ge(sem("dif_o_ready"), 1)
                for h in range(DIF):
                    mm = turn(b[:, h * P:(h + 1) * P], dif_o[:, t * DIF + h, :])
                full(mm)
            for t in range(NT):
                taken(pe, "difT", t)
            for i in range(4):
                features(("pb", i), ("pb",), i * 2 * P, 2, (obT, obT_lo), 4)
            pe.wait_ge(sem("y2_lo_ready"), 4)
            for h in range(2):
                for t in range(NT):
                    tokens(("wo", t, h), ("wo2", h), t, (y2_hi, y2_lo))

            turn_rows(3)
            hT_ready(3)
            b = empty("route")
            pe.wait_ge(sem("w_route_in"), 32)
            W = NGRP + EXPERTS
            for t in range(NT):
                for k in range(KD):
                    mm = pe.matmul(b[:, t * W:(t + 1) * W], hT[:, k, t * P:(t + 1) * P], w_route[:, k, :],
                                   start=(k == 0), stop=(k == KD - 1))
            full(mm)
            b = empty("rank")
            pe.wait_ge(sem("hot_ready"), 1)
            pe.matmul(b[:, 0:EXPERTS], const("lt"), r_hot[:, 0, :], start=True, stop=True)
            pe.matmul(b[:, EXPERTS:2 * EXPERTS], const("ones"), r_hot[:, 0, :], start=True, stop=False)
            full(pe.matmul(b[:, EXPERTS:2 * EXPERTS], const("lt"), r_hot[:, 1, :], start=False, stop=True))
            b = empty("count")
            pe.matmul(b[:, 0:EXPERTS], const("ones"), r_hot[:, 0, :], start=True, stop=False)
            full(pe.matmul(b[:, 0:EXPERTS], const("ones"), r_hot[:, 1, :], start=False, stop=True))

            for b in range(BANKS):
                pe.wait_ge(sem(f"bank_free{b}"), BANK_USES[b])
            pe.wait_ge(sem("passes_known"), 1)
            n = pe.value_load(passes[0:1, 0:1], min_val=1, max_val=MAXPASS)
            ps_h1, ps_h3, ps_x0, ps_x1, ps_t, ps_g, ps_y0, ps_y1 = bank

            def gather(count):
                pe.wait_ge(sem("pick_ready"), count + 1)
                for part, b in enumerate((ps_x0, ps_x1)):
                    for kk in range(4):
                        k = 4 * part + kk
                        for t in range(NT):
                            mm = pe.matmul(b[:, kk * P:(kk + 1) * P], xn[:, t, k * P:(k + 1) * P],
                                           pick[:, t, :], start=(t == 0), stop=(t == 1))
                    mm.then_inc(sem(f"x{part}_full"), 1)

            gather(0)
            with pe.Fori(0, n * (PAIRS // 2)) as half:
                for odd in range(2):
                    it = half * 2 + odd
                    pe.wait_ge(sem("xg0_ready"), it + 1)
                    pe.wait_ge(sem("xg1_ready"), it + 1)
                    for k, (b, done) in enumerate(((ps_h1, "h1_full"), (ps_h3, "h3_full"))):
                        for e in range(2):
                            if k + e == 0:
                                pe.wait_ge(expert_landed(0, odd), (half + (0 if odd else ebase[0]) + 1) * 16)
                            else:
                                pe.wait_ge(expert_landed(2 * k + e, odd), (it + ebase[2 * k + e] + 1) * 16)
                        for kk in range(KD):
                            for e in range(2):
                                mm = pe.matmul(b[e * CAP:(e + 1) * CAP, :], xg[:, odd, kk, e * CAP:(e + 1) * CAP],
                                               expert_view(2 * k + e, odd)[:, kk, :], start=(kk == 0), stop=(kk == KD - 1))
                        mm.then_inc(sem(done), 1)
                    pe.wait_ge(sem("added"), it * 4 + 4)
                    gather(it + 1)
                    for t in range(NT):
                        mm = turn(ps_g[:, t * P:(t + 1) * P], give[:, odd, t, :])
                    mm.then_inc(sem("giveT_full"), 1)
                    pe.wait_ge(sem("act_ready"), it + 1)
                    for f in range(4):
                        mm = turn(ps_t[:, f * P:(f + 1) * P], act[:, f * P:(f + 1) * P])
                    mm.then_inc(sem("t_full"), 1)
                    for e in range(2):
                        pe.wait_ge(expert_landed(4 + e, odd), (it + ebase[4 + e] + 1) * 16)
                    pe.wait_ge(sem("actT_ready"), it + 1)
                    for h, b in enumerate((ps_y0, ps_y1)):
                        for f in range(4):
                            for e in range(2):
                                mm = pe.matmul(b[e * CAP:(e + 1) * CAP, :], actT[:, f, e * CAP:(e + 1) * CAP],
                                               expert_view(4 + e, odd)[:, f, h * 512:(h + 1) * 512],
                                               start=(f == 0), stop=(f == 3))
                        mm.then_inc(sem("y_full"), 1)
                    pe.wait_ge(sem("giveT_ready"), it + 1)
                    pe.wait_ge(sem("xg0_ready"), it + 2)
                    pe.wait_ge(sem("xg1_ready"), it + 2)
                    for h in range(2):
                        pe.wait_ge(sem(f"y{h}_ready"), it + 1)
                        for t in range(NT):
                            b = ((ps_x0, ps_x1), (ps_t, ps_g))[h][t]
                            pe.matmul(b[:, :], giveT[:, t, :], y_e[:, h * 512:(h + 1) * 512],
                                      start=True, stop=True).then_inc(sem("c_full"), 1)

        def rms_reciprocal(chain, ss, rs, n, done):
            chain(nc.scalar.activation(rs, ss, ACT.Ln, scale=1.0 / n, bias=EPS))
            chain.own()
            nc.scalar.activation(rs, rs, ACT.Exp, scale=-0.5).then_inc(sem(done), 1)

        @block.vector
        def _(dve):
            v = Chain(dve, "dve_own")
            TT, TS, STT, RED, CP = (nc.vector.tensor_tensor, nc.vector.tensor_scalar,
                                    nc.vector.scalar_tensor_tensor, nc.vector.tensor_reduce, nc.vector.tensor_copy)

            def squares(stage, junk):
                if 1 <= stage <= 3:
                    taken(dve, ("mix", "ff2", "wo")[stage - 1], 1, 1)
                nc.vector.tensor_tensor_reduce(junk[:, 1, :], x_sb[:, 1, :], x_sb[:, 1, :], 1.0, 0.0,
                                               ALU.mult, ALU.add, ssx[:, stage, 1:2]).then_inc(sem("ss_ready"), 1)

            def normalize(stage):
                squares(stage, xn)
                dve.wait_ge(sem("rms_ready"), stage + 1)
                if stage < 3:
                    TS(xn[:, 0, :], x_sb[:, 0, :], rsx[:, stage, 0:1], None, ALU.mult).then_inc(sem("xn_ready"), 1)
                    return
                dve.wait_ge(sem("g_moe_in"), 16)
                for t in range(NT):
                    STT(xn[:, t, :], x_sb[:, t, :], rsx[:, stage, t:t + 1], bias_c[:, 0:D], ALU.mult, ALU.mult)\
                        .then_inc(sem("xn_ready"), 1)

            def take_hT(stage, name):
                for i in range(4):
                    b = filled(dve, "hT", stage, i)
                    dve.wait_ge(sem("hT_hi_ready"), 4 * stage + i + 1)
                    for j in range(2):
                        k = 2 * i + j
                        ins = STT(rounded(hT_lo[stage][k]), b[:, j * T:(j + 1) * T], vec(name, k),
                                  reread(hT[:, k, :]), ALU.mult, ALU.subtract)
                        v(ins) if j == 0 else ins.then_inc(emptied("hT", stage, i), 1)

            def take_rows():
                for i in (0, 2):
                    b = filled(dve, "hT", 3, i)
                    CP(hT[:, 2 * i:2 * i + 2, :], b[:, :].rearrange("p (a b) -> p a b", b=T))\
                        .then_inc(emptied("hT", 3, i), 1)

            def split(*name, steps=range(PARTS)):
                for q in steps:
                    w, hi, lo = split_step(name, q)
                    dve.wait_ge(sem("hi_ready"), PARTS * SPLIT[name] + q + 1)
                    TT(rounded(lo), w, reread(hi), ALU.subtract).then_inc(sem("lo_ready"), 1)

            def low(dst, b, hi, *task):
                TT(rounded(dst), b, reread(hi), ALU.subtract).then_inc(emptied(*task), 1)

            def sigmoid_end(ap, count):
                dve.wait_ge(sem("small_exp"), count)
                v(TS(ap, ap, 1.0, None, ALU.add))
                v.own()
                v(nc.vector.reciprocal(ap, ap))

            def add_to_x(*task):
                t, h = task[-2:]
                b = filled(dve, *task)
                o = x_sb[:, t, h * 512:(h + 1) * 512]
                TT(o, b[:, :], o, ALU.add).then_inc(emptied(*task), 1)

            CP(vT[:, :], filled(dve, "vec")[:, 0:NVEC]).then_inc(emptied("vec"), 1)
            taken(dve, "vec")
            dve.wait_ge(sem("x_in"), 16)
            normalize(0)
            take_hT(0, "norm_mix")
            split_ready(dve, ("win", 5))
            for i in (3, 4, 6, 0):
                split("win", i)

            def convolve(i):
                b = filled(dve, "qkv", i)
                dve.wait_ge(sem("tap_ready"), i + 1)
                n = 2 if i < 4 else 1
                for s in range(1, CONV):
                    for j in range(n):
                        f = 2 * i + j
                        ins = STT(conv[:, f, s:], b[:, j * T:(j + 1) * T - s], vec("conv_w", (CONV - 1 - s) * QF + f),
                                  conv[:, f, s:], ALU.mult, ALU.add)
                        if s == CONV - 1 and j == n - 1:
                            ins.then_inc(emptied("qkv", i), 1)
                        else:
                            v(ins)
                    v.own()

            taken(dve, "baq", 1)
            dve.wait_ge(sem("rows_in"), 16 * len(ROWS))
            v(TT(g_x.rearrange("p (t h) -> p t h", t=NT), ba[:, :, GH:], over(row("dt_bias"), NT), ALU.add))
            v.own()
            STT(g_t1, g_x, -1.0, g_x, ALU.mult, ALU.max).then_inc(sem("softplus_in"), 1)
            sigmoid_end(beta, 1)
            split("win", 1)
            taken(dve, "gu", 1)
            sigmoid_end(nsa_gate.rearrange("p a b -> p (a b)"), 2)
            dve.wait_ge(sem("softplus_ln"), 1)
            v(STT(g_t2, g_x, 0.0, g_t2, ALU.max, ALU.add))
            v.own()
            v(TS(g_t2, g_t2, -1.0, None, ALU.mult))
            v.own()
            TT(g_log.rearrange("p (t h) -> p t h", t=NT), g_t2.rearrange("p (t h) -> p t h", t=NT),
               over(ealog, NT), ALU.mult).then_inc(sem("g_log_ready"), 1)

            for i in range(2):
                CP(poolT[:, i, :], filled(dve, "poolT", i)[:, 0:T]).then_inc(emptied("poolT", i), 1)

            for k in range(2):
                b = filled(dve, "win", k)[:, :].rearrange("p (j t) -> p j t", j=NKV)
                v(CP(cmp_win[0:HD, 2 * k:2 * k + 2, :], b[0:HD, :, :]))
                CP(cmp_win[HD:P, 2 * k:2 * k + 2, 0:T - 1], b[HD:P, :, 1:T]).then_inc(emptied("win", k), 1)
                taken(dve, "win", k)
                for j in range(NKV):
                    w = cmp_win[:, 2 * k + j, :].rearrange("p (b m two) -> p m b two", m=8, two=2)
                    for half in range(2):
                        at = VEC["cmp_pos"][0] + k * CM + half * 8
                        ins = TT(cmp_x[:, 2 * k + j, 8 * half:8 * half + 8, :], w[:, :, half:half + NC, 0],
                                 wide(vT[:, at:at + 8], NC), ALU.add)
                        v(ins) if (j, half) != (1, 1) else ins.then_inc(sem("cmp_x_ready"), 1)
            nq = cut(6912, NT * NH, HD)
            nk = cut(8704, NT * 4, HD)
            sq_q, sq_k = cut(0, NT * NH, HD), cut(768, NT * 4, HD)
            taken(dve, "kvw", 1)
            taken(dve, "kv4", 1)
            for i in range(4):
                taken(dve, "hT", 0, i)
            v(TT(sq_q, nq, nq, ALU.mult))
            v(TT(sq_k, nk, nk, ALU.mult))
            v.own()
            v(RED(n_ss[:, 0:12], sq_q, AX, ALU.add))
            RED(n_ss[:, 12:20], sq_k, AX, ALU.add).then_inc(sem("n_ss_ready"), 1)
            qn8 = kc_sq
            v(TS(qn8, row("q_norm"), HD ** -0.5, None, ALU.mult))
            dve.wait_ge(sem("n_rs_ready"), 1)
            v(TT(nq, nq, wide(n_rs[:, 0:12], HD), ALU.mult))
            v(TT(nk, nk, wide(n_rs[:, 12:20], HD), ALU.mult))
            v.own()
            v(TT(nq, nq, over(qn8, 12), ALU.mult))
            kn = row("k_norm")
            for t in range(NT):
                for s in range(2):
                    o = cut(8704 + (t * 2 + s) * NKV * HD, NKV, HD)
                    ins = TT(o, o, over(kn[:, (s + 1) * HD:(s + 2) * HD], NKV), ALU.mult)
                    v(ins) if (t, s) != (1, 1) else ins.then_inc(sem("nsa_qk_ready"), 1)

            convolve(0)
            convolve(1)
            for i in range(2):
                TS(yT[:, 6 + i, :], filled(dve, "poolY", i)[:, 0:T], vec("pool_scale", i), None, ALU.mult)\
                    .then_inc(emptied("poolY", i), 1)
            for k in range(2):
                n = 2 * NKV * NC
                b = filled(dve, "hid", k)
                h = cmp_h[:, k, :, :].rearrange("p a b -> p (a b)")
                sigmoid_end(h, 3 + k)
                v.own()
                TT(h, b[:, 0:n], h, ALU.mult).then_inc(emptied("hid", k), 1)
            split("win", 2)
            b = filled(dve, "cmp")
            r = NKV * NC
            dve.wait_ge(sem("zero_nsa"), 1)
            v(CP(kc_raw[0:r, :], b[0:r, 0:HD]))
            for j in range(NKV):
                ins = CP(cmp_vb[j * HD:j * HD + NC, j, :], b[j * HD:j * HD + NC, P:P + HD])
                v(ins) if j == 0 else ins.then_inc(emptied("cmp"), 1)
            v.own()
            v(TT(kc_sq[0:r, :], kc_raw[0:r, :], kc_raw[0:r, :], ALU.mult))
            v.own()
            RED(kc_ss[0:r, :], kc_sq[0:r, :], AX, ALU.add).then_inc(sem("kc_ss_ready"), 1)
            dve.wait_ge(sem("kc_rs_ready"), 1)
            for i in range(2):
                ins = STT(cmp_kd[0:r, i * HD:(i + 1) * HD], kc_raw[0:r, :], kc_rs[0:r, :], kn[0:r, 0:HD],
                          ALU.mult, ALU.mult)
                v(ins) if i == 0 else ins.then_inc(sem("kc_ready"), 1)
            for i in (2, 3, 4):
                convolve(i)
            add, mul = const("cmp_add"), const("cmp_mul")
            for t in range(NT):
                b = filled(dve, "cs", t)
                s = c_sc[:, t, :].rearrange("p (h n) -> p h n", n=NC)
                TT(s, b[:, 0:NH * NC].rearrange("p (h n) -> p h n", n=NC), over(add[:, t * NC:(t + 1) * NC], NH),
                   ALU.add).then_inc(emptied("cs", t), 1)
                taken(dve, "cs", t)
                v(RED(c_mx[:, t, :], s, AX, ALU.max))
                v.own()
                TT(s, s, wide(c_mx[:, t, :], NC), ALU.subtract).then_inc(sem("c_sc_ready"), 1)
            for t in range(NT):
                s = c_sc[:, t, :].rearrange("p (h n) -> p h n", n=NC)
                dve.wait_ge(sem("c_exp_ready"), t + 1)
                v(RED(c_sm[:, t, :], s, AX, ALU.add))
                v.own()
                v(nc.vector.reciprocal(c_sm[:, t, :], c_sm[:, t, :]))
                v(TT(s, s, over(mul[:, t * NC:(t + 1) * NC], NH), ALU.mult))
                v.own()
                gate = nsa_gate[:, t, :].rearrange("p (j g c) -> p g j c", j=NKV, c=3)[:, :, :, 0]
                cs = c_sm[:, t, :].rearrange("p (g j) -> p g j", j=NKV)
                v(TT(cs, cs, gate, ALU.mult))
                v.own()
                o = pc[:, t, :, :].rearrange("p g (j n) -> p (g j) n", j=NKV)[:, :, 0:NC]
                TT(o, s, wide(c_sm[:, t, :], NC), ALU.mult).then_inc(sem("pc_ready"), 1)

            def maxima(g):
                kind, t, m0, n = GROUPS[g]
                b = filled(dve, "scores", g)
                sc = (scores1 if kind == "nsa" else scores2)[:, g % 2, :]
                W = P * (t + 1)
                for i in range(n):
                    if kind == "dif":
                        bias = alibi[:, (m0 + i) // 2, 0:P] if t == 0 else alibi[:, (m0 + i) // 2, P:3 * P]
                    else:
                        bias = const("causal")[:, 0:P] if t == 0 else const("causal")[:, P:3 * P]
                    ins = nc.vector.tensor_tensor_reduce(
                        sc[:, i * W:(i + 1) * W], b[:, i * W:(i + 1) * W], bias, 1.0, -3e38,
                        ALU.add, ALU.max, mx[:, g % 2, i:i + 1])
                    v(ins) if i < n - 1 else ins.then_inc(emptied("scores", g), 1)
                taken(dve, "scores", g)
                TS(nmx[:, g % 2, 0:n], mx[:, g % 2, 0:n], -1.0, None, ALU.mult).then_inc(sem("max_ready"), 1)

            def weights(g):
                kind, t, m0, n = GROUPS[g]
                pr = (probs1 if kind == "nsa" else probs2)[:, g % 2, :]
                W = P * (t + 1)
                c = coef[:, g % 2, 0:n]
                dve.wait_ge(sem("exp_ready"), g + 1)
                v(nc.vector.reciprocal(c, esum[:, g % 2, 0:n]))
                v.own()
                if kind == "nsa":
                    for i in range(n // 2):
                        slot = m0 // 2 + i
                        h = (slot % 2) * NG + slot // 2
                        v(TT(c[:, 2 * i:2 * i + 2], c[:, 2 * i:2 * i + 2], nsa_gate[:, t, 3 * h + 1:3 * h + 3], ALU.mult))
                    v.own()
                if kind == "dif":
                    c2 = c.rearrange("p (a b) -> p a b", b=2)[:, :, 1]
                    v(TS(c2, c2, lam[:, 0:1], None, ALU.mult))
                    v.own()
                    for i in range(0, n, 2):
                        v(TS(pr[:, i * W:(i + 1) * W], pr[:, i * W:(i + 1) * W], c[:, i:i + 1], None, ALU.mult))
                    v.own()
                    for i in range(0, n, 2):
                        ins = STT(pr[:, i * W:(i + 1) * W], pr[:, (i + 1) * W:(i + 2) * W], c[:, i + 1:i + 2],
                                  pr[:, i * W:(i + 1) * W], ALU.mult, ALU.add)
                        v(ins) if i < n - 2 else ins.then_inc(sem("probs_ready"), 1)
                    return
                for i in range(n):
                    ins = TS(pr[:, i * W:(i + 1) * W], pr[:, i * W:(i + 1) * W], c[:, i:i + 1], None, ALU.mult)
                    v(ins) if i < n - 1 else ins.then_inc(sem("probs_ready"), 1)

            def branch_a(i):
                if i == 0:
                    for j in range(8):
                        taken(dve, "gate", j)
                b = filled(dve, "pa", i)[:, :].rearrange("p (a b) -> p a b", b=T)
                TT(yT[:, 2 * i:2 * i + 2, :], gates[:, 2 * i:2 * i + 2, :], b, ALU.mult).then_inc(emptied("pa", i), 1)

            def attention(kind):
                for g in range(GFIRST[kind], GLAST[kind] + 1):
                    if g < GLAST[kind]:
                        maxima(g)
                    if g > GFIRST[kind]:
                        weights(g - 1)
                    if kind == "dif" and g - GFIRST[kind] in (2, 4, 6):
                        branch_a((g - GFIRST[kind]) // 2 - 1)

            attention("nsa")

            for s in range(3):
                taken(dve, "tok", s, 1)
            v(TT(g_sq, g_qk, g_qk, ALU.mult))
            v.own()
            RED(gq_ss, g_sq, AX, ALU.add).then_inc(sem("gq_ss_ready"), 1)
            dve.wait_ge(sem("gq_rs_ready"), 1)
            v(TS(gq_rs[:, 0:12], gq_rs[:, 0:12], HD ** -0.5, None, ALU.mult))
            v.own()
            TT(g_qk, g_qk, wide(gq_rs, HD), ALU.mult).then_inc(sem("g_tok_ready"), 1)
            dve.wait_ge(sem("g_tok_ready"), 1)
            TT(g_kb, g_k, wide(beta, HD), ALU.mult).then_inc(sem("g_tok_ready"), 1)
            taken(dve, "gc")
            dve.wait_ge(sem("g_tok_ready"), 2)
            v(TT(g_kbe, g_kb, wide(e_gc, HD), ALU.mult))
            TT(g_v, g_v, wide(beta, HD), ALU.mult).then_inc(sem("g_tok_ready"), 1)
            dve.wait_ge(sem("zero_kbq"), 1)
            for t in range(NT):
                b = filled(dve, "gT", "kb", t)[:, 0:GW].rearrange("p (j n) -> p j n", n=P)
                for hh in range(2):
                    r = slice(hh * HD, (hh + 1) * HD)
                    ins = CP(g_kbqT[r, hh::2, 0, t * P:(t + 1) * P], b[r, :, :])
                    v(ins) if hh == 0 else ins.then_inc(emptied("gT", "kb", t), 1)
            dve.wait_ge(sem("decay_ready"), 1)
            for i in range(GH):
                b = filled(dve, "kk", i)[:, :].rearrange("p (u w n) -> p u w n", w=2, n=P)
                d = decay[:, 2 * i:2 * i + 2, :]
                v(TT(lT[:, 2 * i:2 * i + 2, :], b[:, :, 0, :], d, ALU.mult))
                TT(qkT[:, 2 * i:2 * i + 2, :], b[:, :, 1, :], d, ALU.mult).then_inc(emptied("kk", i), 1)
            for lev in range(6):
                for bt in range(3):
                    u = slice(4 * bt, 4 * bt + 4)
                    b = filled(dve, "invP", lev, bt)[:, :].rearrange("p (u n) -> p u n", n=P)
                    TT(inv_p[:, u, :], b, over(invmask[:, lev, :], 4), ALU.mult).then_inc(emptied("invP", lev, bt), 1)
                    if lev == 0:
                        dve.wait_ge(sem("inv_start"), 2)
                        taken(dve, "invP", lev, bt)
                        TT(inv_d[:, u, :], inv_d[:, u, :], inv_p[:, u, :], ALU.subtract).then_inc(sem("inv_first"), 1)
                for bt in range(3):
                    u = slice(4 * bt, 4 * bt + 4)
                    for name, m in ((("invQ", inv_d),) if 0 < lev < 5 else ()) + (("invR", inv_t),):
                        b = filled(dve, name, lev, bt)[:, :].rearrange("p (u n) -> p u n", n=P)
                        if lev == 0:
                            dve.wait_ge(sem("inv_start"), 2)
                        TT(m[:, u, :], m[:, u, :], b, ALU.subtract).then_inc(emptied(name, lev, bt), 1)
            for n in range(NCH):
                t, r = n // 2, slice((n % 2) * CHUNK, (n % 2 + 1) * CHUNK)
                b = filled(dve, "wS", n)
                taken(dve, "u", t)
                TT(g_vn[r, t, :], g_u[r, t, :], b[r, 0:GW], ALU.subtract).then_inc(emptied("wS", n), 1)
                if n < NCH - 1:
                    b = filled(dve, "kV", n)[:, 0:GW].rearrange("p (j n) -> p j n", n=P)
                    TT(g_upd, b, over(const("head_diag"), 3), ALU.mult).then_inc(emptied("kV", n), 1)
                    taken(dve, "kV", n)
                    dve.wait_ge(sem("state_ready"), n + 1)
                    taken(dve, "gc")
                    for p in range(3):
                        ins = STT(g_state[:, p, :], g_state[:, p, :], e_last[:, n, p:p + 1], g_upd[:, p, :],
                                  ALU.mult, ALU.add)
                        v(ins) if p < 2 else ins.then_inc(sem("state_ready"), 1)
                if n % 2 == 1:
                    b = filled(dve, "o", t)
                    taken(dve, "qS", n - 1)
                    taken(dve, "qS", n)
                    TT(g_o[:, t, :], g_o[:, t, :], b[:, 0:GW], ALU.add).then_inc(emptied("o", t), 1)
            taken(dve, "o", 1)
            o12 = cut(13824, 12, HD)
            q12 = cut(15360, 12, HD)
            y12 = cut(16128, 12, HD)
            v(TT(q12, o12, o12, ALU.mult))
            v.own()
            RED(go_ss, q12, AX, ALU.add).then_inc(sem("go_ss_ready"), 1)
            v(TT(y12, cut(19200, 12, HD), over(row("gdn_norm"), 12), ALU.mult))
            dve.wait_ge(sem("go_rs_ready"), 1)
            v(TT(o12, o12, wide(go_rs, HD), ALU.mult))
            v.own()
            TT(y12, y12, o12, ALU.mult).then_inc(sem("gdn_y_ready"), 1)

            for t in range(NT):
                dve.wait_ge(sem("gdn_hi_ready"), t + 1)
                b = filled(dve, "gdnY", t)[:, 0:GW].rearrange("p (j n) -> p j n", n=P)
                low(y_lo[:, 0:3, t * P:(t + 1) * P], b, yT[:, 0:3, t * P:(t + 1) * P], "gdnY", t)

            for h in range(2):
                for t in range(NT):
                    add_to_x("mix", t, h)
            normalize(1)
            take_hT(1, "norm_ffn")
            split_ready(dve, ("w1", 0))
            split("w1", 1)

            for i in range(2):
                ins = nc.vector.tensor_tensor_reduce(lam_p[:, i, :], row(f"lam_q{i + 1}"), row(f"lam_k{i + 1}"),
                                                     1.0, 0.0, ALU.mult, ALU.add, lam_s[:, i:i + 1])
            ins.then_inc(sem("lam_in"), 1)
            dve.wait_ge(sem("lam_exp"), 1)
            v(STT(lam, lam_s[:, 1:2], -LAM0, lam_s[:, 0:1], ALU.add, ALU.subtract))
            v(TS(row("g_subln"), row("g_subln"), 1.0 - LAM0, None, ALU.mult))
            for i in range(FT // 2):
                if i % 2 == 0 and i > 0:
                    split(*(("w1", i // 2 + 1) if i < 14 else ("w2", 0)))
                dve.wait_ge(sem("ff_hi_ready"), i + 1)
                r = ff_r[:, i % 2, :].rearrange("p (a b) -> p a b", b=T)
                v(TT(r, r, r, ALU.mult))
                v.own()
                TT(rounded(ff_lo[:, 2 * i:2 * i + 2, :]), r, reread(ff_hi(2 * i, 2)), ALU.subtract)\
                    .then_inc(sem("ff_h_ready"), 1)
            for i in range(1, 8):
                split("w2", i)
            split("win2", 0)
            for t in range(NT):
                for h in range(2):
                    add_to_x("ff2", t, h)

            normalize(2)
            take_hT(2, "g_mix")
            split("win2", 1)
            CP(f_raw[0:FOX, :], filled(dve, "ff")[0:FOX, 0:T]).then_inc(emptied("ff"), 1)

            def take_heads(name, dst, scale):
                dve.wait_ge(sem("zero_q"), 1)
                for i in range(2):
                    b = filled(dve, name, i)[:, :].rearrange("p (a b) -> p a b", b=T)
                    for hh in range(2):
                        r = slice(hh * HD, (hh + 1) * HD)
                        ins = TS(dst[r, 4 * i + hh:4 * i + hh + 3:2, :], b[r, :, :], scale, None, ALU.mult)
                        v(ins) if hh == 0 else ins.then_inc(emptied(name, i), 1)

            take_heads("fq", fqT, HD ** -0.5)
            b = filled(dve, "ffT")
            TT(f_x, b[:, 0:NT * FOX].rearrange("p (t h) -> p t h", t=NT), over(row("b_fgate"), NT), ALU.add)\
                .then_inc(emptied("ffT"), 1)
            taken(dve, "ffT")
            STT(f_t, f_x, -1.0, f_x, ALU.mult, ALU.max).then_inc(sem("softplus_in"), 1)
            dve.wait_ge(sem("softplus_ln"), 2)
            STT(f_log, f_x, 0.0, f_t, ALU.min, ALU.subtract).then_inc(sem("f_log_ready"), 1)
            split("win2", 2)
            split("win2", 3)
            for t in range(NT):
                CP(fv[:, t, :], filled(dve, "fv", t)[:, :]).then_inc(emptied("fv", t), 1)
            split("win2", 4)
            take_heads("dq", dqT, HD ** -0.5)
            split("win2", 5)
            split("win2", 6)
            for t in range(NT):
                CP(dv[:, t, :], filled(dve, "dv", t)[:, :]).then_inc(emptied("dv", t), 1)
            for i in (7, 8, 9):
                split("win2", i)
            split("pa")
            split("pb")
            attention("fox")
            for i in range(4):
                dve.wait_ge(sem("oa_hi_ready"), i + 1)
                low(oaT_lo[:, i, :], filled(dve, "foxY", i)[:, 0:T], oaT[:, i, :], "foxY", i)
            dve.wait_ge(sem("alibi_in"), 16)
            attention("dif")
            for t in range(NT):
                CP(dif_o[:, 4 * t:4 * t + 4, :].rearrange("p a b -> p (a b)"), filled(dve, "difO", t)[:, :])\
                    .then_inc(emptied("difO", t), 1)
            taken(dve, "difO", 0)
            taken(dve, "difO", 1)
            v(TT(dif_sq, dif_o, dif_o, ALU.mult))
            v.own()
            RED(d_ss, dif_sq, AX, ALU.add).then_inc(sem("d_ss_ready"), 1)
            dve.wait_ge(sem("d_rs_ready"), 1)
            v(TT(dif_o, dif_o, wide(d_rs, 2 * HD), ALU.mult))
            v.own()
            TT(dif_o, dif_o, over(row("g_subln"), NT * DIF), ALU.mult).then_inc(sem("dif_o_ready"), 1)
            branch_a(3)
            for t in range(NT):
                dve.wait_ge(sem("ob_hi_ready"), t + 1)
                low(obT_lo[:, :, t * P:(t + 1) * P], filled(dve, "difT", t)[:, :].rearrange("p (j n) -> p j n", n=P),
                    obT[:, :, t * P:(t + 1) * P], "difT", t)
            split("wo2", 0)

            def y2_low(i):
                dve.wait_ge(sem("y2_hi_ready"), i + 1)
                TT(rounded(y2_lo[:, 2 * i:2 * i + 2, :]), yT[:, 2 * i:2 * i + 2, :],
                   reread(y2_hi[:, 2 * i:2 * i + 2, :]), ALU.subtract).then_inc(sem("y2_lo_ready"), 1)

            for i in range(4):
                b = filled(dve, "pb", i)[:, :].rearrange("p (a b) -> p a b", b=T)
                if i >= 2:
                    dve.wait_ge(sem("yT2_ready"), i - 1)
                m = mix_b[:, i % 2, :].rearrange("p (a b) -> p a b", b=T)
                TT(m, gates[:, 8 + 2 * i:10 + 2 * i, :], b, ALU.mult).then_inc(emptied("pb", i), 1)
                taken(dve, "pb", i)
                y = yT[:, 2 * i:2 * i + 2, :]
                TT(y, y, m, ALU.add).then_inc(sem("yT2_ready"), 1)
                if i > 0:
                    y2_low(i - 1)
            y2_low(3)
            split("wo2", 1)
            for h in range(2):
                for t in range(NT):
                    add_to_x("wo", t, h)
            normalize(3)
            take_rows()

            b = filled(dve, "route")
            W = NGRP + EXPERTS
            at = ROWS["b_group"][0]
            TT(logit, b[:, 0:NT * W].rearrange("p (t n) -> p t n", t=NT), over(rows[:, at:at + W], NT), ALU.add)\
                .then_inc(emptied("route"), 1)
            taken(dve, "route")

            def step(ins):
                v(ins)
                v.own()

            def first_largest(src, ranks, top, idx, hot, tmp, n):
                step(RED(top, src, AX, ALU.max))
                step(TT(tmp, src, wide(top, n), ALU.is_equal))
                step(STT(tmp, tmp, -1000.0, over(ranks, NT), ALU.mult, ALU.add))
                step(RED(idx, tmp, AX, ALU.min))
                step(TT(hot, tmp, wide(idx, n), ALU.is_equal))

            gl = logit[:, :, 0:NGRP]
            first_largest(gl, const("rank4"), gm, gidx, ghot, gtmp, NGRP)
            TT(gtmp, gl, wide(gm, NGRP), ALU.subtract).then_inc(sem("group_in"), 1)
            step(TS(ghot, ghot, -NEG, NEG, ALU.mult, ALU.add))
            for t in range(NT):
                o = cut(14080 + 192 + t * EXPERTS, NGRP, EXPERTS // NGRP)
                step(TT(o, logit[:, t, NGRP:].rearrange("p (g e) -> p g e", g=NGRP),
                        wide(ghot[:, t, :], EXPERTS // NGRP), ALU.add))
            first_largest(r_l, const("rank32"), m1, i1, r_hot1, r_a, EXPERTS)
            step(STT(r_b, r_hot1, 3 * NEG, r_l, ALU.mult, ALU.add))
            first_largest(r_b, const("rank32"), m2, i2, r_hot2, r_a, EXPERTS)
            TT(e21, m2, m1, ALU.subtract).then_inc(sem("second_in"), 1)
            TT(r_hot, r_hot1, r_hot2, ALU.add).then_inc(sem("hot_ready"), 1)
            dve.wait_ge(sem("route_exp"), 2)
            step(RED(gsum, gtmp, AX, ALU.add))
            step(TS(den, e21, 1.0, None, ALU.add))
            step(TT(den, den, gsum, ALU.mult))
            step(nc.vector.reciprocal(w1s, den))
            step(TT(w2s, w1s, e21, ALU.mult))
            step(TT(r_a, r_hot1, wide(w1s, EXPERTS), ALU.mult))
            step(TT(r_b, r_hot2, wide(w2s, EXPERTS), ALU.mult))
            step(TT(swgt[:, :, 0:EXPERTS], r_a, r_b, ALU.add))
            step(CP(swgt[:, :, EXPERTS:], swgt[:, :, 0:2]))
            b = filled(dve, "rank")
            s = spos[:, :, 0:EXPERTS]
            dve.wait_ge(sem("hot_ready"), 1)
            STT(s, b[:, 0:NT * EXPERTS].rearrange("p (t e) -> p t e", t=NT), 1.0, r_hot, ALU.add, ALU.mult)\
                .then_inc(emptied("rank"), 1)
            taken(dve, "rank")
            step(TS(s, s, -1.0, None, ALU.add))
            step(TS(spos[:, :, EXPERTS:], spos[:, :, 0:2], -float(CAP), None, ALU.add))
            b = filled(dve, "count")
            RED(cmax[:, 0:1], b[:, 0:EXPERTS], AX, ALU.max).then_inc(emptied("count"), 1)
            taken(dve, "count")
            step(TS(cmax[:, 1:2], cmax[:, 0:1], float(CAP), 1.0, ALU.is_gt, ALU.add))
            for i in range(2, MAXPASS):
                step(STT(cmax[:, i:i + 1], cmax[:, 0:1], float(i * CAP), cmax[:, i - 1:i], ALU.is_gt, ALU.add))
            CP(passes[0:1, 0:1], cmax[0:1, 3:4]).then_inc(sem("passes_known"), 1)

            dve.wait_ge(sem("passes_known"), 1)
            n = dve.value_load(passes[0:1, 0:1], min_val=1, max_val=MAXPASS)
            ps_h3, ps_x0, ps_x1, ps_t, ps_g, ps_y0 = bank[1], bank[2], bank[3], bank[4], bank[5], bank[6]

            def choose(first, odd):
                for t in range(NT):
                    for e in range(2):
                        o = slice(e * CAP, (e + 1) * CAP)
                        pos = spos[:, t, bass.ds(first + e, 1)]
                        TS(pick[:, t, o], const("slot"), pos, None, ALU.is_equal)
                        ins = TS(give[:, odd, t, o], const("slot"), pos, swgt[:, t, bass.ds(first + e, 1)],
                                 ALU.is_equal, ALU.mult)
                ins.then_inc(sem("pick_ready"), 1)

            def take_tokens(to, count):
                dve.wait_ge(sem("x0_full"), count + 1)
                CP(xg[:, to, 0:4, :].rearrange("p a b -> p (a b)"), ps_x0[:, :]).then_inc(sem("xg0_ready"), 1)

            choose(0, 0)
            nc.vector.memset(g_t1[:, 0:1], 0.0).then_inc(sem("added"), 4)
            take_tokens(0, 0)
            with dve.Fori(0, n) as p:
                with dve.Fori(0, PAIRS // 2) as half:
                    for odd in range(2):
                        pair = half * 2 + odd
                        it = p * PAIRS + half * 2 + odd
                        dve.wait_ge(sem("x1_full"), it + 1)
                        choose(pair * 2 + 2, 1 - odd)
                        dve.wait_ge(sem("h3_full"), it + 1)
                        dve.wait_ge(sem("h1_read"), it + 1)
                        TT(act, act1, ps_h3[:, :], ALU.mult).then_inc(sem("act_ready"), 1)
                        take_tokens(1 - odd, it + 1)
                        dve.wait_ge(sem("y_full"), it * 2 + 1)
                        CP(y_e[:, 0:512], ps_y0[:, :]).then_inc(sem("y0_ready"), 1)
                        for h in range(2):
                            for t in range(NT):
                                dve.wait_ge(sem("c_full"), it * 4 + 2 * h + t + 1)
                                o = x_sb[:, t, h * 512:(h + 1) * 512]
                                b = ((ps_x0, ps_x1), (ps_t, ps_g))[h][t]
                                TT(o, b[:, :], o, ALU.add).then_inc(sem("added"), 1)
                dve.wait_ge(sem("pick_ready"), p * PAIRS + PAIRS + 1)
                TS(spos[:, :, :], spos[:, :, :], -float(CAP), None, ALU.add).then_inc(sem("next_slots"), 1)
                dve.wait_ge(sem("next_slots"), p + 1)

            dve.wait_ge(sem("added"), n * (4 * PAIRS) + 4)
            squares(4, out_sb)
            dve.wait_ge(sem("final_g_in"), 16)
            for t in range(NT):
                dve.wait_ge(sem("rms_ready"), 5)
                STT(out_sb[:, t, :], x_sb[:, t, :], rsx[:, 4, t:t + 1], final_g, ALU.mult, ALU.mult)\
                    .then_inc(sem("out_ready"), 1)

        @block.scalar
        def _(act):
            c = Chain(act, "act_own")
            ACTV, CPY = nc.scalar.activation, ACT.Copy

            act.dma_start(cst[:, :], consts).then_inc(sem("const_in"), 16)
            for name, (at, w) in VEC.items():
                src = {"norm_mix": a["norm_mix"][0].rearrange("(k p) -> k p", p=P),
                       "norm_ffn": a["norm_ffn"][0].rearrange("(k p) -> k p", p=P),
                       "g_mix": a["g_mix_2"][0].rearrange("(k p) -> k p", p=P),
                       "g_moe": a["g_moe_2"][0].rearrange("(k p) -> k p", p=P),
                       "b_gate": a["b_gate_2"][0].rearrange("(k p) -> k p", p=P),
                       "conv_w": a["conv_w"][0].rearrange("w (k p) -> (w k) p", p=P),
                       "pool_scale": a["pool_scale"][0].rearrange("(k p) -> k p", p=P),
                       "cmp_pos": a["cmp_pos"][0].rearrange("k (m two) d -> (k m) (two d)", two=2)}[name]
                act.dma_start(vrow[at:at + w, :], src).then_inc(sem("vrow_in"), 16)

            def rms(stage, junk):
                if 1 <= stage <= 3:
                    taken(act, ("mix", "ff2", "wo")[stage - 1], 0, 1)
                c(ACTV(junk[:, 0, :], x_sb[:, 0, :], ACT.Square, accum_out=ssx[:, stage, 0:1]))
                c.own()
                act.wait_ge(sem("ss_ready"), stage + 1)
                rms_reciprocal(c, ssx[:, stage, :], rsx[:, stage, :], D, "rms_ready")

            def normalize(stage):
                act.wait_ge(sem("rms_ready"), stage + 1)
                ACTV(xn[:, 1, :], x_sb[:, 1, :], CPY, scale=rsx[:, stage, 1:2]).then_inc(sem("xn_ready"), 1)

            def take_hT(stage, name):
                for i in range(4):
                    b = filled(act, "hT", stage, i)
                    for j in range(2):
                        k = 2 * i + j
                        ins = ACTV(rounded(hT[:, k, :]), b[:, j * T:(j + 1) * T], CPY, scale=vec(name, k))
                        c(ins) if j == 0 else ins.then_inc(sem("hT_hi_ready"), 1)

            def take_rows():
                for i in (1, 3):
                    copy_out(hT[:, 2 * i:2 * i + 2, :], filled(act, "hT", 3, i)[:, :].rearrange("p (a b) -> p a b", b=T),
                             "hT", 3, i)

            def split(*name, steps=range(PARTS)):
                landed(act, name)
                split_free(act, name)
                for q in steps:
                    w, hi, lo = split_step(name, q)
                    ACTV(rounded(hi), w, CPY).then_inc(sem("hi_ready"), 1)

            def copy_out(dst, src, *task):
                ACTV(dst, src, CPY).then_inc(emptied(*task), 1)

            act.preload_act_table_set("natural_log_exp_and_others")
            act.wait_ge(sem("x_in"), 16)
            rms(0, xn)
            normalize(0)
            split("win", 5)
            taken(act, "vec")
            take_hT(0, "norm_mix")

            def last_tap(i):
                b = filled(act, "qkv", i)
                for j in range(2 if i < 4 else 1):
                    f = 2 * i + j
                    ins = ACTV(conv[:, f, :], b[:, j * T:(j + 1) * T], CPY, scale=vec("conv_w", (CONV - 1) * QF + f))
                    if j == 0 and i < 4:
                        c(ins)
                    else:
                        ins.then_inc(sem("tap_ready"), 1)

            split("win", 3)
            for t in range(NT):
                b = filled(act, "kvw", t)
                c(ACTV(nsa_kr[:, t, 1, :], b[:, 0:2 * HD], CPY))
                copy_out(nsa_v[:, t, 1, :], b[:, 2 * HD:4 * HD], "kvw", t)
            split("win", 4)
            for t in range(NT):
                b = filled(act, "baq", t)
                c(ACTV(ba[:, t, :], b[:, 0:2 * GH], CPY))
                c(ACTV(beta[:, t * GH:(t + 1) * GH], b[:, 0:GH], ACT.Exp, scale=-1.0))
                if t == 1:
                    act.wait_ge(sem("rows_in"), 16 * len(ROWS))
                    ACTV(ealog, row("a_log"), ACT.Exp).then_inc(sem("small_exp"), 1)
                for j in range(NKV):
                    q = b[:, 2 * GH + j * NG * HD:2 * GH + (j + 1) * NG * HD].rearrange("p (g d) -> p g d", d=HD)
                    o = nsa_qr[:, t, :].rearrange("p (g j d) -> p j g d", j=NKV, d=HD)[:, j, :, :]
                    ins = ACTV(o, q, CPY)
                    c(ins) if j == 0 else ins.then_inc(emptied("baq", t), 1)
            split("win", 6)
            for t in range(NT):
                b = filled(act, "kv4", t)
                for i in range(2):
                    c(ACTV(cmp_in[:, t, :, i * HD:(i + 1) * HD], b[:, 0:4 * HD].rearrange("p (a d) -> p a d", d=HD), CPY))
                c(ACTV(nsa_kr[:, t, 0, :], b[:, 4 * HD:6 * HD], CPY))
                copy_out(nsa_v[:, t, 0, :], b[:, 6 * HD:8 * HD], "kv4", t)
            split("win", 0)
            for t in range(NT):
                b = filled(act, "gu", t)
                ins = ACTV(nsa_gate[:, t, :], b[:, 0:3 * NH], ACT.Exp, scale=-1.0)
                c(ins) if t == 0 else ins.then_inc(sem("small_exp"), 1)
                copy_out(pool_in[:, t, :], b[:, 3 * NH:3 * NH + T], "gu", t)
            split("win", 1)
            act.wait_ge(sem("softplus_in"), 1)
            c(ACTV(g_t1, g_t1, ACT.Exp, scale=-1.0))
            c.own()
            ACTV(g_t2, g_t1, ACT.Ln, bias=1.0).then_inc(sem("softplus_ln"), 1)
            act.wait_ge(sem("n_ss_ready"), 1)
            rms_reciprocal(c, n_ss[:, 0:20], n_rs[:, 0:20], HD, "n_rs_ready")
            last_tap(0)
            last_tap(1)
            for k in range(2):
                b = filled(act, "hid", k)
                n = 2 * NKV * NC
                ACTV(cmp_h[:, k, :, :].rearrange("p a b -> p (a b)"), b[:, 0:n], ACT.Exp, scale=-1.0)\
                    .then_inc(sem("small_exp"), 1)
            act.wait_ge(sem("zero_nsa"), 1)
            for t in range(NT):
                b = filled(act, "nq", t)[:, 0:NG * P].rearrange("p (g n) -> p g n", n=P)
                for j in range(NKV):
                    r = slice(j * HD, (j + 1) * HD)
                    ins = ACTV(nsa_qT[r, j::2, t * P:(t + 1) * P], b[r, :, :], CPY)
                    c(ins) if j == 0 else ins.then_inc(emptied("nq", t), 1)
            copy_out(nsa_kT.rearrange("p a b -> p (a b)"), filled(act, "nk")[:, :], "nk")
            split("win", 2)
            last_tap(2)
            act.wait_ge(sem("kc_ss_ready"), 1)
            r = NKV * NC
            rms_reciprocal(c, kc_ss[0:r, :], kc_rs[0:r, :], HD, "kc_rs_ready")
            last_tap(3)
            copy_out(cmp_kT, filled(act, "kcT")[:, 0:r], "kcT")
            last_tap(4)
            for t in range(NT):
                act.wait_ge(sem("c_sc_ready"), t + 1)
                ACTV(c_sc[:, t, :], c_sc[:, t, :], ACT.Exp).then_inc(sem("c_exp_ready"), 1)
            act.preload_act_table(ACT.Silu)
            for i in range(5):
                taken(act, "qkv", i)
                s = conv[:, 2 * i:2 * i + (2 if i < 4 else 1), :]
                ins = ACTV(s, s, ACT.Silu)
                c(ins) if i < 4 else ins.then_inc(sem("conv_ready"), 1)
            for t in range(NT):
                ACTV(z_silu[:, t, :], filled(act, "z", t)[:, 0:GW], ACT.Silu).then_inc(emptied("z", t), 1)
            act.preload_act_table_set("natural_log_exp_and_others")
            for t in range(NT):
                copy_out(pcT[:, :, t * P:(t + 1) * P], filled(act, "pcT", t)[:, 0:NG * P].rearrange("p (g n) -> p g n", n=P),
                         "pcT", t)

            def exps(g):
                kind, t, m0, n = GROUPS[g]
                first = kind == "nsa"
                sc, pr = (scores1 if first else scores2)[:, g % 2, :], (probs1 if first else probs2)[:, g % 2, :]
                W = P * (t + 1)
                act.wait_ge(sem("max_ready"), g + 1)
                if g >= 2:
                    filled(act, "probsT", g - 2)
                for i in range(n):
                    ins = ACTV(pr[:, i * W:(i + 1) * W], sc[:, i * W:(i + 1) * W], ACT.Exp,
                               bias=nmx[:, g % 2, i:i + 1], accum_out=esum[:, g % 2, i:i + 1])
                    c(ins) if i < n - 1 else ins.then_inc(sem("exp_ready"), 1)

            def take_probs(g):
                kind, t, m0, n = GROUPS[g]
                b = filled(act, "probsT", g)
                pT = {"nsa": nsa_pT, "fox": fox_pT, "dif": dif_pT}[kind]
                if kind == "dif":
                    m0, n = m0 // 2, n // 2
                W = P * (t + 1)
                o = pT[:, m0:m0 + n, 0:P] if t == 0 else pT[:, m0:m0 + n, P:3 * P]
                copy_out(o, b[:, 0:n * W].rearrange("p (m n) -> p m n", n=W), "probsT", g)

            def attention(kind):
                for g in range(GFIRST[kind], GLAST[kind] + 1):
                    if g < GLAST[kind]:
                        exps(g)
                    if g > GFIRST[kind]:
                        take_probs(g - 1)

            attention("nsa")
            for i in range(3):
                copy_out(yT[:, 3 + i, :], filled(act, "nsaY", i)[:, 0:T], "nsaY", i)

            b = filled(act, "gc")
            c(ACTV(e_gc, b[:, 0:12], ACT.Exp))
            c(ACTV(e_rest, b[:, 12:24], ACT.Exp))
            last = b[:, 24:24 + NCH * GH].rearrange("p (n q two) -> p n q two", q=3, two=2)
            c(ACTV(e_last[0:HD, :, :], last[0:HD, :, :, 0], ACT.Exp))
            ACTV(e_last[HD:P, :, :], last[HD:P, :, :, 1], ACT.Exp).then_inc(emptied("gc"), 1)
            for i in range(3):
                b = filled(act, "dec", i)
                ACTV(decay[:, 4 * i:4 * i + 4, :].rearrange("p a b -> p (a b)"), b[:, :], ACT.Exp)\
                    .then_inc(emptied("dec", i), 1)
            for s in range(3):
                for t in range(NT):
                    copy_out(cut(7680 + s * 768 + t * GW, GW), filled(act, "tok", s, t)[:, 0:GW], "tok", s, t)
            act.wait_ge(sem("gq_ss_ready"), 1)
            rms_reciprocal(c, gq_ss, gq_rs, 1, "gq_rs_ready")

            def tile3(*task):
                return filled(act, *task)[:, 0:GW].rearrange("p (j n) -> p j n", n=P)

            for t in range(NT):
                copy_out(g_kT[:, :, t * P:(t + 1) * P], tile3("gT", "k", t), "gT", "k", t)
            act.wait_ge(sem("zero_kbq"), 1)
            for t in range(NT):
                b = tile3("gT", "q", t)
                for hh in range(2):
                    r = slice(hh * HD, (hh + 1) * HD)
                    ins = ACTV(g_kbqT[r, hh::2, 1, t * P:(t + 1) * P], b[r, :, :], CPY)
                    c(ins) if hh == 0 else ins.then_inc(emptied("gT", "q", t), 1)
            for t in range(NT):
                copy_out(g_qdT[:, :, t * P:(t + 1) * P], tile3("gT", "qd", t), "gT", "qd", t)
            for h in range(2):
                split("wout", h)
            for t in range(NT):
                copy_out(g_u[:, t, :], filled(act, "u", t)[:, 0:GW], "u", t)
                copy_out(g_wT[:, :, t * P:(t + 1) * P], tile3("wT", t), "wT", t)
            for n in range(NCH):
                r = slice((n % 2) * CHUNK, (n % 2 + 1) * CHUNK)
                copy_out(g_o[r, n // 2, :], filled(act, "qS", n)[r, 0:GW], "qS", n)
            act.wait_ge(sem("go_ss_ready"), 1)
            rms_reciprocal(c, go_ss, go_rs, HD, "go_rs_ready")
            for t in range(NT):
                ACTV(rounded(yT[:, 0:3, t * P:(t + 1) * P]), tile3("gdnY", t), CPY)\
                    .then_inc(sem("gdn_hi_ready"), 1)

            split("w1", 0)
            rms(1, xn)
            normalize(1)
            take_hT(1, "norm_ffn")
            split("w1", 1)
            filled(act, "poolT", 1)
            act.dma_start(bias_c[:, :], alibi_c).then_inc(sem("alibi_in"), 16)
            act.wait_ge(sem("lam_in"), 1)
            ACTV(lam_s, lam_s, ACT.Exp).then_inc(sem("lam_exp"), 1)
            for i in range(FT // 2):
                if i % 2 == 0 and i > 0:
                    split(*(("w1", i // 2 + 1) if i < 14 else ("w2", 0)))
                b = filled(act, "ff1", i)
                if i >= 2:
                    act.wait_ge(sem("ff_h_ready"), i - 1)
                r = ff_r[:, i % 2, :]
                ACTV(r, b[:, :], ACT.Relu).then_inc(emptied("ff1", i), 1)
                taken(act, "ff1", i)
                ACTV(rounded(ff_hi(2 * i, 2)), r.rearrange("p (a b) -> p a b", b=T), ACT.Square)\
                    .then_inc(sem("ff_hi_ready"), 1)
            for i in range(1, 8):
                split("w2", i)
            split("win2", 0)

            rms(2, xn)
            normalize(2)
            take_hT(2, "g_mix")
            split("win2", 1)
            act.wait_ge(sem("softplus_in"), 2)
            c(ACTV(f_t, f_t, ACT.Exp, scale=-1.0))
            c.own()
            ACTV(f_t, f_t, ACT.Ln, bias=1.0).then_inc(sem("softplus_ln"), 1)
            for s, dst, ahead in (("fk", fkT, (2,)), ("dk", dkT, (3, 4, 5))):
                for i in ahead:
                    split("win2", i)
                for i in range(2):
                    copy_out(dst[:, 2 * i:2 * i + 2, :], filled(act, s, i)[:, :].rearrange("p (a b) -> p a b", b=T), s, i)
            act.preload_act_table(ACT.Sigmoid)
            for i in range(8):
                if i % 2 == 0:
                    if i == 0:
                        split("win2", 6)
                    split(*(("win2", 7 + i // 2) if i < 6 else ("pa",)))
                b = filled(act, "gate", i)
                c(ACTV(gates[:, 2 * i, :], b[:, 0:T], ACT.Sigmoid, bias=vec("b_gate", 2 * i)))
                ACTV(gates[:, 2 * i + 1, :], b[:, T:2 * T], ACT.Sigmoid, bias=vec("b_gate", 2 * i + 1))\
                    .then_inc(emptied("gate", i), 1)
            act.preload_act_table_set("natural_log_exp_and_others")
            split("pb")
            attention("fox")
            for i in range(4):
                ACTV(rounded(oaT[:, i, :]), filled(act, "foxY", i)[:, 0:T], CPY).then_inc(sem("oa_hi_ready"), 1)
            attention("dif")
            taken(act, "scores", len(GROUPS) - 1)
            act.dma_start(bias_c[:, 0:D], a["g_moe_2"][0].partition_broadcast(P)).then_inc(sem("g_moe_in"), 16)
            act.wait_ge(sem("d_ss_ready"), 1)
            rms_reciprocal(c, d_ss, d_rs, 2 * HD, "d_rs_ready")
            for t in range(NT):
                ACTV(rounded(obT[:, :, t * P:(t + 1) * P]),
                     filled(act, "difT", t)[:, :].rearrange("p (j n) -> p j n", n=P), CPY).then_inc(sem("ob_hi_ready"), 1)
            split("wo2", 0)
            for i in range(4):
                act.wait_ge(sem("yT2_ready"), i + 1)
                ACTV(rounded(y2_hi[:, 2 * i:2 * i + 2, :]), yT[:, 2 * i:2 * i + 2, :], CPY)\
                    .then_inc(sem("y2_hi_ready"), 1)
            split("wo2", 1)
            rms(3, xn)
            filled(act, "wo", 1, 1)
            fg = yT[:, 0:D // T, :].rearrange("p a b -> p (a b)")
            act.dma_start(fg, a["g_final_2"].partition_broadcast(P)).then_inc(sem("final_g_in"), 16)
            take_rows()
            act.wait_ge(sem("group_in"), 1)
            ACTV(gtmp, gtmp, ACT.Exp).then_inc(sem("route_exp"), 1)
            act.wait_ge(sem("second_in"), 1)
            ACTV(e21, e21, ACT.Exp).then_inc(sem("route_exp"), 1)

            act.preload_act_table(ACT.Silu)
            act.wait_ge(sem("passes_known"), 1)
            n = act.value_load(passes[0:1, 0:1], min_val=1, max_val=MAXPASS)
            ps_h1, ps_x1, ps_t, ps_g, ps_y1 = bank[0], bank[3], bank[4], bank[5], bank[7]

            def take_tokens(to, count):
                act.wait_ge(sem("x1_full"), count + 1)
                ACTV(xg[:, to, 4:8, :].rearrange("p a b -> p (a b)"), ps_x1[:, :], CPY).then_inc(sem("xg1_ready"), 1)

            take_tokens(0, 0)
            with act.Fori(0, n * (PAIRS // 2)) as half:
                for odd in range(2):
                    it = half * 2 + odd
                    act.wait_ge(sem("h1_full"), it + 1)
                    ACTV(act1, ps_h1[:, :], ACT.Silu).then_inc(sem("h1_read"), 1)
                    take_tokens(1 - odd, it + 1)
                    act.wait_ge(sem("giveT_full"), it + 1)
                    ACTV(giveT.rearrange("p a b -> p (a b)"), ps_g[:, 0:T], CPY).then_inc(sem("giveT_ready"), 1)
                    act.wait_ge(sem("t_full"), it + 1)
                    ACTV(actT.rearrange("p a b -> p (a b)"), ps_t[:, :], CPY).then_inc(sem("actT_ready"), 1)
                    act.wait_ge(sem("y_full"), it * 2 + 2)
                    ACTV(y_e[:, 512:1024], ps_y1[:, :], CPY).then_inc(sem("y1_ready"), 1)
            act.preload_act_table_set("natural_log_exp_and_others")
            act.wait_ge(sem("added"), n * (4 * PAIRS) + 4)
            rms(4, out_sb)

        @block.gpsimd
        def _(pool):
            GT = nc.gpsimd.tensor_tensor

            def split(*name):
                for q in range(PARTS):
                    w, hi, lo = split_step(name, q)
                    pool.wait_ge(sem("hi_ready"), PARTS * SPLIT[name] + q + 1)
                    GT(rounded(lo), w, reread(hi), ALU.subtract).then_inc(sem("lo_ready"), 1)

            nc.gpsimd.memset(poolw[:, :, :], 0.0).then_inc(sem("zero_start"), 1)
            nc.gpsimd.memset(nsa_qT, 0.0)
            nc.gpsimd.memset(pc, 0.0)
            nc.gpsimd.memset(cmp_vb, 0.0).then_inc(sem("zero_nsa"), 1)
            split("win", 5)
            pool.wait_ge(sem("g_log_ready"), 1)
            filled(pool, "nsaY", 2)
            pool.wait_ge(sem("const_in"), 16)
            GT(g_cols, over(const("le_chunk"), 12), wide(g_log, P), ALU.mult).then_inc(sem("g_cols_ready"), 1)
            for m in (inv_d, inv_t):
                nc.gpsimd.tensor_copy(m, over(ident, 12)).then_inc(sem("inv_start"), 1)
            for i in range(3):
                taken(pool, "dec", i)
            GT(decay, decay, over(const("le_chunk"), 12), ALU.mult).then_inc(sem("decay_ready"), 1)
            pool.wait_ge(sem("gq_ss_ready"), 1)
            nc.gpsimd.memset(g_kbqT, 0.0).then_inc(sem("zero_kbq"), 1)
            pool.wait_ge(sem("g_tok_ready"), 1)
            taken(pool, "gc")
            GT(g_qd, g_q, wide(e_gc, HD), ALU.mult)
            GT(g_kd, g_k, wide(e_rest, HD), ALU.mult).then_inc(sem("g_pool_ready"), 1)
            for i in range(GH):
                taken(pool, "kk", i)
            nc.gpsimd.memset(g_state, 0.0).then_inc(sem("state_ready"), 1)
            for task in (("nsaY", 0), ("nsaY", 1), ("nsaY", 2), ("poolY", 0), ("poolY", 1)):
                taken(pool, *task)
            y, lo = yT[:, 3:KD, :], y_lo[:, 3:KD, :]
            nc.gpsimd.tensor_copy(rounded(lo), y).then_inc(sem("y_high"), 1)
            pool.wait_ge(sem("y_high"), 1)
            GT(rounded(lo), y, reread(lo), ALU.subtract).then_inc(sem("y_split"), 1)
            pool.wait_ge(sem("y_split"), 1)
            nc.gpsimd.tensor_copy(rounded(y), y).then_inc(sem("y_split"), 1)
            for name in (("wout", 0), ("wout", 1), ("w1", 0)):
                split(*name)
            filled(pool, "ff2", 1, 1)
            nc.gpsimd.memset(fqT, 0.0)
            nc.gpsimd.memset(dqT, 0.0).then_inc(sem("zero_q"), 1)
            pool.wait_ge(sem("f_log_ready"), 1)
            for t in range(NT):
                GT(f_cols[:, t, :, :], over(const("gt"), FOX), wide(f_log[:, t, :], P), ALU.mult)\
                    .then_inc(sem("f_cols_ready"), 1)


_INS = ['x', 'norm_mix', 'w_in', 'conv_w', 'a_log', 'dt_bias', 'gdn_norm', 'nsa_q_norm', 'nsa_k_norm', 'cmp_pos',
        'cmp_w1', 'cmp_w2', 'pool_w', 'pool_scale', 'w_out', 'norm_ffn', 'w_ffn1', 'w_ffn2', 'g_mix_2', 'w_in_2',
        'b_fgate_2', 'b_gate_2', 'lam_q1_2', 'lam_k1_2', 'lam_q2_2', 'lam_k2_2', 'g_subln_2', 'w_pa_2', 'w_pb_2',
        'w_o_2', 'g_moe_2', 'w_group_2', 'b_group_2', 'w_expert_2', 'b_expert_2', 'w1_2', 'w3_2', 'w2_2', 'g_final_2']
_OUT = (1, T, D)


def kernel(**inputs):
    import numpy as _np
    import concourse.bacc as _bacc
    from concourse import mybir as _mybir
    from concourse.bass_utils import run_bass_kernel_spmd as _run

    nc = _bacc.Bacc("TRN2", target_bir_lowering=False, num_devices=1, dynamic_dma_scratch_size=1024)
    arrays, args = {}, {}
    for name in _INS:
        arr = _np.ascontiguousarray(inputs[name])
        arrays[f"in_{name}_dram"] = arr
        args[name] = nc.dram_tensor(f"in_{name}_dram", arr.shape, _mybir.dt.from_np(arr.dtype),
                                    kind="ExternalInput").ap()
    extra = []
    for name, arr in zip(("consts", "band", "alibi"), shape_constants()):
        arrays[f"in_{name}_dram"] = arr
        extra.append(nc.dram_tensor(f"in_{name}_dram", arr.shape, _mybir.dt.from_np(arr.dtype),
                                    kind="ExternalInput").ap())
    out = nc.dram_tensor("out_0_dram", _OUT, _mybir.dt.float32, kind="ExternalOutput").ap()
    mixer_block_kernel(nc, args, *extra, out)
    r = _run(nc, [arrays], core_ids=[0])
    return r.results[0]["out_0_dram"]
```
